# Optimizing a Trainium2 kernel written in Bass

```python
import math
import jax, jax.numpy as jnp
from jax import lax
import numpy as np

D_MODEL = 1024
BATCH = 1
SEQ = 128
DEPTH = 2
DEC_BATCH = 1
DEC_SEQ = 512
PAST_LEN = 256

GRID_W = 64
HEAD_DIM = 64
DIFF_HEADS = 4
SWA_HEADS = 8
SWA_KV_HEADS = 2
SWA_GROUP = SWA_HEADS // SWA_KV_HEADS
WINDOW = 128
MLA_HEADS = 16
MLA_Q_RANK = 384
MLA_KV_RANK = 256
MLA_NOPE_DIM = 64
MLA_ROPE_DIM = 32
MLA_V_DIM = 64
N_EXPERTS = 16
EXPERT_FF = 512
EC_FACTOR = 2
QBLK = 128
ROPE_BASE = 10000.0
EPS = 1e-6
NEG_INF = -1e30
N_EVEN = (DEPTH + 1) // 2
N_ODD = DEPTH // 2
DIFF_W = DIFF_HEADS * 2 * HEAD_DIM
SWA_QW = SWA_HEADS * HEAD_DIM
SWA_KW = SWA_KV_HEADS * HEAD_DIM
EVEN_IN = 3 * DIFF_W + SWA_QW + 2 * SWA_KW
EVEN_OUT = DIFF_W + SWA_QW
ODD_IN = MLA_Q_RANK + MLA_KV_RANK + MLA_ROPE_DIM
ODD_OUT = MLA_HEADS * MLA_V_DIM

kernel_name = "hybrid_diffusion_prefix_trunk_step"

def _rmsnorm(x, g):
    xf = x.astype(jnp.float32)
    y = xf * lax.rsqrt(jnp.mean(xf * xf, axis=-1, keepdims=True) + EPS)
    return (y * g.astype(jnp.float32)).astype(x.dtype)

def _modulate(x, g, shift, scale):
    return _rmsnorm(x, g) * (1 + scale) + shift

def _ada(cvec, w, b):
    mod = (jax.nn.silu(cvec) @ w + b)[:, None, :]
    return jnp.split(mod, 6, axis=-1)

def _rope_1d(x, pos):
    half = x.shape[-1] // 2
    inv = ROPE_BASE ** (-(jnp.arange(half, dtype=jnp.float32) / half))
    ang = pos.astype(jnp.float32)[:, None] * inv[None, :]
    cos = jnp.cos(ang)[:, None, :].astype(x.dtype)
    sin = jnp.sin(ang)[:, None, :].astype(x.dtype)
    x1, x2 = x[..., :half], x[..., half:]
    return jnp.concatenate([x1 * cos - x2 * sin, x1 * sin + x2 * cos], axis=-1)

def _rope_2d(x):
    s = x.shape[1]
    rows = s // GRID_W
    row = jnp.repeat(jnp.arange(rows), GRID_W)
    col = jnp.tile(jnp.arange(GRID_W), rows)
    h = x.shape[-1] // 2
    return jnp.concatenate([_rope_1d(x[..., :h], row), _rope_1d(x[..., h:], col)], axis=-1)

def _map_query_blocks(fn, q):
    b, s = q.shape[0], q.shape[1]
    nb = s // QBLK
    qb = jnp.moveaxis(q.reshape((b, nb, QBLK) + q.shape[2:]), 1, 0)
    out = lax.map(fn, qb)
    out = jnp.moveaxis(out, 0, 1)
    return out.reshape((b, s) + out.shape[3:])

def _lambda_init(layer):
    return 0.8 - 0.6 * math.exp(-0.3 * layer)

def _diff_attend(q, k, v, lam, subln, lam_init):
    b, s = q.shape[:2]
    lamf = lam.astype(jnp.float32)
    lam_full = jnp.exp(jnp.sum(lamf[0] * lamf[1])) - jnp.exp(jnp.sum(lamf[2] * lamf[3])) + lam_init
    scale = HEAD_DIM ** -0.5

    def blk(qb):
        sc = jnp.einsum('bqhcd,bkhcd->bhcqk', qb, k).astype(jnp.float32) * scale
        p = jax.nn.softmax(sc, axis=-1)
        a = p[:, :, 0] - lam_full * p[:, :, 1]
        return jnp.einsum('bhqk,bkhe->bqhe', a.astype(v.dtype), v)

    o = _map_query_blocks(blk, q)
    o = _rmsnorm(o, subln) * (1 - lam_init)
    return o.reshape(b, s, -1)

def _sink_softmax(sc, sink):
    sk = sink.astype(jnp.float32).reshape(SWA_KV_HEADS, SWA_GROUP, 1, 1)
    m = jnp.maximum(jnp.max(sc, axis=-1, keepdims=True), sk)
    e = jnp.exp(sc - m)
    return e / (jnp.sum(e, axis=-1, keepdims=True) + jnp.exp(sk - m))

def _sink_attend(q, k, v, sink):
    b, s = q.shape[:2]
    scale = HEAD_DIM ** -0.5

    def blk(qb):
        sc = jnp.einsum('bqhgd,bkhd->bhgqk', qb, k).astype(jnp.float32) * scale
        p = _sink_softmax(sc, sink)
        return jnp.einsum('bhgqk,bkhd->bqhgd', p.astype(v.dtype), v)

    return _map_query_blocks(blk, q).reshape(b, s, -1)

def _band_blocks(t):
    b, s = t.shape[:2]
    nb = s // WINDOW
    tp = jnp.pad(t, ((0, 0), (WINDOW, WINDOW), (0, 0), (0, 0))).reshape((b, nb + 2, WINDOW) + t.shape[2:])
    return jnp.concatenate([tp[:, :-2], tp[:, 1:-1], tp[:, 2:]], axis=2)

def _swa_latent(q, k, v, k_ctx, v_ctx, sink):
    b, s = q.shape[:2]
    nb = s // WINDOW
    lc = k_ctx.shape[1]
    scale = HEAD_DIM ** -0.5
    qb = q.reshape(b, nb, WINDOW, SWA_KV_HEADS, SWA_GROUP, HEAD_DIM)
    kb, vb = _band_blocks(k), _band_blocks(v)
    s_loc = jnp.einsum('bnqhgd,bnkhd->bnhgqk', qb, kb).astype(jnp.float32) * scale
    s_ctx = jnp.einsum('bnqhgd,bkhd->bnhgqk', qb, k_ctx).astype(jnp.float32) * scale
    start = jnp.arange(nb)[:, None, None] * WINDOW
    qpos = start + jnp.arange(WINDOW)[None, :, None]
    kpos = start - WINDOW + jnp.arange(3 * WINDOW)[None, None, :]
    valid = (jnp.abs(qpos - kpos) <= WINDOW) & (kpos >= 0) & (kpos < s)
    s_loc = jnp.where(valid[None, :, None, None], s_loc, NEG_INF)
    p = _sink_softmax(jnp.concatenate([s_ctx, s_loc], axis=-1), sink).astype(v.dtype)
    o = (jnp.einsum('bnhgqk,bkhd->bnqhgd', p[..., :lc], v_ctx)
         + jnp.einsum('bnhgqk,bnkhd->bnqhgd', p[..., lc:], vb))
    return o.reshape(b, s, -1)

def _even_project(h, w_in):
    b, s = h.shape[:2]
    qa, ka, va, qb, kb, vb = jnp.split(
        h @ w_in, [DIFF_W, 2 * DIFF_W, 3 * DIFF_W, 3 * DIFF_W + SWA_QW, 3 * DIFF_W + SWA_QW + SWA_KW], axis=-1)
    return (qa.reshape(b, s, 2 * DIFF_HEADS, HEAD_DIM), ka.reshape(b, s, 2 * DIFF_HEADS, HEAD_DIM),
            va.reshape(b, s, DIFF_HEADS, 2 * HEAD_DIM), qb.reshape(b, s, SWA_HEADS, HEAD_DIM),
            kb.reshape(b, s, SWA_KV_HEADS, HEAD_DIM), vb.reshape(b, s, SWA_KV_HEADS, HEAD_DIM))

def _even_ctx(h, w_in, w_out, lam, subln, sink, lam_init):
    b, l = h.shape[:2]
    qa, ka, va, qb, kb, vb = _even_project(h, w_in)
    o_a = _diff_attend(qa.reshape(b, l, DIFF_HEADS, 2, HEAD_DIM), ka.reshape(b, l, DIFF_HEADS, 2, HEAD_DIM),
                       va, lam, subln, lam_init)
    o_b = _sink_attend(qb.reshape(b, l, SWA_KV_HEADS, SWA_GROUP, HEAD_DIM), kb, vb, sink)
    out = jnp.concatenate([o_a, o_b], axis=-1) @ w_out
    return out, ka.reshape(b, l, DIFF_HEADS, 2 * HEAD_DIM), va, kb, vb

def _even_lat(h, kd_ctx, vd_ctx, ks_ctx, vs_ctx, w_in, w_out, lam, subln, sink, lam_init):
    b, s = h.shape[:2]
    lc = kd_ctx.shape[1]
    qa, ka, va, qb, kb, vb = _even_project(h, w_in)
    qa, ka, qb, kb = _rope_2d(qa), _rope_2d(ka), _rope_2d(qb), _rope_2d(kb)
    k_all = jnp.concatenate([kd_ctx.reshape(b, lc, DIFF_HEADS, 2, HEAD_DIM),
                             ka.reshape(b, s, DIFF_HEADS, 2, HEAD_DIM)], axis=1)
    v_all = jnp.concatenate([vd_ctx, va], axis=1)
    o_a = _diff_attend(qa.reshape(b, s, DIFF_HEADS, 2, HEAD_DIM), k_all, v_all, lam, subln, lam_init)
    o_b = _swa_latent(qb.reshape(b, s, SWA_KV_HEADS, SWA_GROUP, HEAD_DIM), kb, vb, ks_ctx, vs_ctx, sink)
    return jnp.concatenate([o_a, o_b], axis=-1) @ w_out

def _mla_project(h, w_in, q_norm, w_q_up, kv_norm):
    b, s = h.shape[:2]
    cq, ckv, kr = jnp.split(h @ w_in, [MLA_Q_RANK, MLA_Q_RANK + MLA_KV_RANK], axis=-1)
    q = (_rmsnorm(cq, q_norm) @ w_q_up).reshape(b, s, MLA_HEADS, MLA_NOPE_DIM + MLA_ROPE_DIM)
    return q, _rmsnorm(ckv, kv_norm), kr

def _mla_keys(ckv, kr, w_kv_up):
    b, n = ckv.shape[:2]
    kv = (ckv @ w_kv_up).reshape(b, n, MLA_HEADS, MLA_NOPE_DIM + MLA_V_DIM)
    k_nope, v = kv[..., :MLA_NOPE_DIM], kv[..., MLA_NOPE_DIM:]
    k_rope = jnp.broadcast_to(kr[:, :, None, :], (b, n, MLA_HEADS, MLA_ROPE_DIM))
    return jnp.concatenate([k_nope, k_rope], axis=-1), v

def _mla_attend(q, k, v):
    b, s = q.shape[:2]
    scale = (MLA_NOPE_DIM + MLA_ROPE_DIM) ** -0.5

    def blk(qb):
        sc = jnp.einsum('bqhd,bkhd->bhqk', qb, k).astype(jnp.float32) * scale
        p = jax.nn.softmax(sc, axis=-1)
        return jnp.einsum('bhqk,bkhd->bqhd', p.astype(v.dtype), v)

    return _map_query_blocks(blk, q).reshape(b, s, -1)

def _odd_ctx(h, w_in, q_norm, w_q_up, kv_norm, w_kv_up, w_out):
    q, ckv, kr = _mla_project(h, w_in, q_norm, w_q_up, kv_norm)
    k, v = _mla_keys(ckv, kr, w_kv_up)
    return _mla_attend(q, k, v) @ w_out, ckv, kr

def _odd_lat(h, ckv_ctx, kr_ctx, w_in, q_norm, w_q_up, kv_norm, w_kv_up, w_out):
    q, ckv, kr = _mla_project(h, w_in, q_norm, w_q_up, kv_norm)
    q = jnp.concatenate([q[..., :MLA_NOPE_DIM], _rope_2d(q[..., MLA_NOPE_DIM:])], axis=-1)
    kr = _rope_2d(kr[:, :, None, :])[:, :, 0, :]
    k, v = _mla_keys(jnp.concatenate([ckv_ctx, ckv], axis=1), jnp.concatenate([kr_ctx, kr], axis=1), w_kv_up)
    return _mla_attend(q, k, v) @ w_out

def _moe(h, w_router, w_gate, w_up, w_down):
    b, s, d = h.shape
    n = b * s
    cap = EC_FACTOR * n // N_EXPERTS
    xt = h.reshape(n, d)
    aff = jax.nn.softmax((xt @ w_router).astype(jnp.float32), axis=-1)
    gate, idx = lax.top_k(aff.T, cap)
    xe = xt[idx]
    hid = jax.nn.silu(jnp.einsum('ecd,edf->ecf', xe, w_gate)) * jnp.einsum('ecd,edf->ecf', xe, w_up)
    ye = jnp.einsum('ecf,efd->ecd', hid, w_down) * gate[..., None].astype(h.dtype)
    out = jnp.zeros((n, d), h.dtype).at[idx.reshape(-1)].add(ye.reshape(-1, d))
    return out.reshape(b, s, d)

def _normal(k, shape, scale):
    return jax.random.normal(k, shape, jnp.float32) * scale

def setup_inputs(seed: int = 0) -> dict:
    key = jax.random.key(seed)
    ks = jax.random.split(key, 32)
    D = D_MODEL
    gain = lambda k, shape: 1.0 + _normal(k, shape, 0.02)
    return {
        "x_prompt": _normal(ks[0], (BATCH, SEQ, D), 1.0),
        "x_sample": _normal(ks[1], (DEC_BATCH, DEC_SEQ, D), 1.0),
        "cache_diff_k": _normal(ks[2], (DEC_BATCH, N_EVEN, PAST_LEN, DIFF_HEADS, 2 * HEAD_DIM), 1.0),
        "cache_diff_v": _normal(ks[3], (DEC_BATCH, N_EVEN, PAST_LEN, DIFF_HEADS, 2 * HEAD_DIM), 1.0),
        "cache_swa_k": _normal(ks[4], (DEC_BATCH, N_EVEN, PAST_LEN, SWA_KV_HEADS, HEAD_DIM), 1.0),
        "cache_swa_v": _normal(ks[5], (DEC_BATCH, N_EVEN, PAST_LEN, SWA_KV_HEADS, HEAD_DIM), 1.0),
        "cache_mla_ckv": _normal(ks[6], (DEC_BATCH, N_ODD, PAST_LEN, MLA_KV_RANK), 1.0),
        "cache_mla_krope": _normal(ks[7], (DEC_BATCH, N_ODD, PAST_LEN, MLA_ROPE_DIM), 1.0),
        "c": _normal(ks[8], (DEC_BATCH, D), 1.0),
        "c_ctx": _normal(ks[9], (D,), 1.0),
        "w_ada": _normal(ks[10], (DEPTH, D, 6 * D), 0.5 * D ** -0.5),
        "b_ada": _normal(ks[11], (DEPTH, 6 * D), 0.02),
        "norm_mix": gain(ks[12], (DEPTH, D)),
        "norm_ffn": gain(ks[13], (DEPTH, D)),
        "w_in_even": _normal(ks[14], (N_EVEN, D, EVEN_IN), D ** -0.5),
        "w_out_even": _normal(ks[15], (N_EVEN, EVEN_OUT, D), EVEN_OUT ** -0.5),
        "diff_lambda": _normal(ks[16], (N_EVEN, 4, HEAD_DIM), 0.1),
        "diff_subln": gain(ks[17], (N_EVEN, 2 * HEAD_DIM)),
        "swa_sink": _normal(ks[18], (N_EVEN, SWA_HEADS), 0.5),
        "w_in_odd": _normal(ks[19], (N_ODD, D, ODD_IN), D ** -0.5),
        "mla_q_norm": gain(ks[20], (N_ODD, MLA_Q_RANK)),
        "w_q_up": _normal(ks[21], (N_ODD, MLA_Q_RANK, MLA_HEADS * (MLA_NOPE_DIM + MLA_ROPE_DIM)), MLA_Q_RANK ** -0.5),
        "mla_kv_norm": gain(ks[22], (N_ODD, MLA_KV_RANK)),
        "w_kv_up": _normal(ks[23], (N_ODD, MLA_KV_RANK, MLA_HEADS * (MLA_NOPE_DIM + MLA_V_DIM)), MLA_KV_RANK ** -0.5),
        "w_out_odd": _normal(ks[24], (N_ODD, ODD_OUT, D), ODD_OUT ** -0.5),
        "w_router": _normal(ks[25], (DEPTH, D, N_EXPERTS), D ** -0.5),
        "w_gate_exp": _normal(ks[26], (DEPTH, N_EXPERTS, D, EXPERT_FF), D ** -0.5),
        "w_up_exp": _normal(ks[27], (DEPTH, N_EXPERTS, D, EXPERT_FF), D ** -0.5),
        "w_down_exp": _normal(ks[28], (DEPTH, N_EXPERTS, EXPERT_FF, D), EXPERT_FF ** -0.5),
        "final_norm": gain(ks[29], (D,)),
    }

def reference(x_prompt, x_sample, cache_diff_k, cache_diff_v, cache_swa_k, cache_swa_v,
              cache_mla_ckv, cache_mla_krope, c, c_ctx, w_ada, b_ada, norm_mix, norm_ffn,
              w_in_even, w_out_even, diff_lambda, diff_subln, swa_sink, w_in_odd, mla_q_norm,
              w_q_up, mla_kv_norm, w_kv_up, w_out_odd, w_router, w_gate_exp, w_up_exp,
              w_down_exp, final_norm):
    xc = x_prompt
    diff_k, diff_v, swa_k, swa_v, mla_ckv, mla_kr = [], [], [], [], [], []
    for i in range(DEPTH):
        j = i // 2
        sh1, sc1, g1, sh2, sc2, g2 = _ada(c_ctx[None, :], w_ada[i], b_ada[i])
        h = _modulate(xc, norm_mix[i], sh1, sc1)
        if i % 2 == 0:
            out, kd, vd, ksw, vsw = _even_ctx(h, w_in_even[j], w_out_even[j], diff_lambda[j],
                                              diff_subln[j], swa_sink[j], _lambda_init(i))
            diff_k.append(kd); diff_v.append(vd); swa_k.append(ksw); swa_v.append(vsw)
        else:
            out, ckv, kr = _odd_ctx(h, w_in_odd[j], mla_q_norm[j], w_q_up[j], mla_kv_norm[j],
                                    w_kv_up[j], w_out_odd[j])
            mla_ckv.append(ckv); mla_kr.append(kr)
        xc = xc + g1 * out
        h = _modulate(xc, norm_ffn[i], sh2, sc2)
        xc = xc + g2 * _moe(h, w_router[i], w_gate_exp[i], w_up_exp[i], w_down_exp[i])
    y_prompt = _rmsnorm(xc, final_norm)
    new_diff_k = jnp.stack(diff_k, axis=1)
    new_diff_v = jnp.stack(diff_v, axis=1)
    new_swa_k = jnp.stack(swa_k, axis=1)
    new_swa_v = jnp.stack(swa_v, axis=1)
    new_mla_ckv = jnp.stack(mla_ckv, axis=1)
    new_mla_krope = jnp.stack(mla_kr, axis=1)

    xs = x_sample
    for i in range(DEPTH):
        j = i // 2
        sh1, sc1, g1, sh2, sc2, g2 = _ada(c, w_ada[i], b_ada[i])
        h = _modulate(xs, norm_mix[i], sh1, sc1)
        if i % 2 == 0:
            out = _even_lat(h, cache_diff_k[:, j], cache_diff_v[:, j], cache_swa_k[:, j], cache_swa_v[:, j],
                            w_in_even[j], w_out_even[j], diff_lambda[j], diff_subln[j], swa_sink[j],
                            _lambda_init(i))
        else:
            out = _odd_lat(h, cache_mla_ckv[:, j], cache_mla_krope[:, j], w_in_odd[j], mla_q_norm[j],
                           w_q_up[j], mla_kv_norm[j], w_kv_up[j], w_out_odd[j])
        xs = xs + g1 * out
        h = _modulate(xs, norm_ffn[i], sh2, sc2)
        xs = xs + g2 * _moe(h, w_router[i], w_gate_exp[i], w_up_exp[i], w_down_exp[i])
    y_sample = _rmsnorm(xs, final_norm)

    return (y_prompt, y_sample, new_diff_k, new_diff_v, new_swa_k, new_swa_v, new_mla_ckv, new_mla_krope)


_drawn_inputs = setup_inputs


def setup_inputs(seed=0):
    import zlib

    import numpy as np

    out = dict(_drawn_inputs(seed))
    spreads = {}
    factors = {'cache_swa_k': 4.817,
     'cache_swa_v': 4.148,
     'cache_mla_ckv': 5.018,
     'cache_mla_krope': 8.0,
     'norm_mix': 2.962,
     'norm_ffn': 5.239,
     'diff_lambda': 4.274,
     'diff_subln': 8.0,
     'swa_sink': 64.0,
     'mla_q_norm': 8.0,
     'mla_kv_norm': 3.159,
     'final_norm': 8.573,
     'cache_diff_k': 8.0,
     'cache_diff_v': 8.0}
    for name, (base, spread) in spreads.items():
        noise = np.random.default_rng([zlib.crc32(name.encode()), seed]).standard_normal(out[name].shape)
        drawn = base * np.exp(spread * noise) if base else spread * noise
        out[name] = __import__('jax').numpy.asarray(drawn.astype(out[name].dtype))
    for name, factor in factors.items():
        out[name] = (out[name] * factor).astype(out[name].dtype)
    return out
```

```python
import math
from contextlib import ExitStack

import numpy as np

import concourse.bass as bass
from concourse import mybir

P = 128
D = 1024
KD = D // P
NS, NP_ = 512, 128
TS = NS // P
NT = TS + 1
NTOK = NS + NP_
PAST = 256
NKEY = PAST + NS
KCOL = NKEY + NP_
KT = KCOL // P
HD = 64
EVEN_IN = 2304
QK = 1664
ODD_IN = 672
QR, KVR, RD = 384, 256, 32
MH, MQ = 16, 96
NE, FF = 16, 512
CAP_S, CAP_P = 2 * NS // NE, 2 * NP_ // NE
SLOTS = CAP_S + CAP_P
EPS = 1e-6
LAM_INIT = 0.8 - 0.6 * math.exp(-0.3 * 0)
NEG = -1e30
GRID_W = 64

F32 = mybir.dt.float32
BF16 = mybir.dt.bfloat16
I32 = mybir.dt.int32
U32 = mybir.dt.uint32
ALU = mybir.AluOpType
ACT = mybir.ActivationFunctionType
AX = mybir.AxisListType.X

C_ID, C_LEFT, C_RIGHT = 0, 128, 256
C_C64, C_S64 = 384, 384 + TS * 64
C_C32 = C_S64 + TS * 64
C_S32 = C_C32 + TS * 32
N_CONST = C_S32 + TS * 32


def rope_tables(dim):
    half = dim // 4
    tok = np.arange(NS)
    inv = (10000.0 ** (-(np.arange(half, dtype=np.float32) / np.float32(half)))).astype(np.float32)
    cos, sin = [], []
    for pos in (tok // GRID_W, tok % GRID_W):
        ang = pos.astype(np.float32)[:, None] * inv[None, :]
        c, s = np.cos(ang.astype(np.float64)), np.sin(ang.astype(np.float64))
        cos += [c, c]
        sin += [-s, s]
    return np.concatenate(cos, 1), np.concatenate(sin, 1)


def constants():
    out = np.zeros((P, N_CONST), np.float32)
    i = np.arange(P)
    out[:, C_ID:C_ID + P] = np.eye(P)
    out[:, C_LEFT:C_LEFT + P] = np.where(i[None, :] >= i[:, None], 0.0, NEG)
    out[:, C_RIGHT:C_RIGHT + P] = np.where(i[None, :] <= i[:, None], 0.0, NEG)
    for dim, c0, s0 in ((64, C_C64, C_S64), (32, C_C32, C_S32)):
        cos, sin = rope_tables(dim)
        for t in range(TS):
            out[:, c0 + t * dim:c0 + (t + 1) * dim] = cos[t * P:(t + 1) * P]
            out[:, s0 + t * dim:s0 + (t + 1) * dim] = sin[t * P:(t + 1) * P]
    return out


def bank_pieces(off, n):
    out = []
    while n:
        m = min(n, 512 - off % 512)
        out.append((off, m))
        off, n = off + m, n - m
    return out


def build(nc, a):
    with ExitStack() as ctx:
        def sb(name, shape, dt=F32):
            return ctx.enter_context(nc.sbuf_tensor(name, shape, dt))

        def ps(name, shape):
            return ctx.enter_context(nc.psum_tensor(name, shape, F32))

        def sem(name):
            return ctx.enter_context(nc.semaphore(name))

        pe, dve, act, pool, sp = nc.tensor, nc.vector, nc.scalar, nc.gpsimd, nc.sync

        U = 4096
        ring = sb("ring", [P, 6 * U])
        stage = sb("stage", [P, U])
        XH = sb("XH", [P, 2 * NT * D])
        Z = sb("Z", [P, 8960])
        GB = sb("GB", [P, 2048])
        C = sb("C", [P, N_CONST])
        junk = sb("junk", [P, D], BF16)
        X = XH[:, 0:NT * D].rearrange("p (t n) -> p t n", t=NT)
        HT = XH[:, NT * D:2 * NT * D].rearrange("p (k n) -> p k n", k=KD)
        ident = C[:, C_ID:C_ID + P]

        VC1 = sb("VC1", [P, P])
        VC2 = sb("VC2", [P, 22])
        VR = sb("VR", [P, 2, P])
        sqs = VR[:].rearrange("p a n -> p (a n)").bitcast(BF16)
        csil = sb("csil", [P, 16])
        mods = sb("mods", [P, 2 * 6 * KD * 2])
        mods = mods[:].rearrange("p (l m k s) -> p l m k s", l=2, m=6, s=2)
        modA = sb("modA", [P, 2 * 2 * KD * 2])
        modA = modA[:].rearrange("p (l w k s) -> p l w k s", l=2, w=2, s=2)
        ss = sb("ss", [P, NT])
        rstd = sb("rstd", [P, NT])
        mhalf = sb("mhalf", [P, 8])
        lamv = sb("lamv", [P, 256])
        lam2 = sb("lam2", [P, 2])
        lame = sb("lame", [P, 2])
        coef = sb("coef", [P, 2])
        sink = sb("sink", [P, 8])
        sink8 = sb("sink8", [P, 8])
        wr = sb("wr", [P, 2, KD, NE])
        mx = sb("mx", [P, 4])
        nm = sb("nm", [P, 4])
        den = sb("den", [P, 4])
        snk = sb("snk", [P, 4])
        sne = sb("sne", [P, 4])
        rr = sb("rr", [P, 4])
        sub4 = sb("sub4", [P, 4])
        subr = sb("subr", [P, 4])
        gates = sb("gates", [SLOTS, NE])
        idxi = sb("idxi", [SLOTS, NE], I32)
        idxe = [sb(f"idxe{b}", [SLOTS, 1], I32) for b in range(2)]
        rs5 = sb("rs5", [P, 3, NT])
        ssk = sb("ssk", [P, 2, NT])
        rsk = sb("rsk", [P, 2, NT])

        kaT = Z[:, 0:4 * KCOL].rearrange("p (h n) -> p h n", h=4)
        kbT = Z[:, 3584:3584 + KCOL]
        va = Z[:, 4480:4480 + KT * 512].rearrange("p (k n) -> p k n", k=KT)
        vb = Z[:, 8064:8064 + KT * P].rearrange("p (k n) -> p k n", k=KT)
        w_in_e = ring[:, 0:KD * EVEN_IN].rearrange("p (k n) -> p k n", k=KD)
        raw = [ring[:, 18432 + i * QK:18432 + (i + 1) * QK] for i in range(2)]
        rtmp = ring[:, 18432 + 2 * QK:18432 + 3 * QK]
        ctx_k = GB[:, 0:1024].rearrange("p (j n) -> p j n", j=2)
        ctx_ks = GB[:, 1024:1280].rearrange("p (j n) -> p j n", j=2)
        w_out = ring[:, 4 * U:6 * U].rearrange("p (k n) -> p k n", k=KD)
        QTe = XH[:, 0:NT * D].rearrange("p (t k n) -> p t k n", t=NT, k=KD)
        w_in_o = ring[:, 0:KD * ODD_IN].rearrange("p (k n) -> p k n", k=KD)
        w_qup = ring[:, 5376:5376 + 3 * 1536].rearrange("p (k n) -> p k n", k=3)
        w_kvup = ring[:, 3 * U:4 * U].rearrange("p (k n) -> p k n", k=2)
        cqT = Z[:, 0:3 * NTOK].rearrange("p (k n) -> p k n", k=3)
        ckvT = Z[:, 1920:1920 + 2 * KCOL].rearrange("p (k n) -> p k n", k=2)
        krT = Z[0:RD, 3712:3712 + KCOL]
        Vh = Z[:, 4608:4608 + 2 * KCOL].rearrange("p (b k n) -> p b k n", b=2, k=KT)
        rawo = [Z[:, 6400 + i * ODD_IN:6400 + (i + 1) * ODD_IN] for i in range(2)]
        ctx_c = Z[:, 7744:8256].rearrange("p (j n) -> p j n", j=2)
        ctx_r = Z[:, 8256:8320].rearrange("p (j n) -> p j n", j=2)
        kvn = Z[:, 8320:8576]
        rtk = Z[:, 8576:8608]
        qraw = [stage[:, i * 1536:(i + 1) * 1536] for i in range(2)]
        qtmp = stage[:, 3072:3584]
        KTh = stage[0:MQ, 0:4 * KCOL].rearrange("p (b j n) -> p b j n", b=2, j=2)
        QTo = XH[0:MQ, 0:MH * NTOK].rearrange("p (h n) -> p h n", h=MH)
        pbase = [XH[:, NT * D:NT * D + 4608], ring[:, 5376:5376 + 4608]]
        Pb = [[x[:, b * 1536:(b + 1) * 1536].rearrange("p (c n) -> p c n", c=2) for b in range(2)] for x in pbase]
        Prow = [[Pb[L][n // 2][:, n % 2] for n in range(4)] for L in range(2)]
        PTs = [[x[:, 3072 + b * 768:3072 + (b + 1) * 768] for b in range(2)] for x in pbase]
        Oe = [ring[:, 3 * U + b * D:3 * U + (b + 1) * D] for b in range(2)]
        Oo = [ring[:, t * D:(t + 1) * D] for t in range(NT)]
        OT = [ring[:, 3 * U + 2 * D:3 * U + 3 * D], ring[:, 9984:9984 + D]]
        xin = [ring[:, 3 * U + 3 * D:3 * U + 4 * D], ring[:, 9984 + D:9984 + 2 * D]]
        lg = Z[:, 0:80]
        lge = Z[:, 80:160]
        aff = Z[:, 160:240]
        affT = Z[0:NE, 256:256 + NTOK]
        topv = Z[0:NE, 1024:1024 + SLOTS]
        topi = Z[0:NE, 1152:1152 + SLOTS].bitcast(U32)
        topf = Z[0:NE, 1280:1280 + SLOTS]
        xe = [Z[0:SLOTS, 2048 + b * D:2048 + (b + 1) * D] for b in range(2)]
        xeT = [Z[:, 4096 + b * 640:4096 + (b + 1) * 640].rearrange("p (k n) -> p k n", k=KD) for b in range(2)]
        AXs = Z[:, 5376:6016].rearrange("p (k n) -> p k n", k=KD)
        BXs = Z[:, 6016:6656].rearrange("p (k n) -> p k n", k=KD)
        sg = [Z[:, 6656 + b * 320:6656 + (b + 1) * 320] for b in range(2)]
        hid = [Z[:, 7296 + b * 320:7296 + (b + 1) * 320] for b in range(2)]
        g2b = Z[0:SLOTS, 7936:8960]
        GXs = HT
        gx = XH[:, NT * D:NT * D + 640].rearrange("p (k n) -> p k n", k=KD)
        ys = [GB[0:SLOTS, b * D:(b + 1) * D] for b in range(2)]
        fin = Z[:, 0:D]

        S = [ps("S0", [P, 1024]), ps("S1", [P, 1024])]
        T = ps("T", [P, 1024])
        place = {"S0": S[0][:], "S1": S[1][:], "PT": T[:], "PV": ps("V", [P, 512])[:], "AD": ps("A", [P, 512])[:]}
        full = {r: sem("psum_full_" + r) for r in place}
        free = {r: sem("psum_free_" + r) for r in place}
        uses = {r: 0 for r in place}
        slot = {}

        def claim(tag, r):
            uses[r] += 1
            slot[tag] = (r, uses[r])
            if uses[r] > 1:
                pe.wait_ge(free[r], uses[r] - 1)
            return place[r]

        def filled(eng, tag):
            r, n = slot[tag]
            eng.wait_ge(full[r], n)
            return place[r]

        def emptied(eng, tag):
            r, n = slot[tag]
            eng.wait_ge(free[r], n)

        def full_of(tag):
            return full[slot[tag][0]]

        def free_of(tag):
            return free[slot[tag][0]]

        consts_in, vec_in, small_in = sem("consts_in"), sem("vec_in"), sem("small_in")
        x_in = [sem(f"x_in{t}") for t in range(NT)]
        x_back = [sem(f"x_back{t}") for t in range(NT)]
        ada_first = [sem(f"ada_first{i}") for i in range(3)]
        ada_in = sem("ada_in")
        win_in = [sem(f"win_in{c}") for c in range(5)]
        ctx_in, wout_in = sem("ctx_in"), sem("wout_in")
        odd_in, qup_in, kvup_in, ctxo_in = sem("odd_in"), sem("qup_in"), sem("kvup_in"), sem("ctxo_in")
        csil_ready, mod_ready = sem("csil_ready"), sem("mod_ready")
        ssq_done, rstd_done, xn_done = sem("ssq_done"), sem("rstd_done"), sem("xn_done")
        rope_done = sem("rope_done")
        prompt_out = sem("prompt_out")
        lam_ready, lam_exp = sem("lam_ready"), sem("lam_exp")
        nm_done, snk_done, sne_done = sem("nm_done"), sem("snk_done"), sem("sne_done")
        comb_done = sem("comb_done")
        sub_ss, sub_rstd, o_ready = sem("sub_ss"), sem("sub_rstd"), sem("o_ready")
        xin_in, x1_done = sem("xin_in"), sem("x1_done")
        x1_out, xn_out = sem("x1_out"), sem("xn_out")
        dve_step, act_step, pool_step = sem("dve_step"), sem("act_step"), sem("pool_step")
        lge_done, aff_ready, top_ready = sem("lge_done"), sem("aff_ready"), sem("top_ready")
        ax_ready, g2_ready = sem("ax_ready"), sem("g2_ready")
        wg_in = [sem(f"wg_in{b}") for b in range(2)]
        wu_in = [sem(f"wu_in{b}") for b in range(2)]
        wd_in = [sem(f"wd_in{b}") for b in range(2)]
        idxe_ready, gather_go, add_go = sem("idxe_ready"), sem("gather_go"), sem("add_go")
        xe_in = [sem(f"xe_in{b}") for b in range(2)]
        added = [sem(f"added{b}") for b in range(2)]
        xt_mm, xt_read, xt_ready = sem("xt_mm"), sem("xt_read"), sem("xt_ready")
        gate_mm, up_mm, down_mm = sem("gate_mm"), sem("up_mm"), sem("down_mm")
        silu_done, hid_ready, y_scaled = sem("silu_done"), sem("hid_ready"), sem("y_scaled")
        cq_ready, qr_ready = sem("cq_ready"), sem("qr_ready")
        krs_done = sem("krs_done")
        fin_in, y_ready, y_out = sem("fin_in"), sem("y_ready"), sem("y_out")

        steps = {"dve": 0, "act": 0, "pool": 0}

        def dlink(ins):
            steps["dve"] += 1
            ins.then_inc(dve_step, 1)
            dve.wait_ge(dve_step, steps["dve"])

        def plink(ins):
            steps["pool"] += 1
            ins.then_inc(pool_step, 1)
            pool.wait_ge(pool_step, steps["pool"])

        def wait(eng, s, n):
            if not isinstance(n, int) or n > 0:
                eng.wait_ge(s, n)

        def spread(ap, n):
            return ap.rearrange("p (k a) -> p k a", a=1).to_broadcast([ap.shape[0], ap.shape[1], n])

        def over_heads(ap, heads):
            return ap.rearrange("p (a n) -> p a n", a=1).to_broadcast([ap.shape[0], heads, ap.shape[1]])

        class Plan:

            def __init__(self, layer, units, extra, tail):
                self.layer, self.units, self.extra, self.n = layer, units, extra, len(units)
                self.steps = self.n + tail
                self.parts = []
                self.of_unit = []
                self.read_at = []
                for u, (kind, t, i, c) in enumerate(units):
                    mine = None
                    self.read_at.append(len(self.parts))
                    if kind != "diff" or c == 1:
                        mine = len(self.parts)
                        self.parts.append(u - 1 if kind == "diff" else u)
                    self.of_unit.append(mine)

            def keys(self, u):
                kind, t = self.units[u][:2]
                if t == TS:
                    return [KT - 1]
                if kind == "swa":
                    return [0, 1] + [2 + s for s in range(max(t - 1, 0), min(t + 2, TS))]
                return list(range(NKEY // P))

        per_tile = [(k, i, c) for k in ("diff", "swa") for i in range(4) for c in range(2)]
        even_units = [(k, t, i, c) for t in range(NT) for k, i, c in per_tile]
        even_extra = {}
        for t in range(NT):
            last = 16 * t + 15
            even_extra.setdefault(last + 2, []).append(("norm_o", t))
            even_extra.setdefault(last + 4, []).append(("turn_o", t))
            even_extra.setdefault(last + 6, []).append(("out", t))
        ADA_PROJ = 10
        for n in range(20 - ADA_PROJ):
            even_extra.setdefault(6 * n, []).append(("ada", 4 + ADA_PROJ + n))
        even = Plan(0, even_units, even_extra, 7)
        odd_units = [("mla", t, p, c) for p in range(MH // 2) for t in range(NT) for c in range(2)]
        PAIR = 2 * NT
        odd_extra = {}
        for p in range(1, MH // 2):
            odd_extra.setdefault(PAIR * (p - 1) + 2, []).append(("kv", p))
        for t in range(NT):
            odd_extra.setdefault(PAIR * (MH // 2) + 1 + t, []).append(("turn_o", t))
            odd_extra.setdefault(PAIR * (MH // 2) + 2 + t, []).append(("out", t))
        odd = Plan(1, odd_units, odd_extra, 7)
        plans = [even, odd]
        units_before = [0, even.n]

        def diff_number(u):
            return sum(1 for k, _, _, c in even_units[:u + 1] if k == "diff" and c == 1)

        def swa_number(u):
            return sum(1 for k, _, _, _ in even_units[:u + 1] if k == "swa")

        def v_width(kind):
            return P if kind == "diff" else HD

        def values(L, k, kt):
            kind, t, i, c = plans[L].units[plans[L].parts[k]]
            if kind == "diff":
                return va[:, kt, i * P:(i + 1) * P]
            if kind == "swa":
                return vb[:, kt, c * HD:(c + 1) * HD]
            return Vh[:, i % 2, kt, c * HD:(c + 1) * HD]

        def o_tile(L, t):
            return Oe[t % 2] if L == 0 else Oo[t]

        def o_cols(L, k):
            kind, t, i, c = plans[L].units[plans[L].parts[k]]
            if kind == "diff":
                return i * P, P
            if kind == "swa":
                return 512 + (i + 4 * c) * HD, HD
            return (2 * i + c) * HD, HD

        def ada_buf(u):
            x = [stage[:, :], XH[:, NT * D:NT * D + U], Z[:, 0:U], Z[:, U:2 * U]][u] if u < 4 else stage[:, :]
            return x.rearrange("p (k n) -> p k n", k=KD)

        block = ctx.enter_context(nc.Block())

        @block.tensor
        def _(_):
            def mm(out, lhsT, rhs, start=True, stop=True):
                return pe.matmul(out, lhsT, rhs, start=start, stop=stop)

            def turn(out, in_):
                return pe.transpose(out, in_, ident[0:in_.shape[0], 0:in_.shape[0]])

            def vectors():
                pe.wait_ge(consts_in, 16)
                pe.wait_ge(vec_in, 16 * 11)
                s = claim("vec", "S0")
                turn(s[:, 0:P], VR[:, 0, :])
                turn(s[:, P:P + 22], VR[0:22, 1, :]).then_inc(full["S0"], 1)

            def ada(u):
                s = claim(("ada", u), "AD")
                if u == 0:
                    pe.wait_ge(csil_ready, 1)
                if 0 < u < 4:
                    pe.wait_ge(ada_first[u - 1], 16)
                else:
                    pe.wait_ge(ada_in, 16 * (1 if u == 0 else u - 2))
                w = ada_buf(u)
                for j in range(4):
                    for k in range(KD):
                        ins = mm(s[:, 2 * j:2 * j + 2], w[:, k, j * P:(j + 1) * P], csil[:, k:16:KD], k == 0, k == KD - 1)
                ins.then_inc(full["AD"], 1)

            def turn_x(n):
                for k in range(KD):
                    s = claim(("nt", n, k), ("S0", "S1", "PT")[k % 3])
                    for t in range(TS):
                        if k == 0:
                            pe.wait_ge(xn_done, NT * n + t + 1)
                        ins = turn(s[:, t * P:(t + 1) * P], X[:, t, k * P:(k + 1) * P])
                    ins.then_inc(full_of(("nt", n, k)), 1)
                pe.wait_ge(xn_done, NT * n + NT)
                for g in range(2):
                    s = claim(("ntp", n, g), ("S0", "S1")[g])
                    for j in range(4):
                        k = 4 * g + j
                        ins = turn(s[:, j * P:(j + 1) * P], X[:, TS, k * P:(k + 1) * P])
                    ins.then_inc(full_of(("ntp", n, g)), 1)

            def wait_ht(n):
                emptied(pe, ("ntp", n, 0))
                emptied(pe, ("ntp", n, 1))

            def even_project():
                n = [0]

                def region():
                    n[0] += 1
                    return ("S0", "S1", "PT")[n[0] % 3]

                def project(t):
                    for c in range(5):
                        w = 512 if c < 4 else 256
                        tag = ("proj", t, c)
                        s = claim(tag, region())
                        if t == 0:
                            pe.wait_ge(win_in[c], 16)
                        for k in range(KD):
                            ins = mm(s[:, 0:w], HT[:, k, t * P:(t + 1) * P], w_in_e[:, k, c * 512:c * 512 + w], k == 0, k == KD - 1)
                        ins.then_inc(full_of(tag), 1)

                def turn_qk(t):
                    r = raw[t % 2]
                    if t < TS:
                        pe.wait_ge(rope_done, t + 1)
                    else:
                        emptied(pe, ("proj", t, 4))
                    s = claim(("qT", t), region())
                    for h in range(4):
                        ins = turn(s[:, h * P:(h + 1) * P], r[:, h * P:(h + 1) * P])
                    ins.then_inc(full_of(("qT", t)), 1)
                    s = claim(("kT", t), region())
                    for h in range(4):
                        ins = turn(s[:, h * P:(h + 1) * P], r[:, 512 + h * P:512 + (h + 1) * P])
                    ins.then_inc(full_of(("kT", t)), 1)
                    s = claim(("qbT", t), region())
                    for h in range(4):
                        ins = turn(s[:, h * P:(h + 1) * P], r[:, 1024 + h * P:1024 + (h + 1) * P])
                    ins.then_inc(full_of(("qbT", t)), 1)
                    s = claim(("kbT", t), region())
                    turn(s[:, 0:P], r[:, 1536:1664]).then_inc(full_of(("kbT", t)), 1)

                pe.wait_ge(ctx_in, 16 * 4)
                for j in range(2):
                    s = claim(("ckT", j), region())
                    for h in range(4):
                        ins = turn(s[:, h * P:(h + 1) * P], ctx_k[:, j, h * P:(h + 1) * P])
                    ins.then_inc(full_of(("ckT", j)), 1)
                s = claim("cksT", region())
                for j in range(2):
                    ins = turn(s[:, j * P:(j + 1) * P], ctx_ks[:, j, :])
                ins.then_inc(full_of("cksT"), 1)
                wait_ht(0)
                for t in range(NT):
                    project(t)
                    if t > 0:
                        turn_qk(t - 1)
                    ada(4 + 2 * t)
                    ada(5 + 2 * t)
                turn_qk(NT - 1)

            def gate_rows(L):
                emptied(pe, ("ada", 12 * L + 5))
                for s_ in range(2):
                    tag = ("gb", L, s_)
                    s = claim(tag, ("S0", "S1")[s_])
                    for k in range(KD):
                        ins = mm(s[:, k * P:(k + 1) * P], mods[:, L, 2, k, s_:s_ + 1].to_broadcast([P, P]), ident)
                    ins.then_inc(full_of(tag), 1)

            def odd_project():
                pe.wait_ge(ctxo_in, 16 * 3)
                s = claim("occ", "PT")
                for j in range(2):
                    for k in range(2):
                        ins = turn(s[:, (2 * k + j) * P:(2 * k + j + 1) * P], ctx_c[:, j, k * P:(k + 1) * P])
                ins.then_inc(full["PT"], 1)
                s = claim("ocr", "S0")
                for j in range(2):
                    ins = turn(s[0:RD, j * P:(j + 1) * P], ctx_r[:, j, :])
                ins.then_inc(full["S0"], 1)
                wait_ht(2)
                pe.wait_ge(odd_in, 16)

                def project(t):
                    s = claim(("oproj", t), ("S0", "S1")[t % 2])
                    for c0, w in ((0, 512), (512, ODD_IN - 512)):
                        for k in range(KD):
                            ins = mm(s[:, c0:c0 + w], HT[:, k, t * P:(t + 1) * P], w_in_o[:, k, c0:c0 + w], k == 0, k == KD - 1)
                    ins.then_inc(full_of(("oproj", t)), 1)

                def turn_c(t):
                    pe.wait_ge(cq_ready, t + 1)
                    s = claim(("oc", t), "PT")
                    for k in range(5):
                        ins = turn(s[:, k * P:(k + 1) * P], rawo[t % 2][:, k * P:(k + 1) * P])
                    ins = turn(s[0:RD, 5 * P:6 * P], rawo[t % 2][:, 640:672])
                    ins.then_inc(full["PT"], 1)

                for t in range(NT):
                    project(t)
                    if t > 0:
                        turn_c(t - 1)
                turn_c(NT - 1)

                def q_up(t):
                    for c in range(3):
                        s = claim(("qup", t, c), ("S0", "S1")[(t + c) % 2])
                        for k in range(3):
                            ins = mm(s[:, 0:512], cqT[:, k, t * P:(t + 1) * P], w_qup[:, k, c * 512:(c + 1) * 512], k == 0, k == 2)
                        ins.then_inc(full_of(("qup", t, c)), 1)

                def turn_q(t):
                    if t < TS:
                        pe.wait_ge(qr_ready, t + 1)
                    else:
                        emptied(pe, ("qup", t, 2))
                    for g in range(4):
                        s = claim(("oq", t, g), "PT")
                        for j in range(4):
                            h = 4 * g + j
                            ins = turn(s[0:MQ, j * P:(j + 1) * P], qraw[t % 2][:, h * MQ:(h + 1) * MQ])
                        ins.then_inc(full["PT"], 1)

                pe.wait_ge(qup_in, 16)
                for t in range(NT):
                    if t == 0:
                        emptied(pe, ("oc", NT - 1))
                    q_up(t)
                    if t > 0:
                        turn_q(t - 1)
                turn_q(NT - 1)

            def kv(p):
                if p == 0:
                    pe.wait_ge(kvup_in, 16 * 4)
                s = claim(("kT2", p), ("S0", "S1")[p % 2])
                for c0, w in ((0, 512), (512, KCOL - 512)):
                    for k in range(2):
                        ins = mm(s[:, c0:c0 + w], w_kvup[:, k, p * P:(p + 1) * P], ckvT[:, k, c0:c0 + w], k == 0, k == 1)
                ins.then_inc(full_of(("kT2", p)), 1)
                s = claim(("v2", p), ("S1", "S0")[p % 2])
                for kt in range(KT):
                    for k in range(2):
                        ins = mm(s[:, kt * P:(kt + 1) * P], ckvT[:, k, kt * P:(kt + 1) * P], w_kvup[:, k, D + p * P:D + (p + 1) * P], k == 0, k == 1)
                ins.then_inc(full_of(("v2", p)), 1)

            def scores(L, u):
                pl = plans[L]
                kind, t, i, c = pl.units[u]
                s = claim(("s", L, u), ("S0", "S1")[u % 2])
                keys = pl.keys(u)
                runs = []
                for n, kt in enumerate(keys):
                    if runs and runs[-1][1] + runs[-1][2] == kt:
                        runs[-1][2] += 1
                    else:
                        runs.append([n, kt, 1])
                for n, kt, cnt in runs:
                    for o, w in bank_pieces(n * P, cnt * P):
                        k0 = kt * P + o - n * P
                        if kind == "diff":
                            q, ks = QTe[c * HD:(c + 1) * HD, t, i, :], kaT[c * HD:(c + 1) * HD, i, k0:k0 + w]
                        elif kind == "swa":
                            q, ks = QTe[c * HD:(c + 1) * HD, t, 4 + i, :], kbT[c * HD:(c + 1) * HD, k0:k0 + w]
                        else:
                            q, ks = QTo[:, 2 * i + c, t * P:(t + 1) * P], KTh[:, i % 2, c, k0:k0 + w]
                        masks = []
                        if kind == "swa" and t < TS:
                            for m, kk in enumerate(keys):
                                if kk >= 2 and o <= m * P < o + w and kk - 2 != t:
                                    masks.append((m * P, C[:, C_LEFT:C_LEFT + P] if kk - 2 < t else C[:, C_RIGHT:C_RIGHT + P]))
                        ins = mm(s[:, o:o + w], q, ks, True, not masks)
                        for x, (at, mask) in enumerate(masks):
                            ins = pe.matmul(s[:, at:at + P], ident, mask, start=False, stop=x == len(masks) - 1)
                ins.then_inc(full_of(("s", L, u)), 1)

            def turn_p(L, k):
                pl = plans[L]
                u = pl.parts[k]
                if pl.units[u][0] == "diff":
                    pe.wait_ge(comb_done, diff_number(u + 1))
                else:
                    emptied(pe, ("s", L, u))
                s = claim(("pt", L, k), "PT")
                for n in range(len(pl.keys(u))):
                    ins = turn(s[:, n * P:(n + 1) * P], Prow[L][u % 4][:, n * P:(n + 1) * P])
                ins.then_inc(full["PT"], 1)

            def pv(L, k):
                pl = plans[L]
                u = pl.parts[k]
                keys = pl.keys(u)
                s = claim(("pv", L, k), "PV")
                emptied(pe, ("pt", L, k))
                w = v_width(pl.units[u][0])
                for n, kt in enumerate(keys):
                    ins = mm(s[:, 0:w], PTs[L][k % 2][:, n * P:(n + 1) * P], values(L, k, kt), n == 0, n == len(keys) - 1)
                ins.then_inc(full["PV"], 1)

            def turn_o(L, t):
                if L == 0:
                    pe.wait_ge(o_ready, t + 1)
                else:
                    emptied(pe, ("pv", 1, len(odd.parts) - 1))
                s = claim(("oT", L, t), "S0" if t % 2 else "S1")
                for k in range(KD):
                    ins = turn(s[:, k * P:(k + 1) * P], o_tile(L, t)[:, k * P:(k + 1) * P])
                ins.then_inc(full_of(("oT", L, t)), 1)

            def out(L, t):
                if t == 0:
                    pe.wait_ge(wout_in, 16 * (L + 1))
                emptied(pe, ("oT", L, t))
                s = claim(("out", L, t), "S0" if t % 2 else "S1")
                for c in range(2):
                    for k in range(KD):
                        ins = mm(s[:, c * 512:(c + 1) * 512], OT[L][:, k * P:(k + 1) * P], w_out[:, k, c * 512:(c + 1) * 512], k == 0, k == KD - 1)
                ins.then_inc(full_of(("out", L, t)), 1)

            def attention(L):
                pl = plans[L]
                if L == 0:
                    emptied(pe, ("qbT", NT - 1))
                    emptied(pe, ("kbT", NT - 1))
                else:
                    emptied(pe, ("oq", NT - 1, 3))
                    emptied(pe, ("kT2", 0))
                    emptied(pe, ("v2", 0))
                scores(L, 0)
                k_done = 0
                for i in range(pl.steps):
                    if i + 1 < pl.n:
                        if L == 1 and (i + 1) % PAIR == 0:
                            emptied(pe, ("kT2", (i + 1) // PAIR))
                            emptied(pe, ("v2", (i + 1) // PAIR))
                        scores(L, i + 1)
                    if i < pl.n:
                        k = pl.of_unit[i]
                        if k is not None:
                            turn_p(L, k)
                            if k > 0:
                                pv(L, k - 1)
                    elif i == pl.n:
                        pv(L, len(pl.parts) - 1)
                    for what, n in pl.extra.get(i, []):
                        if what == "ada":
                            ada(n)
                        elif what == "kv":
                            kv(n)
                        elif what == "turn_o":
                            turn_o(L, n)
                        elif what == "out":
                            out(L, n)

            def router(L):
                wait_ht(2 * L + 1)
                if L == 0:
                    pe.wait_ge(small_in, 16 * 4)
                s = claim(("lg", L), "S0")
                for t in range(NT):
                    for k in range(KD):
                        ins = mm(s[:, t * NE:(t + 1) * NE], HT[:, k, t * P:(t + 1) * P], wr[:, L, k, :], k == 0, k == KD - 1)
                ins.then_inc(full["S0"], 1)
                pe.wait_ge(aff_ready, L + 1)
                s = claim(("affT", L), "S1")
                for t in range(NT):
                    ins = turn(s[0:NE, t * P:(t + 1) * P], aff[:, t * NE:(t + 1) * NE])
                ins.then_inc(full["S1"], 1)
                pe.wait_ge(ax_ready, L + 1)
                s = claim(("g2", L), "S0")
                for k in range(KD):
                    ins = mm(s[0:SLOTS, k * P:(k + 1) * P], gx[:, k, :], ident)
                ins.then_inc(full["S0"], 1)
                pe.wait_ge(top_ready, L + 1)
                s = claim(("idx", L), "PT")
                turn(s[0:SLOTS, 0:NE], topv)
                turn(s[0:SLOTS, NE:2 * NE], topf).then_inc(full["PT"], 1)
                for r in place:
                    if uses[r]:
                        pe.wait_ge(free[r], uses[r])

            def experts(L):
                G, Up, XT = S[1][:, 0:320], S[1][:, 512:832], S[0][:, 0:1024].rearrange("p (k n) -> p k n", k=KD)
                base, half = L * NE, L * NE // 2

                def turn_xe(i, b, e):
                    pe.wait_ge(xe_in[b], 16 * (half + i + 1))
                    wait(pe, xt_read, base + e)
                    for k in range(KD):
                        ins = turn(XT[:, k, 0:SLOTS], xe[b][:, k * P:(k + 1) * P])
                    ins.then_inc(xt_mm, 1)

                def expert(i, b, last):
                    e = 2 * i + b
                    wg = ring[:, (3 * b) * U:(3 * b + 1) * U].rearrange("p (k n) -> p k n", k=KD)
                    wu = ring[:, (3 * b + 1) * U:(3 * b + 2) * U].rearrange("p (k n) -> p k n", k=KD)
                    wd = ring[:, (3 * b + 2) * U:(3 * b + 3) * U].rearrange("p (k n) -> p k n", k=4)
                    pe.wait_ge(xt_ready, base + e + 1)
                    wait(pe, silu_done, base + e)
                    pe.wait_ge(wg_in[b], 16 * (half + i + 1))
                    for f in range(4):
                        for k in range(KD):
                            ins = mm(G[:, f * SLOTS:(f + 1) * SLOTS], wg[:, k, f * P:(f + 1) * P], xeT[b][:, k, :], k == 0, k == KD - 1)
                    ins.then_inc(gate_mm, 1)
                    wait(pe, hid_ready, base + e)
                    pe.wait_ge(wu_in[b], 16 * (half + i + 1))
                    for f in range(4):
                        for k in range(KD):
                            ins = mm(Up[:, f * SLOTS:(f + 1) * SLOTS], wu[:, k, f * P:(f + 1) * P], xeT[b][:, k, :], k == 0, k == KD - 1)
                    ins.then_inc(up_mm, 1)
                    if not last:
                        turn_xe(i + b, 1 - b, e + 1)
                    pe.wait_ge(hid_ready, base + e + 1)
                    wait(pe, y_scaled, base + e)
                    pe.wait_ge(wd_in[b], 16 * (half + i + 1))
                    for c in range(2):
                        for f in range(4):
                            ins = mm(T[0:SLOTS, c * 512:(c + 1) * 512], hid[b][:, f * SLOTS:(f + 1) * SLOTS], wd[:, f, c * 512:(c + 1) * 512], f == 0, f == 3)
                    ins.then_inc(down_mm, 1)

                turn_xe(0, 0, 0)
                expert(0, 0, False)
                expert(0, 1, False)
                with pe.Fori(1, NE // 2 - 1, 1) as i:
                    expert(i, 0, False)
                    expert(i, 1, False)
                expert(NE // 2 - 1, 0, False)
                expert(NE // 2 - 1, 1, True)
                pe.wait_ge(y_scaled, base + NE)

            vectors()
            for u in range(4):
                ada(u)
            turn_x(0)
            even_project()
            gate_rows(0)
            attention(0)
            turn_x(1)
            router(0)
            experts(0)
            turn_x(2)
            odd_project()
            kv(0)
            gate_rows(1)
            attention(1)
            turn_x(3)
            router(1)
            experts(1)

        @block.vector
        def _(_):
            def ada_out(u):
                L, m, half = u // 12, (u % 12) // 2, u % 2
                s = filled(dve, ("ada", u))
                dst = mods[:, L, m, 4 * half:4 * half + 4, :]
                bias = VC1[:, 64 * L + 8 * m + 4 * half:64 * L + 8 * m + 4 * half + 4]
                dve.tensor_tensor(dst, s[:, 0:8].rearrange("p (k s) -> p k s", s=2), spread(bias, 2), ALU.add).then_inc(free["AD"], 1)
                if m in (1, 4):
                    gain = VC1[:, 64 * L + 48 + 8 * (m == 4) + 4 * half:64 * L + 52 + 8 * (m == 4) + 4 * half]
                    dve.wait_ge(free["AD"], u + 1)
                    dve.scalar_tensor_tensor(modA[:, L, int(m == 4), 4 * half:4 * half + 4, :], dst, 1.0, spread(gain, 2),
                                             ALU.add, ALU.mult).then_inc(mod_ready, 1)

            def scale_x(n):
                for t in range(NT):
                    if n in (1, 3):
                        dve.wait_ge(x1_out, 16 * (NT * (n // 2) + NT))
                    dve.wait_ge(rstd_done, NT * n + t + 1)
                    dve.tensor_scalar(X[:, t, :], X[:, t, :], rstd[:, t:t + 1], None, ALU.mult).then_inc(xn_done, 1)

            def ht(n):
                L, w = n // 2, n % 2
                dve.wait_ge(mod_ready, 2 * (n + 1))
                for k in range(1, KD, 2):
                    s = filled(dve, ("nt", n, k))
                    dve.tensor_scalar(HT[:, k, 0:NS], s[:, 0:NS], modA[:, L, w, k, 0:1], mods[:, L, 3 * w, k, 0:1], ALU.mult, ALU.add)\
                       .then_inc(free_of(("nt", n, k)), 1)
                s = filled(dve, ("ntp", n, 1))
                for j in range(4):
                    k = 4 + j
                    ins = dve.tensor_scalar(HT[:, k, NS:NTOK], s[:, j * P:(j + 1) * P], modA[:, L, w, k, 1:2], mods[:, L, 3 * w, k, 1:2],
                                            ALU.mult, ALU.add)
                ins.then_inc(free_of(("ntp", n, 1)), 1)

            dve.wait_ge(small_in, 16 * 4)
            dlink(dve.memset(coef[:, 0:1], 1.0))
            s = filled(dve, "vec")
            dve.tensor_copy(VC1[:], s[:, 0:P])
            dve.tensor_copy(VC2[:], s[:, P:P + 22]).then_inc(free["S0"], 1)
            dve.wait_ge(free["S0"], 1)
            lq = lamv[:].rearrange("p (a b n) -> p a b n", a=2, b=2)
            lprod = GB[:, 1280:1408]
            dlink(dve.tensor_tensor(lprod.rearrange("p (a n) -> p a n", a=2), lq[:, :, 0, :], lq[:, :, 1, :], ALU.mult))
            dve.tensor_reduce(lam2[:], lprod.rearrange("p (a n) -> p a n", a=2), AX, ALU.add).then_inc(lam_ready, 1)
            dve.tensor_scalar(sink8[:], sink[:], 8.0, None, ALU.mult)
            dlink(dve.tensor_scalar(VC2[:, 21:22], VC2[:, 21:22], 1.0 - LAM_INIT, None, ALU.mult))
            for u in range(4):
                ada_out(u)
            scale_x(0)
            ht(0)
            dve.wait_ge(lam_exp, 1)
            dlink(dve.tensor_tensor(coef[:, 1:2], lame[:, 1:2], lame[:, 0:1], ALU.subtract))
            dlink(dve.tensor_scalar(coef[:, 1:2], coef[:, 1:2], -LAM_INIT, None, ALU.add))

            def rope(dst, tmp, cos, sin, heads, quarter, done):
                width = 4 * quarter
                d4 = dst.rearrange("p h (r x q) -> p h r x q", r=2, x=2)
                t4 = tmp.rearrange("p h (r x q) -> p h r x q", r=2, x=2)
                s4 = over_heads(sin, heads).rearrange("p h (r x q) -> p h r x q", r=2, x=2)
                for x in range(2):
                    ins = dve.tensor_tensor(t4[:, :, :, x, :], d4[:, :, :, 1 - x, :], s4[:, :, :, x, :], ALU.mult)
                dlink(ins)
                dlink(dve.tensor_tensor(dst, dst, over_heads(cos, heads), ALU.mult))
                dve.tensor_tensor(dst, dst, tmp, ALU.add).then_inc(done, 1)

            for j in range(2):
                s = filled(dve, ("ckT", j))
                dve.tensor_copy(kaT[:, :, j * P:(j + 1) * P], s[:, 0:512].rearrange("p (h n) -> p h n", h=4)).then_inc(free_of(("ckT", j)), 1)
            s = filled(dve, "cksT")
            dve.tensor_copy(kbT[:, 0:PAST], s[:, 0:PAST]).then_inc(free_of("cksT"), 1)

            def k_turned(t):
                kt = t + 2
                s = filled(dve, ("kT", t))
                dve.tensor_copy(kaT[:, :, kt * P:(kt + 1) * P], s[:, 0:512].rearrange("p (h n) -> p h n", h=4)).then_inc(free_of(("kT", t)), 1)
                s = filled(dve, ("kbT", t))
                dve.tensor_copy(kbT[:, kt * P:(kt + 1) * P], s[:, 0:P]).then_inc(free_of(("kbT", t)), 1)

            for t in range(NT):
                if t > 0:
                    k_turned(t - 1)
                ada_out(4 + 2 * t)
                ada_out(5 + 2 * t)
                if t < TS:
                    emptied(dve, ("proj", t, 4))
                    rope(raw[t % 2].rearrange("p (h n) -> p h n", n=HD), rtmp.rearrange("p (h n) -> p h n", n=HD),
                         C[:, C_C64 + 64 * t:C_C64 + 64 * (t + 1)], C[:, C_S64 + 64 * t:C_S64 + 64 * (t + 1)], QK // HD, 16, rope_done)
            k_turned(NT - 1)

            def row_max(L, u):
                pl = plans[L]
                kind, t, i, c = pl.units[u]
                nk = len(pl.keys(u)) * P
                b = u % 4
                s = filled(dve, ("s", L, u))[:, 0:nk]
                g = units_before[L] + u
                if u >= 4:
                    emptied(dve, ("s", L, u - 4))
                    if pl.units[u - 4][0] == "swa":
                        dve.wait_ge(sne_done, swa_number(u - 4))
                dlink(dve.tensor_reduce(mx[:, b:b + 1], s, AX, ALU.max))
                scale = -(HD ** -0.5) if L == 0 else -(MQ ** -0.5)
                if kind == "swa":
                    h = i + 4 * c
                    dve.tensor_scalar(nm[:, b:b + 1], mx[:, b:b + 1], sink8[:, h:h + 1], scale, ALU.max, ALU.mult).then_inc(nm_done, 1)
                    dve.wait_ge(nm_done, g + 1)
                    dve.tensor_tensor(snk[:, b:b + 1], sink[:, h:h + 1], nm[:, b:b + 1], ALU.add).then_inc(snk_done, 1)
                else:
                    dve.tensor_scalar(nm[:, b:b + 1], mx[:, b:b + 1], scale, None, ALU.mult).then_inc(nm_done, 1)

            def combine(L, u):
                pl = plans[L]
                kind, t, i, c = pl.units[u]
                nk = len(pl.keys(u)) * P
                b = u % 4
                emptied(dve, ("s", L, u))
                if kind == "swa":
                    dve.wait_ge(sne_done, swa_number(u))
                    dlink(dve.tensor_tensor(den[:, b:b + 1], den[:, b:b + 1], sne[:, b:b + 1], ALU.add))
                dlink(dve.reciprocal(rr[:, b:b + 1], den[:, b:b + 1]))
                if kind == "diff" and c == 1:
                    p0, p1 = Prow[L][b - 1][:, 0:nk], Prow[L][b][:, 0:nk]
                    dlink(dve.tensor_scalar(p1, p1, rr[:, b:b + 1], coef[:, 1:2], ALU.mult, ALU.mult))
                    dve.scalar_tensor_tensor(p0, p0, rr[:, b - 1:b], p1, ALU.mult, ALU.add).then_inc(comb_done, 1)

            def pv_read(L, k):
                pl = plans[L]
                u = pl.parts[k]
                kind, t, i, c = pl.units[u]
                s = filled(dve, ("pv", L, k))
                c0, w = o_cols(L, k)
                o = o_tile(L, t)
                if L == 0 and t >= 2:
                    filled(dve, ("oT", L, t - 2))
                if kind == "diff":
                    dve.tensor_copy(o[:, c0:c0 + w], s[:, 0:w]).then_inc(free["PV"], 1)
                else:
                    dve.tensor_scalar(o[:, c0:c0 + w], s[:, 0:w], rr[:, u % 4:u % 4 + 1], None, ALU.mult).then_inc(free["PV"], 1)

            def norm_o(t):
                o = Oe[t % 2]
                emptied(dve, ("pv", 0, even.of_unit[16 * t + 15]))
                o3 = o[:, 0:512].rearrange("p (h n) -> p h n", h=4)
                for h in range(4):
                    ins = dve.scalar_tensor_tensor(sqs[:, h * P:(h + 1) * P], o3[:, h, :], 1.0, o3[:, h, :], ALU.mult, ALU.mult, accum_out=sub4[:, h:h + 1])
                ins.then_inc(sub_ss, 1)
                dve.wait_ge(sub_rstd, t + 1)
                dve.tensor_tensor(o3, o3, spread(subr[:], P), ALU.mult).then_inc(o_ready, 1)

            def o_turned(L, t):
                if L == 0:
                    s = filled(dve, ("oT", L, t))
                    if t > 0:
                        filled(dve, ("out", L, t - 1))
                    dve.tensor_scalar(OT[L][:, 0:512], s[:, 0:512], VC2[:, 21:22], None, ALU.mult)
                    dve.tensor_copy(OT[L][:, 512:1024], s[:, 512:1024]).then_inc(free_of(("oT", L, t)), 1)
                else:
                    s = filled(dve, ("oT", L, t))
                    if t > 0:
                        filled(dve, ("out", L, t - 1))
                    dve.tensor_copy(OT[L][:, 0:1024], s[:, 0:1024]).then_inc(free_of(("oT", L, t)), 1)

            def residual(L, t):
                if t == 0:
                    emptied(dve, ("gb", L, 0))
                    emptied(dve, ("gb", L, 1))
                s = filled(dve, ("out", L, t))
                g = GB[:, 0:D] if t < TS else GB[:, D:2 * D]
                dve.wait_ge(xin_in, 16 * (NT * L + t + 1))
                dve.tensor_tensor(X[:, t, :], s[:, 0:D], g, ALU.mult).then_inc(free_of(("out", L, t)), 1)
                emptied(dve, ("out", L, t))
                dve.tensor_tensor(X[:, t, :], X[:, t, :], xin[L], ALU.add).then_inc(x1_done, 1)

            def attention(L):
                pl = plans[L]
                row_max(L, 0)
                for i in range(pl.steps):
                    if i + 1 < pl.n:
                        row_max(L, i + 1)
                    if i < pl.n:
                        combine(L, i)
                        if pl.of_unit[i]:
                            pv_read(L, pl.of_unit[i] - 1)
                    elif i == pl.n:
                        pv_read(L, len(pl.parts) - 1)
                    for what, n in pl.extra.get(i, []):
                        if what == "ada":
                            ada_out(n)
                        elif what == "norm_o":
                            norm_o(n)
                        elif what == "turn_o":
                            o_turned(L, n)
                        elif what == "out":
                            residual(L, n)
                        elif what == "kv":
                            kv_read(n)

            def router(L):
                s = filled(dve, ("lg", L))
                s3 = s[:, 0:NT * NE].rearrange("p (t e) -> p t e", t=NT)
                dlink(dve.tensor_reduce(rs5[:, 0, :], s3, AX, ALU.max))
                dve.tensor_tensor(lg.rearrange("p (t e) -> p t e", t=NT), s3, spread(rs5[:, 0, :], NE), ALU.subtract).then_inc(free["S0"], 1)
                for dst, src in ((AXs, modA[:, L, 1]), (BXs, mods[:, L, 3]), (gx, mods[:, L, 5])):
                    dve.tensor_copy(dst[:, :, 0:CAP_S], spread(src[:, :, 0], CAP_S))
                    ins = dve.tensor_copy(dst[:, :, CAP_S:SLOTS], spread(src[:, :, 1], CAP_P))
                ins.then_inc(ax_ready, 1)
                dve.wait_ge(lge_done, L + 1)
                dlink(dve.tensor_reduce(rs5[:, 1, :], lge.rearrange("p (t e) -> p t e", t=NT), AX, ALU.add))
                dlink(dve.reciprocal(rs5[:, 2, :], rs5[:, 1, :]))
                dve.tensor_tensor(aff.rearrange("p (t e) -> p t e", t=NT), lge.rearrange("p (t e) -> p t e", t=NT),
                                  spread(rs5[:, 2, :], NE), ALU.mult).then_inc(aff_ready, 1)
                s = filled(dve, ("affT", L))
                dve.tensor_copy(affT, s[0:NE, 0:NTOK]).then_inc(free["S1"], 1)
                emptied(dve, ("affT", L))
                s = filled(dve, ("g2", L))
                dve.tensor_copy(g2b, s[0:SLOTS, 0:D]).then_inc(free["S0"], 1)
                for c0, n, w, at in ((0, CAP_S, NS, 0), (NS, CAP_P, NP_, CAP_S)):
                    for r in range(n // 8):
                        v, ix, src = topv[:, at + 8 * r:at + 8 * r + 8], topi[:, at + 8 * r:at + 8 * r + 8], affT[:, c0:c0 + w]
                        dlink(dve.max(v, src))
                        ins = dve.max_index(ix, v, src)
                        if r < n // 8 - 1:
                            dlink(dve.match_replace(src, v, src, -1.0))
                dlink(ins)
                dve.tensor_copy(topf[:, 0:CAP_S], topi[:, 0:CAP_S])
                dlink(dve.tensor_copy(topf[:, CAP_S:SLOTS], topi[:, CAP_S:SLOTS]))
                dve.tensor_scalar(topf[:, CAP_S:SLOTS], topf[:, CAP_S:SLOTS], float(NS), None, ALU.add).then_inc(top_ready, 1)
                s = filled(dve, ("idx", L))
                dve.tensor_copy(gates[:], s[0:SLOTS, 0:NE])
                dve.tensor_copy(idxi[:], s[0:SLOTS, NE:2 * NE]).then_inc(free["PT"], 1)

            def experts(L):
                G, Up, XT = S[1][:, 0:320], S[1][:, 512:832], S[0][:, 0:1024].rearrange("p (k n) -> p k n", k=KD)
                base, half = L * NE, L * NE // 2

                def modulate_xe(b, e):
                    dve.wait_ge(xt_mm, base + e + 1)
                    wait(dve, up_mm, base + e - 1)
                    dve.tensor_tensor(xeT[b], XT[:, :, 0:SLOTS], AXs, ALU.mult).then_inc(xt_read, 1)
                    dve.wait_ge(xt_read, base + e + 1)
                    dve.tensor_tensor(xeT[b], xeT[b], BXs, ALU.add).then_inc(xt_ready, 1)

                def expert(i, b, last):
                    e = 2 * i + b
                    dve.wait_ge(silu_done, base + e + 1)
                    dve.wait_ge(up_mm, base + e + 1)
                    wait(dve, down_mm, base + e - 1)
                    dve.tensor_tensor(hid[b], sg[b], Up, ALU.mult).then_inc(hid_ready, 1)
                    if not last:
                        modulate_xe(1 - b, e + 1)
                    dve.wait_ge(down_mm, base + e + 1)
                    wait(dve, added[b], 16 * (half + i))
                    dve.scalar_tensor_tensor(ys[b], T[0:SLOTS, 0:D], gates[:, bass.ds(e, 1)] if not isinstance(e, int) else gates[:, e:e + 1],
                                             g2b, ALU.mult, ALU.mult).then_inc(y_scaled, 1)

                dve.wait_ge(free["S0"], slot[("g2", L)][1])
                modulate_xe(0, 0)
                expert(0, 0, False)
                expert(0, 1, False)
                with dve.Fori(1, NE // 2 - 1, 1) as i:
                    expert(i, 0, False)
                    expert(i, 1, False)
                expert(NE // 2 - 1, 0, False)
                expert(NE // 2 - 1, 1, True)

            def odd_project():
                s = filled(dve, "occ")
                dve.tensor_copy(ckvT[:, :, 0:PAST], s[:, 0:512].rearrange("p (k n) -> p k n", k=2)).then_inc(free["PT"], 1)
                s = filled(dve, "ocr")
                dve.tensor_copy(krT[:, 0:PAST], s[0:RD, 0:PAST]).then_inc(free["S0"], 1)

                def c_turned(t):
                    kt = t + 2
                    s = filled(dve, ("oc", t))
                    for k in range(3):
                        dve.tensor_scalar(cqT[:, k, t * P:(t + 1) * P], s[:, k * P:(k + 1) * P], VC2[:, 16 + k:17 + k], None, ALU.mult)
                    dve.tensor_copy(ckvT[:, :, kt * P:(kt + 1) * P], s[:, 384:640].rearrange("p (k n) -> p k n", k=2))
                    dve.tensor_copy(krT[:, kt * P:(kt + 1) * P], s[0:RD, 640:768]).then_inc(free["PT"], 1)

                for t in range(NT):
                    r = rawo[t % 2]
                    dve.wait_ge(krs_done, t + 1)
                    wait(dve, cq_ready, t)
                    dve.tensor_scalar(r[:, 0:QR], r[:, 0:QR], rsk[:, 0, t:t + 1], None, ALU.mult)
                    if t < TS:
                        x = r[:, 640:672].rearrange("p (h n) -> p h n", h=1)
                        d4 = x.rearrange("p h (r x q) -> p h r x q", r=2, x=2)
                        t4 = rtk.rearrange("p (h n) -> p h n", h=1).rearrange("p h (r x q) -> p h r x q", r=2, x=2)
                        sn = C[:, C_S32 + 32 * t:C_S32 + 32 * (t + 1)].rearrange("p (h r x q) -> p h r x q", h=1, r=2, x=2)
                        for xx in range(2):
                            ins = dve.tensor_tensor(t4[:, :, :, xx, :], d4[:, :, :, 1 - xx, :], sn[:, :, :, xx, :], ALU.mult)
                        dlink(ins)
                        dlink(dve.tensor_tensor(r[:, 640:672], r[:, 640:672], C[:, C_C32 + 32 * t:C_C32 + 32 * (t + 1)], ALU.mult))
                        dve.tensor_tensor(r[:, 640:672], r[:, 640:672], rtk, ALU.add)
                    dve.scalar_tensor_tensor(r[:, QR:640], r[:, QR:640], rsk[:, 1, t:t + 1], kvn, ALU.mult, ALU.mult).then_inc(cq_ready, 1)
                    if t > 0:
                        c_turned(t - 1)
                c_turned(NT - 1)

                def q_rope(t):
                    q = qraw[t % 2].rearrange("p (h n) -> p h n", n=MQ)[:, :, HD:MQ]
                    rope(q, qtmp.rearrange("p (h n) -> p h n", n=RD), C[:, C_C32 + 32 * t:C_C32 + 32 * (t + 1)],
                         C[:, C_S32 + 32 * t:C_S32 + 32 * (t + 1)], MH, 8, qr_ready)

                for t in range(TS):
                    emptied(dve, ("qup", t, 2))
                    wait(dve, qr_ready, t)
                    q_rope(t)

            def kv_read(p):
                s = filled(dve, ("v2", p))
                if p >= 2:
                    filled(dve, ("pv", 1, odd.of_unit[PAIR * (p - 1) - 1]))
                dve.tensor_copy(Vh[:, p % 2], s[:, 0:KCOL].rearrange("p (k n) -> p k n", k=KT)).then_inc(free_of(("v2", p)), 1)

            attention(0)
            scale_x(1)
            ht(1)
            router(0)
            experts(0)
            scale_x(2)
            ht(2)
            odd_project()
            kv_read(0)
            attention(1)
            scale_x(3)
            ht(3)
            router(1)
            experts(1)
            dve.wait_ge(fin_in, 16)
            for t in range(NT):
                dve.wait_ge(rstd_done, 4 * NT + t + 1)
                dve.scalar_tensor_tensor(X[:, t, :], X[:, t, :], rstd[:, t:t + 1], fin, ALU.mult, ALU.mult).then_inc(y_ready, 1)

        @block.scalar
        def _(_):
            def squares(n):
                for t in range(NT):
                    if n == 0:
                        act.wait_ge(x_in[t], 16)
                    elif n in (1, 3):
                        act.wait_ge(x1_done, NT * (n // 2) + t + 1)
                    else:
                        act.wait_ge(x_back[t], 16 * (n // 2))
                    wait(act, rstd_done, NT * (n - 1) + t + 1)
                    wait(act, ssq_done, NT * n + t)
                    act.activation(junk[:], X[:, t, :], ACT.Square, accum_out=ss[:, t:t + 1]).then_inc(ssq_done, 1)

            def ht(n):
                L, w = n // 2, n % 2
                act.wait_ge(mod_ready, 2 * (n + 1))
                for k in range(0, KD, 2):
                    s = filled(act, ("nt", n, k))
                    act.activation(HT[:, k, 0:NS], s[:, 0:NS], ACT.Identity, bias=mods[:, L, 3 * w, k, 0:1], scale=modA[:, L, w, k, 0:1])\
                       .then_inc(free_of(("nt", n, k)), 1)
                s = filled(act, ("ntp", n, 0))
                for j in range(4):
                    ins = act.activation(HT[:, j, NS:NTOK], s[:, j * P:(j + 1) * P], ACT.Identity, bias=mods[:, L, 3 * w, j, 1:2],
                                         scale=modA[:, L, w, j, 1:2])
                ins.then_inc(free_of(("ntp", n, 0)), 1)

            act.wait_ge(free["S0"], 1)
            act.activation(csil[:], VC2[:, 0:16], ACT.Silu).then_inc(csil_ready, 1)
            squares(0)
            ht(0)
            act.wait_ge(lam_ready, 1)
            act.activation(lame[:], lam2[:], ACT.Exp).then_inc(lam_exp, 1)

            def raw_read(t):
                r = raw[t % 2]
                kt = t + 2
                for c in range(5):
                    s = filled(act, ("proj", t, c))
                    if c == 0 and t >= 2:
                        filled(act, ("kbT", t - 2))
                    if c < 2:
                        ins = act.copy(r[:, c * 512:(c + 1) * 512], s[:, 0:512])
                    elif c == 2:
                        ins = act.copy(va[:, kt, :], s[:, 0:512])
                    elif c == 3:
                        ins = act.copy(r[:, 1024:1536].rearrange("p (h a d) -> p a h d", a=2, h=4),
                                       s[:, 0:512].rearrange("p (a h d) -> p a h d", a=2, h=4))
                    else:
                        act.copy(r[:, 1536:1664], s[:, 0:P])
                        ins = act.copy(vb[:, kt, :], s[:, P:2 * P])
                    ins.then_inc(free_of(("proj", t, c)), 1)

            def q_turned(t):
                s = filled(act, ("qT", t))
                act.copy(QTe[:, t, 0:4, :], s[:, 0:512].rearrange("p (h n) -> p h n", h=4)).then_inc(free_of(("qT", t)), 1)
                s = filled(act, ("qbT", t))
                act.copy(QTe[:, t, 4:8, :], s[:, 0:512].rearrange("p (h n) -> p h n", h=4)).then_inc(free_of(("qbT", t)), 1)

            for t in range(NT):
                raw_read(t)
                if t > 0:
                    q_turned(t - 1)
            q_turned(NT - 1)

            def gate_rows(L):
                for s_ in range(2):
                    s = filled(act, ("gb", L, s_))
                    act.copy(GB[:, s_ * D:(s_ + 1) * D], s[:, 0:D]).then_inc(free_of(("gb", L, s_)), 1)

            def exps(L, u):
                pl = plans[L]
                kind, t, i, c = pl.units[u]
                nk = len(pl.keys(u)) * P
                b = u % 4
                s = filled(act, ("s", L, u))
                act.wait_ge(nm_done, units_before[L] + u + 1)
                if u >= 4:
                    filled(act, ("pt", L, pl.read_at[u - 4]))
                scale = HD ** -0.5 if L == 0 else MQ ** -0.5
                act.activation(Prow[L][b][:, 0:nk], s[:, 0:nk], ACT.Exp, bias=nm[:, b:b + 1], scale=scale,
                               accum_out=den[:, b:b + 1]).then_inc(free_of(("s", L, u)), 1)
                if kind == "swa":
                    act.wait_ge(snk_done, swa_number(u))
                    act.activation(sne[:, b:b + 1], snk[:, b:b + 1], ACT.Exp).then_inc(sne_done, 1)

            def pt_read(L, k):
                pl = plans[L]
                n = len(pl.keys(pl.parts[k])) * P
                s = filled(act, ("pt", L, k))
                if k >= 2:
                    filled(act, ("pv", L, k - 2))
                act.copy(PTs[L][k % 2][:, 0:n], s[:, 0:n]).then_inc(free["PT"], 1)

            def kv_read(p):
                s = filled(act, ("kT2", p))
                if p == 0:
                    filled(act, ("oq", NT - 1, 3))
                if p >= 2:
                    filled(act, ("s", 1, PAIR * (p - 1) - 1))
                for j in range(2):
                    act.copy(KTh[0:HD, p % 2, j, :], s[j * HD:(j + 1) * HD, 0:KCOL])
                    ins = act.copy(KTh[HD:MQ, p % 2, j, :], krT)
                ins.then_inc(free_of(("kT2", p)), 1)

            def attention(L):
                pl = plans[L]
                exps(L, 0)
                for i in range(pl.steps):
                    if i + 1 < pl.n:
                        exps(L, i + 1)
                    if i < pl.n and pl.of_unit[i] is not None:
                        pt_read(L, pl.of_unit[i])
                    for what, n in pl.extra.get(i, []):
                        if what == "kv":
                            kv_read(n)

            def router(L):
                emptied(act, ("lg", L))
                act.activation(lge, lg, ACT.Exp).then_inc(lge_done, 1)

            def experts(L):
                G = S[1][:, 0:320]
                base = L * NE

                def expert(i, b):
                    e = 2 * i + b
                    act.wait_ge(gate_mm, base + e + 1)
                    wait(act, hid_ready, base + e - 1)
                    act.activation(sg[b], G, ACT.Silu).then_inc(silu_done, 1)

                expert(0, 0)
                expert(0, 1)
                with act.Fori(1, NE // 2, 1) as i:
                    expert(i, 0)
                    expert(i, 1)

            def odd_project():
                for t in range(NT):
                    s = filled(act, ("oproj", t))
                    if t >= 2:
                        filled(act, ("oc", t - 2))
                    act.copy(rawo[t % 2], s[:, 0:ODD_IN])
                    if t > 0:
                        emptied(act, ("oproj", t - 1))
                    act.activation(junk[:, 0:QR], s[:, 0:QR], ACT.Square, accum_out=ssk[:, 0, t:t + 1])
                    act.activation(junk[:, QR:640], s[:, QR:640], ACT.Square, accum_out=ssk[:, 1, t:t + 1]).then_inc(free_of(("oproj", t)), 1)

                def q_read(t):
                    if t >= 2:
                        filled(act, ("oq", t - 2, 3))
                    for c in range(3):
                        s = filled(act, ("qup", t, c))
                        act.copy(qraw[t % 2][:, c * 512:(c + 1) * 512], s[:, 0:512]).then_inc(free_of(("qup", t, c)), 1)

                def q_turned(t):
                    for g in range(4):
                        s = filled(act, ("oq", t, g))
                        ins = act.copy(QTo[:, 4 * g:4 * g + 4, t * P:(t + 1) * P], s[0:MQ, 0:512].rearrange("p (h n) -> p h n", h=4))
                        ins.then_inc(free["PT"], 1)

                for t in range(NT):
                    q_read(t)
                    if t > 0:
                        q_turned(t - 1)
                q_turned(NT - 1)

            gate_rows(0)
            attention(0)
            squares(1)
            ht(1)
            router(0)
            experts(0)
            squares(2)
            ht(2)
            odd_project()
            kv_read(0)
            gate_rows(1)
            attention(1)
            squares(3)
            ht(3)
            router(1)
            experts(1)
            squares(4)

        @block.gpsimd
        def _(_):
            def rms(n):
                for t in range(NT):
                    pool.wait_ge(ssq_done, NT * n + t + 1)
                    plink(pool.tensor_scalar(rstd[:, t:t + 1], ss[:, t:t + 1], 1.0 / D, EPS, ALU.mult, ALU.add))
                    pool.tensor_tensor(rstd[:, t:t + 1], rstd[:, t:t + 1], mhalf[:, 0:1], ALU.pow).then_inc(rstd_done, 1)

            x_of = [a["x_sample"].rearrange("b s d -> (b s) d"), a["x_prompt"].rearrange("b s d -> (b s) d")]

            def x_tile(t):
                return x_of[0][t * P:(t + 1) * P, :] if t < TS else x_of[1]

            def store_xn(n):
                for t in range(NT):
                    pool.wait_ge(xn_done, NT * n + t + 1)
                    pool.dma_start(a["xn"][n // 2][t * P:(t + 1) * P, :], X[:, t, :]).then_inc(xn_out, 16)

            def tiles(L):
                for t in range(NT):
                    if L == 0 and t == 0:
                        filled(pool, ("kbT", NT - 1))
                    wait(pool, x1_done, NT * L + t)
                    if L == 1 and t == 0:
                        filled(pool, ("kT2", 0))
                    src = x_tile(t) if L == 0 else a["xr"][0][t * P:(t + 1) * P, :]
                    pool.dma_start(xin[L], src).then_inc(xin_in, 16)
                    pool.wait_ge(x1_done, NT * L + t + 1)
                    pool.dma_start(a["xr"][L][t * P:(t + 1) * P, :], X[:, t, :]).then_inc(x1_out, 16)

            def sub_norm(t):
                pool.wait_ge(sub_ss, t + 1)
                plink(pool.tensor_scalar(subr[:], sub4[:], 1.0 / P, EPS, ALU.mult, ALU.add))
                pool.tensor_tensor(subr[:], subr[:], mhalf[:, 0:4], ALU.pow).then_inc(sub_rstd, 1)

            def experts(L):
                base, half = L * NE, L * NE // 2

                def gather(i, b, e):
                    wait(pool, xt_mm, base + e - 1)
                    wait(pool, added[b], 16 * (half + i))
                    src = idxi[:, e:e + 1] if isinstance(e, int) else idxi[:, bass.ds(e, 1)]
                    pool.tensor_copy(idxe[b][:], src).then_inc(idxe_ready, 1)
                    pool.wait_ge(idxe_ready, base + e + 1)
                    pool.sem_inc(gather_go, 1)
                    pool.indirect_dma_start(xe[b], None, a["xn"][L], bass.IndirectOffsetOnAxis(ap=idxe[b][:, 0:1], axis=0))\
                        .then_inc(xe_in[b], 16)

                def expert(i, b, last):
                    e = 2 * i + b
                    if not last:
                        gather(i + b, 1 - b, e + 1)
                    pool.wait_ge(y_scaled, base + e + 1)
                    wait(pool, added[1 - b], 16 * (half + i + b))
                    pool.sem_inc(add_go, 1)
                    pool.indirect_dma_start(a["xr"][L], bass.IndirectOffsetOnAxis(ap=idxe[b][:, 0:1], axis=0), ys[b], None,
                                            compute_op=ALU.add).then_inc(added[b], 16)

                pool.wait_ge(xn_out, 16 * NT * (L + 1))
                pool.wait_ge(x1_out, 16 * NT * (L + 1))
                emptied(pool, ("idx", L))
                gather(0, 0, 0)
                expert(0, 0, False)
                expert(0, 1, False)
                with pool.Fori(1, NE // 2 - 1, 1) as i:
                    expert(i, 0, False)
                    expert(i, 1, False)
                expert(NE // 2 - 1, 0, False)
                expert(NE // 2 - 1, 1, True)
                for b in range(2):
                    pool.wait_ge(added[b], 16 * (half + NE // 2))

            def reload(L):
                for t in range(NT):
                    pool.dma_start(X[:, t, :], a["xr"][L][t * P:(t + 1) * P, :]).then_inc(x_back[t], 16)

            plink(pool.memset(mhalf[:], -0.5))
            rms(0)
            emptied(pool, ("proj", TS, 4))
            r = raw[TS % 2]
            pool.dma_start(a["new_diff_k"].rearrange("a b s h d -> (a b s) (h d)"), r[:, 512:1024]).then_inc(prompt_out, 16)
            pool.dma_start(a["new_diff_v"].rearrange("a b s h d -> (a b s) (h d)"), va[:, KT - 1, :]).then_inc(prompt_out, 16)
            pool.dma_start(a["new_swa_k"].rearrange("a b s h d -> (a b s) (h d)"), r[:, 1536:1664]).then_inc(prompt_out, 16)
            pool.dma_start(a["new_swa_v"].rearrange("a b s h d -> (a b s) (h d)"), vb[:, KT - 1, :]).then_inc(prompt_out, 16)
            for t in range(NT):
                if t == 0:
                    filled(pool, ("kbT", NT - 1))
                wait(pool, x1_done, t)
                pool.dma_start(xin[0], x_tile(t)).then_inc(xin_in, 16)
                sub_norm(t)
                pool.wait_ge(x1_done, t + 1)
                pool.dma_start(a["xr"][0][t * P:(t + 1) * P, :], X[:, t, :]).then_inc(x1_out, 16)
            rms(1)
            store_xn(1)
            experts(0)
            reload(0)
            rms(2)
            for t in range(NT):
                emptied(pool, ("oproj", t))
                pool.tensor_scalar(rsk[:, 0, t:t + 1], ssk[:, 0, t:t + 1], 1.0 / QR, EPS, ALU.mult, ALU.add)
                plink(pool.tensor_scalar(rsk[:, 1, t:t + 1], ssk[:, 1, t:t + 1], 1.0 / KVR, EPS, ALU.mult, ALU.add))
                pool.tensor_tensor(rsk[:, :, t:t + 1], rsk[:, :, t:t + 1], mhalf[:, 0:2].rearrange("p (a b) -> p a b", b=1), ALU.pow)\
                    .then_inc(krs_done, 1)
            pool.wait_ge(cq_ready, NT)
            pool.dma_start(a["new_mla_ckv"].rearrange("a b s c -> (a b s) c"), rawo[TS % 2][:, QR:640]).then_inc(prompt_out, 16)
            pool.dma_start(a["new_mla_krope"].rearrange("a b s c -> (a b s) c"), rawo[TS % 2][:, 640:672]).then_inc(prompt_out, 16)
            tiles(1)
            rms(3)
            store_xn(3)
            experts(1)
            reload(1)
            rms(4)
            ys_of = [a["y_sample"].rearrange("b s d -> (b s) d"), a["y_prompt"].rearrange("b s d -> (b s) d")]
            for t in range(NT):
                pool.wait_ge(y_ready, t + 1)
                dst = ys_of[0][t * P:(t + 1) * P, :] if t < TS else ys_of[1]
                pool.dma_start(dst, X[:, t, :]).then_inc(y_out, 16)
            pool.wait_ge(y_out, 16 * NT)
            pool.wait_ge(prompt_out, 16 * 6)

        @block.sync
        def _(_):
            sp.dma_start(C[:], a["consts"]).then_inc(consts_in, 16)
            for L in range(2):
                for row, src, n in ((64 * L, a["b_ada"][L], 48), (64 * L + 48, a["norm_mix"][L], 8), (64 * L + 56, a["norm_ffn"][L], 8)):
                    sp.dma_start(VR[row:row + n, 0, :], src.rearrange("(k n) -> k n", n=P)).then_inc(vec_in, 16)
            for row, src, n in ((0, a["c"][0], 8), (8, a["c_ctx"], 8), (16, a["mla_q_norm"][0], 3), (19, a["mla_kv_norm"][0], 2),
                                (21, a["diff_subln"][0], 1)):
                sp.dma_start(VR[row:row + n, 1, :], src.rearrange("(k n) -> k n", n=P)).then_inc(vec_in, 16)

            def load_ada(u):
                L, c0 = u // 12, (u % 12) * 512
                done = ada_first[u - 1] if 0 < u < 4 else ada_in
                sp.dma_start(ada_buf(u), a["w_ada"][L][:, c0:c0 + 512].rearrange("(k p) n -> p k n", p=P)).then_inc(done, 16)

            for u in range(2):
                load_ada(u)
            x_s, x_p = a["x_sample"].rearrange("b s d -> (b s) d"), a["x_prompt"].rearrange("b s d -> (b s) d")
            for t in range(NT):
                sp.dma_start(X[:, t, :], x_s[t * P:(t + 1) * P, :] if t < TS else x_p).then_inc(x_in[t], 16)
            for u in range(2, 4):
                load_ada(u)
            sp.dma_start(lamv[:], a["diff_lambda"][0].rearrange("a d -> (a d)").partition_broadcast(P)).then_inc(small_in, 16)
            sp.dma_start(sink[:], a["swa_sink"][0].partition_broadcast(P)).then_inc(small_in, 16)
            for L in range(2):
                sp.dma_start(wr[:, L], a["w_router"][L].rearrange("(k p) n -> p k n", p=P)).then_inc(small_in, 16)
            kd = a["cache_diff_k"].rearrange("a b s h d -> (a b s) (h d)").rearrange("(j p) n -> p j n", p=P)
            vd = a["cache_diff_v"].rearrange("a b s h d -> (a b s) (h d)").rearrange("(j p) n -> p j n", p=P)
            kw = a["cache_swa_k"].rearrange("a b s h d -> (a b s) (h d)").rearrange("(j p) n -> p j n", p=P)
            vw = a["cache_swa_v"].rearrange("a b s h d -> (a b s) (h d)").rearrange("(j p) n -> p j n", p=P)
            sp.dma_start(ctx_k, kd).then_inc(ctx_in, 16)
            sp.dma_start(ctx_ks, kw).then_inc(ctx_in, 16)
            w = a["w_in_even"][0].rearrange("(k p) n -> p k n", p=P)
            for c in range(5):
                n = 512 if c < 4 else 256
                sp.dma_start(w_in_e[:, :, c * 512:c * 512 + n], w[:, :, c * 512:c * 512 + n]).then_inc(win_in[c], 16)
            filled(sp, ("ada", 3))
            sp.dma_start(va[:, 0:2, :], vd).then_inc(ctx_in, 16)
            sp.dma_start(vb[:, 0:2, :], vw).then_inc(ctx_in, 16)

            def stage_ada(u):
                filled(sp, ("ada", u - 1))
                load_ada(u)

            def expert_loads(L, e, units="gud"):
                b = e % 2
                for i, (x, name, sems) in enumerate((("g", "w_gate_exp", wg_in), ("u", "w_up_exp", wu_in), ("d", "w_down_exp", wd_in))):
                    if x in units:
                        k = 4 if x == "d" else KD
                        sp.dma_start(ring[:, (3 * b + i) * U:(3 * b + i + 1) * U].rearrange("p (k n) -> p k n", k=k),
                                     a[name][L][e].rearrange("(k p) n -> p k n", p=P)).then_inc(sems[b], 16)

            def expert_stream(L):
                base = L * NE
                with sp.Fori(1, NE // 2, 1) as i:
                    for b in range(2):
                        for x, (name, sems, used) in enumerate((("w_gate_exp", wg_in, gate_mm), ("w_up_exp", wu_in, up_mm),
                                                                ("w_down_exp", wd_in, down_mm))):
                            k = 4 if x == 2 else KD
                            sp.wait_ge(used, base + 2 * i + b - 1)
                            src = a[name][L][bass.ds(2 * i + b, 1)].rearrange("e (k p) n -> p (e k) n", p=P)
                            sp.dma_start(ring[:, (3 * b + x) * U:(3 * b + x + 1) * U].rearrange("p (k n) -> p k n", k=k), src)\
                              .then_inc(sems[b], 16)

            for u in range(4, 4 + ADA_PROJ):
                stage_ada(u)
            filled(sp, ("kbT", NT - 1))
            sp.wait_ge(prompt_out, 16 * 4)
            sp.dma_start(w_out, a["w_out_even"][0].rearrange("(k p) n -> p k n", p=P)).then_inc(wout_in, 16)
            stage_ada(4 + ADA_PROJ)
            expert_loads(0, 0)
            for u in range(5 + ADA_PROJ, 24):
                stage_ada(u)
            sp.wait_ge(x1_done, NT)
            expert_loads(0, 1)
            expert_stream(0)
            sp.wait_ge(down_mm, NE - 1)
            sp.dma_start(w_in_o, a["w_in_odd"][0].rearrange("(k p) n -> p k n", p=P)).then_inc(odd_in, 16)
            sp.dma_start(w_qup, a["w_q_up"][0].rearrange("(k p) n -> p k n", p=P)).then_inc(qup_in, 16)
            sp.wait_ge(down_mm, NE)
            for k in range(2):
                src = a["w_kv_up"][0].rearrange("(k p) (h c n) -> k c p h n", p=P, h=MH, c=2)
                for c in range(2):
                    sp.dma_start(w_kvup[:, k, c * D:(c + 1) * D].rearrange("p (h n) -> p h n", h=MH), src[k, c]).then_inc(kvup_in, 16)
            sp.dma_start(w_out, a["w_out_odd"][0].rearrange("(k p) n -> p k n", p=P)).then_inc(wout_in, 16)
            sp.wait_ge(y_scaled, NE)
            sp.dma_start(ctx_c, a["cache_mla_ckv"].rearrange("a b s c -> (a b s) c").rearrange("(j p) n -> p j n", p=P)).then_inc(ctxo_in, 16)
            sp.dma_start(ctx_r, a["cache_mla_krope"].rearrange("a b s c -> (a b s) c").rearrange("(j p) n -> p j n", p=P)).then_inc(ctxo_in, 16)
            sp.dma_start(kvn, a["mla_kv_norm"][0].partition_broadcast(P)).then_inc(ctxo_in, 16)
            sp.wait_ge(x1_done, 2 * NT)
            expert_loads(1, 0)
            expert_loads(1, 1)
            expert_stream(1)
            sp.wait_ge(y_scaled, 2 * NE)
            sp.dma_start(fin, a["final_norm"].partition_broadcast(P)).then_inc(fin_in, 16)


_INS = ["x_prompt", "x_sample", "cache_diff_k", "cache_diff_v", "cache_swa_k", "cache_swa_v", "cache_mla_ckv",
        "cache_mla_krope", "c", "c_ctx", "w_ada", "b_ada", "norm_mix", "norm_ffn", "w_in_even", "w_out_even",
        "diff_lambda", "diff_subln", "swa_sink", "w_in_odd", "mla_q_norm", "w_q_up", "mla_kv_norm", "w_kv_up",
        "w_out_odd", "w_router", "w_gate_exp", "w_up_exp", "w_down_exp", "final_norm"]
_OUTS = [("y_prompt", (1, 128, 1024)), ("y_sample", (1, 512, 1024)), ("new_diff_k", (1, 1, 128, 4, 128)),
         ("new_diff_v", (1, 1, 128, 4, 128)), ("new_swa_k", (1, 1, 128, 2, 64)), ("new_swa_v", (1, 1, 128, 2, 64)),
         ("new_mla_ckv", (1, 1, 128, 256)), ("new_mla_krope", (1, 1, 128, 32))]


def kernel(**inputs):
    import concourse.bacc as bacc
    from concourse.bass_utils import run_bass_kernel_spmd

    nc = bacc.Bacc("TRN2", target_bir_lowering=False, num_devices=1)
    arrays, aps = {}, {}
    for name in _INS:
        x = np.ascontiguousarray(inputs[name])
        arrays["in_" + name] = x
        aps[name] = nc.dram_tensor("in_" + name, x.shape, mybir.dt.from_np(x.dtype), kind="ExternalInput").ap()
    arrays["in_consts"] = constants()
    aps["consts"] = nc.dram_tensor("in_consts", arrays["in_consts"].shape, F32, kind="ExternalInput").ap()
    for name, shape in _OUTS:
        aps[name] = nc.dram_tensor("out_" + name, shape, F32, kind="ExternalOutput").ap()
    for name in ("xn", "xr"):
        aps[name] = [nc.dram_tensor(f"{name}{L}", (NTOK, D), F32).ap() for L in range(2)]
    build(nc, aps)
    r = run_bass_kernel_spmd(nc, [arrays], core_ids=[0])
    return tuple(r.results[0]["out_" + name] for name, _ in _OUTS)
```

```python
import math
from contextlib import ExitStack

import numpy as np

import concourse.bass as bass
from concourse import mybir

P = 128
D = 1024
KD = D // P
NS, NP_ = 512, 128
TS = NS // P
NT = TS + 1
NTOK = NS + NP_
PAST = 256
NKEY = PAST + NS
KCOL = NKEY + NP_
KT = KCOL // P
HD = 64
EVEN_IN = 2304
QK = 1664
ODD_IN = 672
QR, KVR, RD = 384, 256, 32
MH, MQ = 16, 96
NE, FF = 16, 512
CAP_S, CAP_P = 2 * NS // NE, 2 * NP_ // NE
SLOTS = CAP_S + CAP_P
EPS = 1e-6
LAM_INIT = 0.8 - 0.6 * math.exp(-0.3 * 0)
NEG = -1e30
GRID_W = 64

F32 = mybir.dt.float32
BF16 = mybir.dt.bfloat16
I32 = mybir.dt.int32
U32 = mybir.dt.uint32
ALU = mybir.AluOpType
ACT = mybir.ActivationFunctionType
AX = mybir.AxisListType.X

C_ID, C_LEFT, C_RIGHT = 0, 128, 256
C_C64, C_S64 = 384, 384 + TS * 64
C_C32 = C_S64 + TS * 64
C_S32 = C_C32 + TS * 32
C_SEL = C_S32 + TS * 32
C_SELE = C_SEL + 2
N_CONST = C_SELE + NE


def rope_tables(dim):
    half = dim // 4
    tok = np.arange(NS)
    inv = (10000.0 ** (-(np.arange(half, dtype=np.float32) / np.float32(half)))).astype(np.float32)
    cos, sin = [], []
    for pos in (tok // GRID_W, tok % GRID_W):
        ang = pos.astype(np.float32)[:, None] * inv[None, :]
        c, s = np.cos(ang.astype(np.float64)), np.sin(ang.astype(np.float64))
        cos += [c, c]
        sin += [-s, s]
    return np.concatenate(cos, 1), np.concatenate(sin, 1)


def constants():
    out = np.zeros((P, N_CONST), np.float32)
    i = np.arange(P)
    out[:, C_ID:C_ID + P] = np.eye(P)
    out[:, C_LEFT:C_LEFT + P] = np.where(i[None, :] >= i[:, None], 0.0, NEG)
    out[:, C_RIGHT:C_RIGHT + P] = np.where(i[None, :] <= i[:, None], 0.0, NEG)
    for stream in range(2):
        out[stream::32, C_SEL + stream] = 1.0
    for e in range(NE):
        out[e::32, C_SELE + e] = 1.0
    for dim, c0, s0 in ((64, C_C64, C_S64), (32, C_C32, C_S32)):
        cos, sin = rope_tables(dim)
        for t in range(TS):
            out[:, c0 + t * dim:c0 + (t + 1) * dim] = cos[t * P:(t + 1) * P]
            out[:, s0 + t * dim:s0 + (t + 1) * dim] = sin[t * P:(t + 1) * P]
    return out


def bank_pieces(off, n):
    out = []
    while n:
        m = min(n, 512 - off % 512)
        out.append((off, m))
        off, n = off + m, n - m
    return out


def build(nc, a):
    with ExitStack() as ctx:
        def sb(name, shape, dt=F32):
            return ctx.enter_context(nc.sbuf_tensor(name, shape, dt))

        def ps(name, shape):
            return ctx.enter_context(nc.psum_tensor(name, shape, F32))

        def sem(name):
            return ctx.enter_context(nc.semaphore(name))

        pe, dve, act, pool, sp = nc.tensor, nc.vector, nc.scalar, nc.gpsimd, nc.sync

        U = 4096
        ring = sb("ring", [P, 6 * U])
        stage = sb("stage", [P, U])
        XH = sb("XH", [P, 2 * NT * D])
        Z = sb("Z", [P, 8960])
        GB = sb("GB", [P, 2048])
        C = sb("C", [P, N_CONST])
        junk = sb("junk", [P, D], BF16)
        X = XH[:, 0:NT * D].rearrange("p (t n) -> p t n", t=NT)
        HT = XH[:, NT * D:2 * NT * D].rearrange("p (k n) -> p k n", k=KD)
        ident = C[:, C_ID:C_ID + P]

        VC1 = sb("VC1", [P, P])
        VC2 = sb("VC2", [P, 22])
        VR = sb("VR", [P, 2, P])
        csil = VR[:].rearrange("p a n -> p (a n)").rearrange("p (k m) -> p k m", k=KD)
        tail = XH[:, NT * D + 4608:NT * D + 5120].bitcast(BF16)
        sqs = tail[:, 0:512]
        xn_p = stage[:, 0:D]
        squares_at = [tail, ring[:, 3 * U - 512:3 * U].bitcast(BF16), junk[:], junk[:], junk[:]]
        ada_sum = junk[:].bitcast(F32)
        mods = sb("mods", [P, 2 * 6 * KD * 2])
        mods = mods[:].rearrange("p (l m k s) -> p l m k s", l=2, m=6, s=2)
        modA = sb("modA", [P, 2 * 2 * KD * 2])
        modA = modA[:].rearrange("p (l w k s) -> p l w k s", l=2, w=2, s=2)
        ss = sb("ss", [P, NT])
        rstd = sb("rstd", [P, NT])
        mhalf = sb("mhalf", [P, 8])
        lamv = sb("lamv", [P, 256])
        lam2 = sb("lam2", [P, 2])
        lame = sb("lame", [P, 2])
        coef = sb("coef", [P, 2])
        sink = sb("sink", [P, 8])
        sink8 = sb("sink8", [P, 8])
        wr = csil
        mx = sb("mx", [P, 8])
        nm = sb("nm", [P, 8])
        den = sb("den", [P, 8])
        snk = sb("snk", [P, 8])
        sne = sb("sne", [P, 8])
        rr = sb("rr", [P, 8])
        sub4 = sb("sub4", [P, 4])
        subr = sb("subr", [P, 4])
        gates = sb("gates", [SLOTS, NE])
        idxi = sb("idxi", [SLOTS, NE], I32)
        idx_from = [sb(f"idx_from{b}", [SLOTS, 1], I32) for b in range(2)]
        idx_to = [sb(f"idx_to{b}", [SLOTS, 1], I32) for b in range(2)]
        rs5 = sb("rs5", [P, 3, NT])
        ssk = sb("ssk", [P, 2, NT])
        rsk = sb("rsk", [P, 2, NT])

        kaT = Z[:, 0:4 * KCOL].rearrange("p (h n) -> p h n", h=4)
        kbT = Z[:, 3584:3584 + KCOL]
        va = Z[:, 4480:4480 + KT * 512].rearrange("p (k n) -> p k n", k=KT)
        vb = Z[:, 8064:8064 + KT * P].rearrange("p (k n) -> p k n", k=KT)
        w_in_e = ring[:, 0:KD * EVEN_IN].rearrange("p (k n) -> p k n", k=KD)
        raw = [ring[:, 18432 + i * QK:18432 + (i + 1) * QK] for i in range(2)]
        rtmp = ring[:, 18432 + 2 * QK:18432 + 3 * QK]
        ctx_k = GB[:, 0:1024].rearrange("p (j n) -> p j n", j=2)
        ctx_ks = GB[:, 1024:1280].rearrange("p (j n) -> p j n", j=2)
        w_out = ring[:, 4 * U:6 * U].rearrange("p (k n) -> p k n", k=KD)
        QTe = XH[:, 0:NT * D].rearrange("p (t k n) -> p t k n", t=NT, k=KD)
        QZ = ring[:, 2 * U:2 * U + 2048].rearrange("p (m c h n) -> p m c h n", m=2, c=2, h=4)
        w_in_o = ring[:, 0:KD * ODD_IN].rearrange("p (k n) -> p k n", k=KD)
        w_qup = ring[:, 5376:5376 + 3 * 1536].rearrange("p (k n) -> p k n", k=3)
        w_kvup = ring[:, 3 * U:4 * U].rearrange("p (k n) -> p k n", k=2)
        cqT = Z[:, 0:3 * NTOK].rearrange("p (k n) -> p k n", k=3)
        ckvT = Z[:, 1920:1920 + 2 * KCOL].rearrange("p (k n) -> p k n", k=2)
        krT = Z[0:RD, 3712:3712 + KCOL]
        Vh = Z[:, 4608:4608 + 2 * KCOL].rearrange("p (b k n) -> p b k n", b=2, k=KT)
        rawo = [Z[:, 6400 + i * ODD_IN:6400 + (i + 1) * ODD_IN] for i in range(2)]
        ctx_c = Z[:, 7744:8256].rearrange("p (j n) -> p j n", j=2)
        ctx_r = Z[:, 8256:8320].rearrange("p (j n) -> p j n", j=2)
        kvn = Z[:, 8320:8576]
        rtk = Z[:, 8576:8608]
        qraw = [stage[:, i * 1536:(i + 1) * 1536] for i in range(2)]
        qtmp = stage[:, 3072:3584]
        KTh = stage[0:MQ, 0:4 * KCOL].rearrange("p (b j n) -> p b j n", b=2, j=2)
        QTo = XH[0:MQ, 0:MH * NTOK].rearrange("p (h n) -> p h n", h=MH)
        pbase = [XH[:, NT * D:NT * D + 4608], ring[:, 5376:5376 + 4608]]
        Pb = [[x[:, b * 1536:(b + 1) * 1536].rearrange("p (c n) -> p c n", c=2) for b in range(2)] for x in pbase]
        Prow = [[Pb[L][n // 2][:, n % 2] for n in range(4)] for L in range(2)]
        Prow[0] += [ring[:, 2 * U + 2048 + n * NKEY:2 * U + 2048 + (n + 1) * NKEY] for n in range(2)]
        ROWS = [len(rows) for rows in Prow]
        PTs = [[x[:, 3072 + b * 768:3072 + (b + 1) * 768] for b in range(2)] for x in pbase]
        Oe = [ring[:, 3 * U + b * D:3 * U + (b + 1) * D] for b in range(2)]
        Oo = [ring[:, t * D:(t + 1) * D] for t in range(NT)]
        OT = [ring[:, 3 * U + 2 * D:3 * U + 3 * D], ring[:, 9984:9984 + D]]
        xin = [ring[:, 3 * U + 3 * D:3 * U + 4 * D], ring[:, 9984 + D:9984 + 2 * D]]
        lg = Z[:, 0:80]
        lgT = Z[:, 1408:2048]
        lge = Z[:, 80:160]
        aff = Z[:, 160:240]
        R = 32 + NE
        affT = Z[0:R, 256:256 + NS]
        topv = Z[0:R, 1024:1024 + SLOTS]
        topi = Z[0:R, 1152:1152 + SLOTS].bitcast(U32)
        topf = Z[0:R, 1280:1280 + SLOTS]
        xe = [Z[0:SLOTS, 2048 + b * D:2048 + (b + 1) * D] for b in range(2)]
        xeT = [Z[:, 4096 + b * 640:4096 + (b + 1) * 640].rearrange("p (k n) -> p k n", k=KD) for b in range(2)]
        AXs = Z[:, 5376:6016].rearrange("p (k n) -> p k n", k=KD)
        BXs = Z[:, 6016:6656].rearrange("p (k n) -> p k n", k=KD)
        sg = [Z[:, 6656 + b * 320:6656 + (b + 1) * 320] for b in range(2)]
        hid = [Z[:, 7296 + b * 320:7296 + (b + 1) * 320] for b in range(2)]
        g2b = Z[0:SLOTS, 7936:8960]
        GXs = HT
        gx = XH[:, NT * D:NT * D + 640].rearrange("p (k n) -> p k n", k=KD)
        ys = [GB[0:SLOTS, b * D:(b + 1) * D] for b in range(2)]
        fin = Z[:, 0:D]

        S = [ps("S0", [P, 1024]), ps("S1", [P, 1024])]
        T = ps("T", [P, 1024])
        place = {"S0": S[0][:], "S1": S[1][:], "PT": T[:], "PV": ps("V", [P, 512])[:], "AD": ps("A", [P, 512])[:]}
        full = {r: sem("psum_full_" + r) for r in place}
        free = {r: sem("psum_free_" + r) for r in place}
        uses = {r: 0 for r in place}
        slot = {}

        def claim(tag, r):
            uses[r] += 1
            slot[tag] = (r, uses[r])
            if uses[r] > 1:
                pe.wait_ge(free[r], uses[r] - 1)
            return place[r]

        def filled(eng, tag):
            r, n = slot[tag]
            eng.wait_ge(full[r], n)
            return place[r]

        def emptied(eng, tag):
            r, n = slot[tag]
            eng.wait_ge(free[r], n)

        def full_of(tag):
            return full[slot[tag][0]]

        def free_of(tag):
            return free[slot[tag][0]]

        consts_in, vec_in, small_in = sem("consts_in"), sem("vec_in"), sem("small_in")
        x_in = [sem(f"x_in{t}") for t in range(NT)]
        x_back = [sem(f"x_back{t}") for t in range(NT)]
        ada_first = [sem(f"ada_first{i}") for i in range(3)]
        ada_in = sem("ada_in")
        win_in = [sem(f"win_in{c}") for c in range(5)]
        ctx_in, wout_in = sem("ctx_in"), sem("wout_in")
        odd_in, qup_in, kvup_in, ctxo_in = sem("odd_in"), sem("qup_in"), sem("kvup_in"), sem("ctxo_in")
        csil_ready, mod_ready = sem("csil_ready"), sem("mod_ready")
        ssq_done, rstd_done, xn_done = sem("ssq_done"), sem("rstd_done"), sem("xn_done")
        rope_done, zeroed, q_spread = sem("rope_done"), sem("zeroed"), sem("q_spread")
        prompt_out = sem("prompt_out")
        lam_ready, lam_exp = sem("lam_ready"), sem("lam_exp")
        nm_done, snk_done, sne_done = sem("nm_done"), sem("snk_done"), sem("sne_done")
        comb_done = sem("comb_done")
        sub_ss, sub_rstd, o_ready = sem("sub_ss"), sem("sub_rstd"), sem("o_ready")
        xin_in, x1_done = sem("xin_in"), sem("x1_done")
        x1_out, xn_out = [sem(f"x1_out{t}") for t in range(NT)], sem("xn_out")
        dve_step, act_step, pool_step = sem("dve_step"), sem("act_step"), sem("pool_step")
        router_in, lge_done, aff_ready, top_ready = sem("router_in"), sem("lge_done"), sem("aff_ready"), sem("top_ready")
        ax_ready, g2_ready = sem("ax_ready"), sem("g2_ready")
        wg_in = [sem(f"wg_in{b}") for b in range(2)]
        wu_in = [sem(f"wu_in{b}") for b in range(2)]
        wd_in = [sem(f"wd_in{b}") for b in range(2)]
        from_ready, to_ready = sem("from_ready"), sem("to_ready")
        gather_go, add_go = sem("gather_go"), sem("add_go")
        xe_in = [sem(f"xe_in{b}") for b in range(2)]
        added = [sem(f"added{b}") for b in range(2)]
        xt_mm, xt_read, xt_ready = sem("xt_mm"), sem("xt_read"), sem("xt_ready")
        gate_mm, up_mm, down_mm = sem("gate_mm"), sem("up_mm"), sem("down_mm")
        silu_done, hid_ready, y_scaled = sem("silu_done"), sem("hid_ready"), sem("y_scaled")
        cq_ready, qr_ready = sem("cq_ready"), sem("qr_ready")
        krs_done = sem("krs_done")
        fin_in, y_ready, y_out = sem("fin_in"), sem("y_ready"), sem("y_out")

        steps = {"dve": 0, "act": 0, "pool": 0}

        def dlink(ins):
            steps["dve"] += 1
            ins.then_inc(dve_step, 1)
            dve.wait_ge(dve_step, steps["dve"])

        def plink(ins):
            steps["pool"] += 1
            ins.then_inc(pool_step, 1)
            pool.wait_ge(pool_step, steps["pool"])

        def wait(eng, s, n):
            if not isinstance(n, int) or n > 0:
                eng.wait_ge(s, n)

        def spread(ap, n):
            return ap.rearrange("p (k a) -> p k a", a=1).to_broadcast([ap.shape[0], ap.shape[1], n])

        def over_heads(ap, heads):
            return ap.rearrange("p (a n) -> p a n", a=1).to_broadcast([ap.shape[0], heads, ap.shape[1]])

        LAG = [2, 1]
        class Plan:

            def __init__(self, layer, units, extra, tail):
                self.layer, self.units, self.extra, self.n = layer, units, extra, len(units)
                self.steps = self.n + tail
                self.due = {}
                self.parts = []
                self.of_unit = []
                self.read_at = []
                for u, (kind, t, i, c) in enumerate(units):
                    mine = None
                    self.read_at.append(len(self.parts))
                    if kind != "diff" or c == 1:
                        mine = len(self.parts)
                        self.parts.append(u - 1 if kind == "diff" else u)
                    self.of_unit.append(mine)
                    if mine is not None:
                        self.due[u + LAG[layer]] = mine

            def keys(self, u):
                kind, t = self.units[u][:2]
                if t == TS:
                    return [KT - 1]
                if kind == "swa":
                    return [0, 1] + [2 + s for s in range(max(t - 1, 0), min(t + 2, TS))]
                return list(range(NKEY // P))

        per_tile = [(k, i, c) for k in ("diff", "swa") for i in range(4) for c in range(2)]
        even_units = [(k, t, i, c) for t in range(NT) for k, i, c in per_tile]
        even_extra = {}
        for t in range(NT):
            last = 16 * t + 15
            even_extra.setdefault(last + 2 + LAG[0], []).append(("norm_o", t))
            even_extra.setdefault(last + 4 + LAG[0], []).append(("turn_o", t))
            even_extra.setdefault(last + 6 + LAG[0], []).append(("out", t))
            even_extra.setdefault(last + 7 + LAG[0], []).append(("square", t))
            even_extra.setdefault(last + 9 + LAG[0], []).append(("scale", t))
        ADA_PROJ = 10
        for n in range(20 - ADA_PROJ):
            even_extra.setdefault(6 * n, []).append(("ada", 4 + ADA_PROJ + n))
            even_extra.setdefault(6 * n + 1, []).append(("ada_turn", 4 + ADA_PROJ + n))
        even = Plan(0, even_units, even_extra, 10 + LAG[0])
        odd_units = [("mla", t, p, c) for p in range(MH // 2) for t in range(NT) for c in range(2)]
        PAIR = 2 * NT
        odd_extra = {}
        for p in range(1, MH // 2):
            odd_extra.setdefault(PAIR * (p - 1) + 2, []).append(("kv", p))
        for t in range(NT):
            odd_extra.setdefault(PAIR * (MH // 2) + 1 + LAG[1] + t, []).append(("turn_o", t))
        for t in range(NT):
            odd_extra.setdefault(PAIR * (MH // 2) + 2 + LAG[1] + t, []).extend([("out", t), ("square", t), ("scale", t)])
        odd = Plan(1, odd_units, odd_extra, 7 + LAG[1])
        plans = [even, odd]
        units_before = [0, even.n]

        def diff_number(u):
            return sum(1 for k, _, _, c in even_units[:u + 1] if k == "diff" and c == 1)

        def swa_number(u):
            return sum(1 for k, _, _, _ in even_units[:u + 1] if k == "swa")

        def v_width(kind):
            return P if kind == "diff" else HD

        def values(L, k, kt):
            kind, t, i, c = plans[L].units[plans[L].parts[k]]
            if kind == "diff":
                return va[:, kt, i * P:(i + 1) * P]
            if kind == "swa":
                return vb[:, kt, c * HD:(c + 1) * HD]
            return Vh[:, i % 2, kt, c * HD:(c + 1) * HD]

        def o_tile(L, t):
            return Oe[t % 2] if L == 0 else Oo[t]

        def o_cols(L, k):
            kind, t, i, c = plans[L].units[plans[L].parts[k]]
            if kind == "diff":
                return i * P, P
            if kind == "swa":
                return 512 + (i + 4 * c) * HD, HD
            return (2 * i + c) * HD, HD

        def ada_buf(u):
            x = [stage[:, :], XH[:, NT * D:NT * D + U], Z[:, 0:U], Z[:, U:2 * U]][u] if u < 4 else stage[:, :]
            return x.rearrange("p (k n) -> p k n", k=KD)

        def xn_tile(n, t):
            return xn_p if n in (1, 3) and t == TS else X[:, t, :]

        block = ctx.enter_context(nc.Block())

        @block.tensor
        def _(_):
            def mm(out, lhsT, rhs, start=True, stop=True):
                return pe.matmul(out, lhsT, rhs, start=start, stop=stop)

            def turn(out, in_):
                return pe.transpose(out, in_, ident[0:in_.shape[0], 0:in_.shape[0]])

            def vectors():
                pe.wait_ge(consts_in, 16)
                pe.wait_ge(vec_in, 16 * 11)
                s = claim("vec", "S0")
                turn(s[:, 0:P], VR[:, 0, :])
                turn(s[:, P:P + 22], VR[0:22, 1, :]).then_inc(full["S0"], 1)

            def ada(u):
                s = claim(("ada", u), "AD")
                if u == 0:
                    pe.wait_ge(csil_ready, 1)
                if 0 < u < 4:
                    pe.wait_ge(ada_first[u - 1], 16)
                else:
                    pe.wait_ge(ada_in, 16 * (1 if u == 0 else u - 2))
                w = ada_buf(u)
                for k in range(KD):
                    g = 32 * (k % 4)
                    ins = mm(s[g:g + 32, 0:512], csil[:, k, :], w[:, k, :], k < 4, k >= 4)
                ins.then_inc(full["AD"], 1)

            def ada_turn(u):
                s = claim(("ada_t", u), "AD")
                for j in range(4):
                    ins = mm(s[:, 2 * j:2 * j + 2], ada_sum[:, j * P:(j + 1) * P], C[:, C_SEL:C_SEL + 2])
                ins.then_inc(full["AD"], 1)

            def turn_x(n):
                for k in range(KD):
                    s = claim(("nt", n, k), ("S0", "S1", "PT")[k % 3])
                    for t in range(TS):
                        if k == 0:
                            pe.wait_ge(xn_done, NT * n + t + 1)
                        ins = turn(s[:, t * P:(t + 1) * P], X[:, t, k * P:(k + 1) * P])
                    ins.then_inc(full_of(("nt", n, k)), 1)
                pe.wait_ge(xn_done, NT * n + NT)
                for g in range(2):
                    s = claim(("ntp", n, g), ("S0", "S1")[g])
                    for j in range(4):
                        k = 4 * g + j
                        ins = turn(s[:, j * P:(j + 1) * P], xn_tile(n, TS)[:, k * P:(k + 1) * P])
                    ins.then_inc(full_of(("ntp", n, g)), 1)

            def wait_ht(n):
                emptied(pe, ("ntp", n, 0))
                emptied(pe, ("ntp", n, 1))

            def even_project():
                n = [0]

                def region():
                    n[0] += 1
                    return ("S0", "S1", "PT")[n[0] % 3]

                def project(t):
                    for c in range(5):
                        if c == 1 and t > 0:
                            ada_turn(3 + 2 * t)
                        elif c == 2:
                            ada(4 + 2 * t)
                        elif c == 4:
                            ada_turn(4 + 2 * t)
                        w = 512 if c < 4 else 256
                        tag = ("proj", t, c)
                        s = claim(tag, region())
                        if t == 0:
                            pe.wait_ge(win_in[c], 16)
                        for k in range(KD):
                            ins = mm(s[:, 0:w], HT[:, k, t * P:(t + 1) * P], w_in_e[:, k, c * 512:c * 512 + w], k == 0, k == KD - 1)
                        ins.then_inc(full_of(tag), 1)

                def turn_qk(t):
                    r = raw[t % 2]
                    if t < TS:
                        pe.wait_ge(rope_done, t + 1)
                    else:
                        emptied(pe, ("proj", t, 4))
                    s = claim(("qT", t), region())
                    for h in range(4):
                        ins = turn(s[:, h * P:(h + 1) * P], r[:, h * P:(h + 1) * P])
                    ins.then_inc(full_of(("qT", t)), 1)
                    s = claim(("kT", t), region())
                    for h in range(4):
                        ins = turn(s[:, h * P:(h + 1) * P], r[:, 512 + h * P:512 + (h + 1) * P])
                    ins.then_inc(full_of(("kT", t)), 1)
                    s = claim(("qbT", t), region())
                    for h in range(4):
                        ins = turn(s[:, h * P:(h + 1) * P], r[:, 1024 + h * P:1024 + (h + 1) * P])
                    ins.then_inc(full_of(("qbT", t)), 1)
                    s = claim(("kbT", t), region())
                    turn(s[:, 0:P], r[:, 1536:1664]).then_inc(full_of(("kbT", t)), 1)

                pe.wait_ge(ctx_in, 16 * 4)
                for j in range(2):
                    s = claim(("ckT", j), region())
                    for h in range(4):
                        ins = turn(s[:, h * P:(h + 1) * P], ctx_k[:, j, h * P:(h + 1) * P])
                    ins.then_inc(full_of(("ckT", j)), 1)
                s = claim("cksT", region())
                for j in range(2):
                    ins = turn(s[:, j * P:(j + 1) * P], ctx_ks[:, j, :])
                ins.then_inc(full_of("cksT"), 1)
                wait_ht(0)
                for t in range(NT):
                    project(t)
                    if t > 0:
                        turn_qk(t - 1)
                    ada(5 + 2 * t)
                turn_qk(NT - 1)
                ada_turn(3 + 2 * NT)

            def gate_rows(L):
                emptied(pe, ("ada_t", 12 * L + 5))
                for s_ in range(2):
                    tag = ("gb", L, s_)
                    s = claim(tag, ("S0", "S1")[s_])
                    for k in range(KD):
                        ins = mm(s[:, k * P:(k + 1) * P], mods[:, L, 2, k, s_:s_ + 1].to_broadcast([P, P]), ident)
                    ins.then_inc(full_of(tag), 1)

            def odd_project():
                pe.wait_ge(ctxo_in, 16 * 3)
                s = claim("occ", "PT")
                for j in range(2):
                    for k in range(2):
                        ins = turn(s[:, (2 * k + j) * P:(2 * k + j + 1) * P], ctx_c[:, j, k * P:(k + 1) * P])
                ins.then_inc(full["PT"], 1)
                s = claim("ocr", "S0")
                for j in range(2):
                    ins = turn(s[0:RD, j * P:(j + 1) * P], ctx_r[:, j, :])
                ins.then_inc(full["S0"], 1)
                wait_ht(2)
                pe.wait_ge(odd_in, 16)

                def project(t):
                    s = claim(("oproj", t), ("S0", "S1")[t % 2])
                    for c0, w in ((0, 512), (512, ODD_IN - 512)):
                        for k in range(KD):
                            ins = mm(s[:, c0:c0 + w], HT[:, k, t * P:(t + 1) * P], w_in_o[:, k, c0:c0 + w], k == 0, k == KD - 1)
                    ins.then_inc(full_of(("oproj", t)), 1)

                def turn_c(t):
                    pe.wait_ge(cq_ready, t + 1)
                    s = claim(("oc", t), "PT")
                    for k in range(5):
                        ins = turn(s[:, k * P:(k + 1) * P], rawo[t % 2][:, k * P:(k + 1) * P])
                    ins = turn(s[0:RD, 5 * P:6 * P], rawo[t % 2][:, 640:672])
                    ins.then_inc(full["PT"], 1)

                for t in range(NT):
                    project(t)
                    if t > 0:
                        turn_c(t - 1)
                turn_c(NT - 1)

                def q_up(t):
                    for c in range(3):
                        s = claim(("qup", t, c), ("S0", "S1")[(t + c) % 2])
                        for k in range(3):
                            ins = mm(s[:, 0:512], cqT[:, k, t * P:(t + 1) * P], w_qup[:, k, c * 512:(c + 1) * 512], k == 0, k == 2)
                        ins.then_inc(full_of(("qup", t, c)), 1)

                def turn_q(t):
                    if t < TS:
                        pe.wait_ge(qr_ready, t + 1)
                    else:
                        emptied(pe, ("qup", t, 2))
                    for g in range(4):
                        s = claim(("oq", t, g), "PT")
                        for j in range(4):
                            h = 4 * g + j
                            ins = turn(s[0:MQ, j * P:(j + 1) * P], qraw[t % 2][:, h * MQ:(h + 1) * MQ])
                        ins.then_inc(full["PT"], 1)

                pe.wait_ge(qup_in, 16)
                for t in range(NT):
                    if t == 0:
                        emptied(pe, ("oc", NT - 1))
                    q_up(t)
                    if t > 0:
                        turn_q(t - 1)
                turn_q(NT - 1)

            def kv(p):
                if p == 0:
                    pe.wait_ge(kvup_in, 16 * 4)
                s = claim(("kT2", p), ("S0", "S1")[p % 2])
                for c0, w in ((0, 512), (512, KCOL - 512)):
                    for k in range(2):
                        ins = mm(s[:, c0:c0 + w], w_kvup[:, k, p * P:(p + 1) * P], ckvT[:, k, c0:c0 + w], k == 0, k == 1)
                ins.then_inc(full_of(("kT2", p)), 1)
                s = claim(("v2", p), ("S1", "S0")[p % 2])
                for kt in range(KT):
                    for k in range(2):
                        ins = mm(s[:, kt * P:(kt + 1) * P], ckvT[:, k, kt * P:(kt + 1) * P], w_kvup[:, k, D + p * P:D + (p + 1) * P], k == 0, k == 1)
                ins.then_inc(full_of(("v2", p)), 1)

            def scores(L, u):
                pl = plans[L]
                kind, t, i, c = pl.units[u]
                s = claim(("s", L, u), ("S0", "S1")[u % 2])
                if L == 0 and u % 8 == 0:
                    pe.wait_ge(q_spread, 2 * (u // 8 + 1))
                keys = pl.keys(u)
                runs = []
                for n, kt in enumerate(keys):
                    if runs and runs[-1][1] + runs[-1][2] == kt:
                        runs[-1][2] += 1
                    else:
                        runs.append([n, kt, 1])
                for n, kt, cnt in runs:
                    for o, w in bank_pieces(n * P, cnt * P):
                        k0 = kt * P + o - n * P
                        if kind == "diff":
                            q, ks = QZ[:, 0, c, i, :], kaT[:, i, k0:k0 + w]
                        elif kind == "swa":
                            q, ks = QZ[:, 1, c, i, :], kbT[:, k0:k0 + w]
                        else:
                            q, ks = QTo[:, 2 * i + c, t * P:(t + 1) * P], KTh[:, i % 2, c, k0:k0 + w]
                        masks = []
                        if kind == "swa" and t < TS:
                            for m, kk in enumerate(keys):
                                if kk >= 2 and o <= m * P < o + w and kk - 2 != t:
                                    masks.append((m * P, C[:, C_LEFT:C_LEFT + P] if kk - 2 < t else C[:, C_RIGHT:C_RIGHT + P]))
                        ins = mm(s[:, o:o + w], q, ks, True, not masks)
                        for x, (at, mask) in enumerate(masks):
                            ins = pe.matmul(s[:, at:at + P], ident, mask, start=False, stop=x == len(masks) - 1)
                ins.then_inc(full_of(("s", L, u)), 1)

            def turn_p(L, k):
                pl = plans[L]
                u = pl.parts[k]
                if pl.units[u][0] == "diff":
                    pe.wait_ge(comb_done, diff_number(u + 1))
                else:
                    emptied(pe, ("s", L, u))
                s = claim(("pt", L, k), "PT")
                for n in range(len(pl.keys(u))):
                    ins = turn(s[:, n * P:(n + 1) * P], Prow[L][u % ROWS[L]][:, n * P:(n + 1) * P])
                ins.then_inc(full["PT"], 1)

            def pv(L, k):
                pl = plans[L]
                u = pl.parts[k]
                keys = pl.keys(u)
                s = claim(("pv", L, k), "PV")
                emptied(pe, ("pt", L, k))
                w = v_width(pl.units[u][0])
                for n, kt in enumerate(keys):
                    ins = mm(s[:, 0:w], PTs[L][k % 2][:, n * P:(n + 1) * P], values(L, k, kt), n == 0, n == len(keys) - 1)
                ins.then_inc(full["PV"], 1)

            def turn_o(L, t):
                if L == 0:
                    pe.wait_ge(o_ready, t + 1)
                else:
                    emptied(pe, ("pv", 1, len(odd.parts) - 1))
                s = claim(("oT", L, t), "S0" if t % 2 else "S1")
                for k in range(KD):
                    ins = turn(s[:, k * P:(k + 1) * P], o_tile(L, t)[:, k * P:(k + 1) * P])
                ins.then_inc(full_of(("oT", L, t)), 1)

            def out(L, t):
                if t == 0:
                    pe.wait_ge(wout_in, 16 * (L + 1))
                emptied(pe, ("oT", L, t))
                s = claim(("out", L, t), "S0" if t % 2 else "S1")
                for c in range(2):
                    for k in range(KD):
                        ins = mm(s[:, c * 512:(c + 1) * 512], OT[L][:, k * P:(k + 1) * P], w_out[:, k, c * 512:(c + 1) * 512], k == 0, k == KD - 1)
                ins.then_inc(full_of(("out", L, t)), 1)

            def attention(L):
                pl = plans[L]
                if L == 0:
                    emptied(pe, ("qbT", NT - 1))
                    emptied(pe, ("kbT", NT - 1))
                else:
                    emptied(pe, ("oq", NT - 1, 3))
                    emptied(pe, ("kT2", 0))
                    emptied(pe, ("v2", 0))
                scores(L, 0)
                for i in range(pl.steps):
                    if i + 1 < pl.n:
                        if L == 1 and (i + 1) % PAIR == 0:
                            emptied(pe, ("kT2", (i + 1) // PAIR))
                            emptied(pe, ("v2", (i + 1) // PAIR))
                        scores(L, i + 1)
                    k = pl.due.get(i)
                    if k is not None:
                        turn_p(L, k)
                        if k > 0:
                            pv(L, k - 1)
                    elif i == pl.n + LAG[L]:
                        pv(L, len(pl.parts) - 1)
                    for what, n in pl.extra.get(i, []):
                        if what == "ada":
                            ada(n)
                        elif what == "ada_turn":
                            ada_turn(n)
                        elif what == "kv":
                            kv(n)
                        elif what == "turn_o":
                            turn_o(L, n)
                        elif what == "out":
                            out(L, n)

            def router(L):
                wait_ht(2 * L + 1)
                pe.wait_ge(router_in, 16 * (L + 1))
                s = claim(("lgT", L), "S0")
                for c0, w in ((0, NS), (NS, NP_)):
                    for k in range(KD):
                        g = 32 * (k % 4)
                        ins = mm(s[g:g + 32, c0:c0 + w], wr[:, k, :], HT[:, k, c0:c0 + w], k < 4, k >= 4)
                ins.then_inc(full["S0"], 1)
                emptied(pe, ("lgT", L))
                s = claim(("lg", L), "S0")
                for t in range(NT):
                    ins = mm(s[:, t * NE:(t + 1) * NE], lgT[:, t * P:(t + 1) * P], C[:, C_SELE:C_SELE + NE])
                ins.then_inc(full["S0"], 1)
                pe.wait_ge(aff_ready, L + 1)
                s = claim(("affT", L), "S1")
                for t in range(TS):
                    turn(s[0:NE, t * P:(t + 1) * P], aff[:, t * NE:(t + 1) * NE])
                turn(s[0:R, NS:NTOK], aff[:, (NT - 3) * NE:]).then_inc(full["S1"], 1)
                pe.wait_ge(ax_ready, L + 1)
                s = claim(("g2", L), "S0")
                for k in range(KD):
                    ins = mm(s[0:SLOTS, k * P:(k + 1) * P], gx[:, k, :], ident)
                ins.then_inc(full["S0"], 1)
                pe.wait_ge(top_ready, L + 1)
                s = claim(("idx", L), "PT")
                turn(s[0:SLOTS, 0:R], topv)
                turn(s[0:SLOTS, 64:64 + R], topf).then_inc(full["PT"], 1)
                for r in place:
                    if uses[r]:
                        pe.wait_ge(free[r], uses[r])

            def experts(L):
                G, Up, XT = S[1][:, 0:320], S[1][:, 512:832], S[0][:, 0:1024].rearrange("p (k n) -> p k n", k=KD)
                base, half = L * NE, L * NE // 2

                def turn_xe(i, b, e):
                    pe.wait_ge(xe_in[b], 16 * (half + i + 1))
                    wait(pe, xt_read, base + e)
                    for k in range(KD):
                        ins = turn(XT[:, k, 0:SLOTS], xe[b][:, k * P:(k + 1) * P])
                    ins.then_inc(xt_mm, 1)

                def expert(i, b, last):
                    e = 2 * i + b
                    wg = ring[:, (3 * b) * U:(3 * b + 1) * U].rearrange("p (k n) -> p k n", k=KD)
                    wu = ring[:, (3 * b + 1) * U:(3 * b + 2) * U].rearrange("p (k n) -> p k n", k=KD)
                    wd = ring[:, (3 * b + 2) * U:(3 * b + 3) * U].rearrange("p (k n) -> p k n", k=4)
                    pe.wait_ge(xt_ready, base + e + 1)
                    wait(pe, silu_done, base + e)
                    pe.wait_ge(wg_in[b], 16 * (half + i + 1))
                    for f in range(4):
                        for k in range(KD):
                            ins = mm(G[:, f * SLOTS:(f + 1) * SLOTS], wg[:, k, f * P:(f + 1) * P], xeT[b][:, k, :], k == 0, k == KD - 1)
                    ins.then_inc(gate_mm, 1)
                    wait(pe, hid_ready, base + e)
                    pe.wait_ge(wu_in[b], 16 * (half + i + 1))
                    for f in range(4):
                        for k in range(KD):
                            ins = mm(Up[:, f * SLOTS:(f + 1) * SLOTS], wu[:, k, f * P:(f + 1) * P], xeT[b][:, k, :], k == 0, k == KD - 1)
                    ins.then_inc(up_mm, 1)
                    if not last:
                        turn_xe(i + b, 1 - b, e + 1)
                    pe.wait_ge(hid_ready, base + e + 1)
                    wait(pe, y_scaled, base + e)
                    pe.wait_ge(wd_in[b], 16 * (half + i + 1))
                    for c in range(2):
                        for f in range(4):
                            ins = mm(T[0:SLOTS, c * 512:(c + 1) * 512], hid[b][:, f * SLOTS:(f + 1) * SLOTS], wd[:, f, c * 512:(c + 1) * 512], f == 0, f == 3)
                    ins.then_inc(down_mm, 1)

                turn_xe(0, 0, 0)
                expert(0, 0, False)
                expert(0, 1, False)
                with pe.Fori(1, NE // 2 - 1, 1) as i:
                    expert(i, 0, False)
                    expert(i, 1, False)
                expert(NE // 2 - 1, 0, False)
                expert(NE // 2 - 1, 1, True)
                pe.wait_ge(y_scaled, base + NE)

            vectors()
            for u in range(4):
                ada(u)
                ada_turn(u)
            turn_x(0)
            even_project()
            gate_rows(0)
            attention(0)
            turn_x(1)
            router(0)
            experts(0)
            turn_x(2)
            odd_project()
            kv(0)
            gate_rows(1)
            attention(1)
            turn_x(3)
            router(1)
            experts(1)

        @block.vector
        def _(_):
            def ada_out(u):
                L, m, half = u // 12, (u % 12) // 2, u % 2
                s = filled(dve, ("ada_t", u))
                dst = mods[:, L, m, 4 * half:4 * half + 4, :]
                bias = VC1[:, 64 * L + 8 * m + 4 * half:64 * L + 8 * m + 4 * half + 4]
                dve.tensor_tensor(dst, s[:, 0:8].rearrange("p (k s) -> p k s", s=2), spread(bias, 2), ALU.add).then_inc(free["AD"], 1)
                if m in (1, 4):
                    gain = VC1[:, 64 * L + 48 + 8 * (m == 4) + 4 * half:64 * L + 52 + 8 * (m == 4) + 4 * half]
                    emptied(dve, ("ada_t", u))
                    dve.scalar_tensor_tensor(modA[:, L, int(m == 4), 4 * half:4 * half + 4, :], dst, 1.0, spread(gain, 2),
                                             ALU.add, ALU.mult).then_inc(mod_ready, 1)

            def scale_x(n, t):
                if n in (1, 3) and t < TS:
                    dve.wait_ge(x1_out[t], 16 * (n // 2 + 1))
                dve.wait_ge(rstd_done, NT * n + t + 1)
                dve.tensor_scalar(xn_tile(n, t), X[:, t, :], rstd[:, t:t + 1], None, ALU.mult).then_inc(xn_done, 1)

            def ht(n):
                L, w = n // 2, n % 2
                dve.wait_ge(mod_ready, 2 * (n + 1))
                for k in range(1, KD, 2):
                    s = filled(dve, ("nt", n, k))
                    dve.tensor_scalar(HT[:, k, 0:NS], s[:, 0:NS], modA[:, L, w, k, 0:1], mods[:, L, 3 * w, k, 0:1], ALU.mult, ALU.add)\
                       .then_inc(free_of(("nt", n, k)), 1)
                s = filled(dve, ("ntp", n, 1))
                for j in range(4):
                    k = 4 + j
                    ins = dve.tensor_scalar(HT[:, k, NS:NTOK], s[:, j * P:(j + 1) * P], modA[:, L, w, k, 1:2], mods[:, L, 3 * w, k, 1:2],
                                            ALU.mult, ALU.add)
                ins.then_inc(free_of(("ntp", n, 1)), 1)

            dlink(dve.memset(coef[:, 0:1], 1.0))
            s = filled(dve, "vec")
            dve.memset(csil, 0.0)
            dve.tensor_copy(VC1[:], s[:, 0:P])
            dve.tensor_copy(VC2[:], s[:, P:P + 22]).then_inc(free["S0"], 1)
            dve.wait_ge(free["S0"], 1)
            dlink(dve.tensor_scalar(VC2[:, 21:22], VC2[:, 21:22], 1.0 - LAM_INIT, None, ALU.mult))
            for u in range(4):
                ada_out(u)
            dve.wait_ge(small_in, 16 * 2)
            lq = lamv[:].rearrange("p (a b n) -> p a b n", a=2, b=2)
            lprod = GB[:, 1280:1408]
            dlink(dve.tensor_tensor(lprod.rearrange("p (a n) -> p a n", a=2), lq[:, :, 0, :], lq[:, :, 1, :], ALU.mult))
            dve.tensor_reduce(lam2[:], lprod.rearrange("p (a n) -> p a n", a=2), AX, ALU.add).then_inc(lam_ready, 1)
            dve.tensor_scalar(sink8[:], sink[:], 8.0, None, ALU.mult)
            for t in range(NT):
                scale_x(0, t)
            ht(0)
            dve.wait_ge(lam_exp, 1)
            dlink(dve.tensor_tensor(coef[:, 1:2], lame[:, 1:2], lame[:, 0:1], ALU.subtract))
            dlink(dve.tensor_scalar(coef[:, 1:2], coef[:, 1:2], -LAM_INIT, None, ALU.add))

            def rope(dst, tmp, cos, sin, heads, quarter, done):
                width = 4 * quarter
                d4 = dst.rearrange("p h (r x q) -> p h r x q", r=2, x=2)
                t4 = tmp.rearrange("p h (r x q) -> p h r x q", r=2, x=2)
                s4 = over_heads(sin, heads).rearrange("p h (r x q) -> p h r x q", r=2, x=2)
                for x in range(2):
                    ins = dve.tensor_tensor(t4[:, :, :, x, :], d4[:, :, :, 1 - x, :], s4[:, :, :, x, :], ALU.mult)
                dlink(ins)
                dlink(dve.tensor_tensor(dst, dst, over_heads(cos, heads), ALU.mult))
                dve.tensor_tensor(dst, dst, tmp, ALU.add).then_inc(done, 1)

            for j in range(2):
                s = filled(dve, ("ckT", j))
                dve.tensor_copy(kaT[:, :, j * P:(j + 1) * P], s[:, 0:512].rearrange("p (h n) -> p h n", h=4)).then_inc(free_of(("ckT", j)), 1)
            s = filled(dve, "cksT")
            dve.tensor_copy(kbT[:, 0:PAST], s[:, 0:PAST]).then_inc(free_of("cksT"), 1)

            def k_turned(t):
                kt = t + 2
                s = filled(dve, ("kT", t))
                dve.tensor_copy(kaT[:, :, kt * P:(kt + 1) * P], s[:, 0:512].rearrange("p (h n) -> p h n", h=4)).then_inc(free_of(("kT", t)), 1)
                s = filled(dve, ("kbT", t))
                dve.tensor_copy(kbT[:, kt * P:(kt + 1) * P], s[:, 0:P]).then_inc(free_of(("kbT", t)), 1)

            for t in range(NT):
                if t > 0:
                    ada_out(3 + 2 * t)
                ada_out(4 + 2 * t)
                if t > 0:
                    k_turned(t - 1)
                if t < TS:
                    emptied(dve, ("proj", t, 4))
                    rope(raw[t % 2].rearrange("p (h n) -> p h n", n=HD), rtmp.rearrange("p (h n) -> p h n", n=HD),
                         C[:, C_C64 + 64 * t:C_C64 + 64 * (t + 1)], C[:, C_S64 + 64 * t:C_S64 + 64 * (t + 1)], QK // HD, 16, rope_done)
            k_turned(NT - 1)
            ada_out(3 + 2 * NT)

            def row_max(L, u):
                pl = plans[L]
                kind, t, i, c = pl.units[u]
                nk = len(pl.keys(u)) * P
                b = u % 8
                s = filled(dve, ("s", L, u))[:, 0:nk]
                g = units_before[L] + u
                if u >= 8:
                    emptied(dve, ("s", L, u - 8))
                    if pl.units[u - 8][0] == "swa":
                        dve.wait_ge(sne_done, swa_number(u - 8))
                dlink(dve.tensor_reduce(mx[:, b:b + 1], s, AX, ALU.max))
                scale = -(HD ** -0.5) if L == 0 else -(MQ ** -0.5)
                if kind == "swa":
                    h = i + 4 * c
                    dve.tensor_scalar(nm[:, b:b + 1], mx[:, b:b + 1], sink8[:, h:h + 1], scale, ALU.max, ALU.mult).then_inc(nm_done, 1)
                    dve.wait_ge(nm_done, g + 1)
                    dve.tensor_tensor(snk[:, b:b + 1], sink[:, h:h + 1], nm[:, b:b + 1], ALU.add).then_inc(snk_done, 1)
                else:
                    dve.tensor_scalar(nm[:, b:b + 1], mx[:, b:b + 1], scale, None, ALU.mult).then_inc(nm_done, 1)

            def combine(L, u):
                pl = plans[L]
                kind, t, i, c = pl.units[u]
                nk = len(pl.keys(u)) * P
                b = u % 8
                emptied(dve, ("s", L, u))
                if kind == "swa":
                    dve.wait_ge(sne_done, swa_number(u))
                    dlink(dve.tensor_tensor(den[:, b:b + 1], den[:, b:b + 1], sne[:, b:b + 1], ALU.add))
                dlink(dve.reciprocal(rr[:, b:b + 1], den[:, b:b + 1]))
                if kind == "diff" and c == 1:
                    p0, p1 = Prow[L][(u - 1) % ROWS[L]][:, 0:nk], Prow[L][u % ROWS[L]][:, 0:nk]
                    dlink(dve.tensor_scalar(p1, p1, rr[:, b:b + 1], coef[:, 1:2], ALU.mult, ALU.mult))
                    dve.scalar_tensor_tensor(p0, p0, rr[:, b - 1:b], p1, ALU.mult, ALU.add).then_inc(comb_done, 1)

            def pv_read(L, k):
                pl = plans[L]
                u = pl.parts[k]
                kind, t, i, c = pl.units[u]
                s = filled(dve, ("pv", L, k))
                c0, w = o_cols(L, k)
                o = o_tile(L, t)
                if L == 0 and t >= 2:
                    filled(dve, ("oT", L, t - 2))
                if kind == "diff":
                    dve.tensor_copy(o[:, c0:c0 + w], s[:, 0:w]).then_inc(free["PV"], 1)
                else:
                    dve.tensor_scalar(o[:, c0:c0 + w], s[:, 0:w], rr[:, u % 8:u % 8 + 1], None, ALU.mult).then_inc(free["PV"], 1)

            def norm_o(t):
                o = Oe[t % 2]
                emptied(dve, ("pv", 0, even.of_unit[16 * t + 15]))
                o3 = o[:, 0:512].rearrange("p (h n) -> p h n", h=4)
                for h in range(4):
                    ins = dve.scalar_tensor_tensor(sqs[:, h * P:(h + 1) * P], o3[:, h, :], 1.0, o3[:, h, :], ALU.mult, ALU.mult, accum_out=sub4[:, h:h + 1])
                ins.then_inc(sub_ss, 1)
                dve.wait_ge(sub_rstd, t + 1)
                dve.tensor_tensor(o3, o3, spread(subr[:], P), ALU.mult).then_inc(o_ready, 1)

            def o_turned(L, t):
                if L == 0:
                    s = filled(dve, ("oT", L, t))
                    if t > 0:
                        filled(dve, ("out", L, t - 1))
                    dve.tensor_scalar(OT[L][:, 0:512], s[:, 0:512], VC2[:, 21:22], None, ALU.mult)
                    dve.tensor_copy(OT[L][:, 512:1024], s[:, 512:1024]).then_inc(free_of(("oT", L, t)), 1)
                else:
                    s = filled(dve, ("oT", L, t))
                    if t > 0:
                        filled(dve, ("out", L, t - 1))
                    dve.tensor_copy(OT[L][:, 0:1024], s[:, 0:1024]).then_inc(free_of(("oT", L, t)), 1)

            def residual(L, t):
                if t == 0:
                    emptied(dve, ("gb", L, 0))
                    emptied(dve, ("gb", L, 1))
                s = filled(dve, ("out", L, t))
                g = GB[:, 0:D] if t < TS else GB[:, D:2 * D]
                dve.wait_ge(xin_in, 16 * (NT * L + t + 1))
                dve.tensor_tensor(X[:, t, :], s[:, 0:D], g, ALU.mult).then_inc(free_of(("out", L, t)), 1)
                emptied(dve, ("out", L, t))
                dve.tensor_tensor(X[:, t, :], X[:, t, :], xin[L], ALU.add).then_inc(x1_done, 1)

            def attention(L):
                pl = plans[L]
                row_max(L, 0)
                for i in range(pl.steps):
                    if i + 1 < pl.n:
                        row_max(L, i + 1)
                    if i < pl.n:
                        combine(L, i)
                    if pl.due.get(i):
                        pv_read(L, pl.due[i] - 1)
                    elif i == pl.n + LAG[L]:
                        pv_read(L, len(pl.parts) - 1)
                    for what, n in pl.extra.get(i, []):
                        if what == "ada_turn":
                            ada_out(n)
                        elif what == "norm_o":
                            norm_o(n)
                        elif what == "turn_o":
                            o_turned(L, n)
                        elif what == "out":
                            residual(L, n)
                        elif what == "scale":
                            scale_x(2 * L + 1, n)
                        elif what == "kv":
                            kv_read(n)

            def router(L):
                s = filled(dve, ("lgT", L))
                dve.tensor_copy(lgT, s[:, 0:NTOK]).then_inc(free["S0"], 1)
                s = filled(dve, ("lg", L))
                s3 = s[:, 0:NT * NE].rearrange("p (t e) -> p t e", t=NT)
                dlink(dve.tensor_reduce(rs5[:, 0, :], s3, AX, ALU.max))
                dve.tensor_tensor(lg.rearrange("p (t e) -> p t e", t=NT), s3, spread(rs5[:, 0, :], NE), ALU.subtract).then_inc(free["S0"], 1)
                for dst, src in ((AXs, modA[:, L, 1]), (BXs, mods[:, L, 3]), (gx, mods[:, L, 5])):
                    dve.tensor_copy(dst[:, :, 0:CAP_S], spread(src[:, :, 0], CAP_S))
                    ins = dve.tensor_copy(dst[:, :, CAP_S:SLOTS], spread(src[:, :, 1], CAP_P))
                ins.then_inc(ax_ready, 1)
                dve.wait_ge(lge_done, L + 1)
                dlink(dve.tensor_reduce(rs5[:, 1, :], lge.rearrange("p (t e) -> p t e", t=NT), AX, ALU.add))
                dlink(dve.reciprocal(rs5[:, 2, :], rs5[:, 1, :]))
                dve.tensor_tensor(aff.rearrange("p (t e) -> p t e", t=NT), lge.rearrange("p (t e) -> p t e", t=NT),
                                  spread(rs5[:, 2, :], NE), ALU.mult).then_inc(aff_ready, 1)
                s = filled(dve, ("affT", L))
                dve.memset(topv[:, CAP_S:], 0.0)
                dve.memset(topf[:, CAP_S:], 0.0)
                dlink(dve.memset(affT, -1.0))
                dve.tensor_copy(affT[0:NE, :], s[0:NE, 0:NS])
                dve.tensor_copy(affT[32:R, 0:NP_], s[32:R, NS:NTOK]).then_inc(free["S1"], 1)
                emptied(dve, ("affT", L))
                s = filled(dve, ("g2", L))
                dve.tensor_copy(g2b, s[0:SLOTS, 0:D]).then_inc(free["S0"], 1)
                for r in range(CAP_S // 8):
                    v, ix = topv[:, 8 * r:8 * r + 8], topi[:, 8 * r:8 * r + 8]
                    dlink(dve.max(v, affT))
                    ins = dve.max_index(ix, v, affT)
                    if r < CAP_S // 8 - 1:
                        dlink(dve.match_replace(affT, v, affT, -1.0))
                dlink(ins)
                dve.tensor_copy(topv[32:R, CAP_S:], topv[32:R, 0:CAP_P])
                dve.tensor_copy(topf[32:R, CAP_S:], topi[32:R, 0:CAP_P])
                dlink(dve.tensor_copy(topf[:, 0:CAP_S], topi[:, 0:CAP_S]))
                dve.tensor_scalar(topf[32:R, CAP_S:], topf[32:R, CAP_S:], float(NS), None, ALU.add).then_inc(top_ready, 1)
                s = filled(dve, ("idx", L))
                for to, at in ((gates, 0), (idxi, 64)):
                    dve.tensor_copy(to[0:CAP_S, :], s[0:CAP_S, at:at + NE])
                    ins = dve.tensor_copy(to[CAP_S:, :], s[CAP_S:SLOTS, at + 32:at + R])
                ins.then_inc(free["PT"], 1)

            def experts(L):
                G, Up, XT = S[1][:, 0:320], S[1][:, 512:832], S[0][:, 0:1024].rearrange("p (k n) -> p k n", k=KD)
                base, half = L * NE, L * NE // 2

                def modulate_xe(b, e):
                    dve.wait_ge(xt_mm, base + e + 1)
                    wait(dve, up_mm, base + e - 1)
                    dve.tensor_tensor(xeT[b], XT[:, :, 0:SLOTS], AXs, ALU.mult).then_inc(xt_read, 1)
                    dve.wait_ge(xt_read, base + e + 1)
                    dve.tensor_tensor(xeT[b], xeT[b], BXs, ALU.add).then_inc(xt_ready, 1)

                def expert(i, b, last):
                    e = 2 * i + b
                    dve.wait_ge(silu_done, base + e + 1)
                    dve.wait_ge(up_mm, base + e + 1)
                    wait(dve, down_mm, base + e - 1)
                    dve.tensor_tensor(hid[b], sg[b], Up, ALU.mult).then_inc(hid_ready, 1)
                    if not last:
                        modulate_xe(1 - b, e + 1)
                    dve.wait_ge(down_mm, base + e + 1)
                    wait(dve, added[b], 16 * (half + i))
                    dve.scalar_tensor_tensor(ys[b], T[0:SLOTS, 0:D], gates[:, bass.ds(e, 1)] if not isinstance(e, int) else gates[:, e:e + 1],
                                             g2b, ALU.mult, ALU.mult).then_inc(y_scaled, 1)

                dve.wait_ge(free["S0"], slot[("g2", L)][1])
                modulate_xe(0, 0)
                expert(0, 0, False)
                expert(0, 1, False)
                with dve.Fori(1, NE // 2 - 1, 1) as i:
                    expert(i, 0, False)
                    expert(i, 1, False)
                expert(NE // 2 - 1, 0, False)
                expert(NE // 2 - 1, 1, True)

            def odd_project():
                s = filled(dve, "occ")
                dve.tensor_copy(ckvT[:, :, 0:PAST], s[:, 0:512].rearrange("p (k n) -> p k n", k=2)).then_inc(free["PT"], 1)
                s = filled(dve, "ocr")
                dve.tensor_copy(krT[:, 0:PAST], s[0:RD, 0:PAST]).then_inc(free["S0"], 1)

                def c_turned(t):
                    kt = t + 2
                    s = filled(dve, ("oc", t))
                    for k in range(3):
                        dve.tensor_scalar(cqT[:, k, t * P:(t + 1) * P], s[:, k * P:(k + 1) * P], VC2[:, 16 + k:17 + k], None, ALU.mult)
                    dve.tensor_copy(ckvT[:, :, kt * P:(kt + 1) * P], s[:, 384:640].rearrange("p (k n) -> p k n", k=2))
                    dve.tensor_copy(krT[:, kt * P:(kt + 1) * P], s[0:RD, 640:768]).then_inc(free["PT"], 1)

                for t in range(NT):
                    r = rawo[t % 2]
                    dve.wait_ge(krs_done, t + 1)
                    wait(dve, cq_ready, t)
                    dve.tensor_scalar(r[:, 0:QR], r[:, 0:QR], rsk[:, 0, t:t + 1], None, ALU.mult)
                    if t < TS:
                        x = r[:, 640:672].rearrange("p (h n) -> p h n", h=1)
                        d4 = x.rearrange("p h (r x q) -> p h r x q", r=2, x=2)
                        t4 = rtk.rearrange("p (h n) -> p h n", h=1).rearrange("p h (r x q) -> p h r x q", r=2, x=2)
                        sn = C[:, C_S32 + 32 * t:C_S32 + 32 * (t + 1)].rearrange("p (h r x q) -> p h r x q", h=1, r=2, x=2)
                        for xx in range(2):
                            ins = dve.tensor_tensor(t4[:, :, :, xx, :], d4[:, :, :, 1 - xx, :], sn[:, :, :, xx, :], ALU.mult)
                        dlink(ins)
                        dlink(dve.tensor_tensor(r[:, 640:672], r[:, 640:672], C[:, C_C32 + 32 * t:C_C32 + 32 * (t + 1)], ALU.mult))
                        dve.tensor_tensor(r[:, 640:672], r[:, 640:672], rtk, ALU.add)
                    dve.scalar_tensor_tensor(r[:, QR:640], r[:, QR:640], rsk[:, 1, t:t + 1], kvn, ALU.mult, ALU.mult).then_inc(cq_ready, 1)
                    if t > 0:
                        c_turned(t - 1)
                c_turned(NT - 1)

                def q_rope(t):
                    q = qraw[t % 2].rearrange("p (h n) -> p h n", n=MQ)[:, :, HD:MQ]
                    rope(q, qtmp.rearrange("p (h n) -> p h n", n=RD), C[:, C_C32 + 32 * t:C_C32 + 32 * (t + 1)],
                         C[:, C_S32 + 32 * t:C_S32 + 32 * (t + 1)], MH, 8, qr_ready)

                for t in range(TS):
                    emptied(dve, ("qup", t, 2))
                    wait(dve, qr_ready, t)
                    q_rope(t)

            def kv_read(p):
                s = filled(dve, ("v2", p))
                if p >= 2:
                    filled(dve, ("pv", 1, odd.of_unit[PAIR * (p - 1) - 1]))
                dve.tensor_copy(Vh[:, p % 2], s[:, 0:KCOL].rearrange("p (k n) -> p k n", k=KT)).then_inc(free_of(("v2", p)), 1)

            attention(0)
            ht(1)
            router(0)
            experts(0)
            for t in range(NT):
                scale_x(2, t)
            ht(2)
            odd_project()
            kv_read(0)
            attention(1)
            ht(3)
            router(1)
            experts(1)
            dve.wait_ge(fin_in, 16)
            for t in range(NT):
                dve.wait_ge(rstd_done, 4 * NT + t + 1)
                dve.scalar_tensor_tensor(X[:, t, :], X[:, t, :], rstd[:, t:t + 1], fin, ALU.mult, ALU.mult).then_inc(y_ready, 1)

        @block.scalar
        def _(_):
            def square(n, t):
                if n == 0:
                    act.wait_ge(x_in[t], 16)
                elif n in (1, 3):
                    act.wait_ge(x1_done, NT * (n // 2) + t + 1)
                else:
                    act.wait_ge(x_back[t], 16 * (n // 2))
                wait(act, rstd_done, NT * (n - 1) + t + 1)
                wait(act, ssq_done, NT * n + t)
                act.activation(squares_at[n], X[:, t, :], ACT.Square, accum_out=ss[:, t:t + 1]).then_inc(ssq_done, 1)

            def ht(n):
                L, w = n // 2, n % 2
                act.wait_ge(mod_ready, 2 * (n + 1))
                for k in range(0, KD, 2):
                    s = filled(act, ("nt", n, k))
                    act.activation(HT[:, k, 0:NS], s[:, 0:NS], ACT.Identity, bias=mods[:, L, 3 * w, k, 0:1], scale=modA[:, L, w, k, 0:1])\
                       .then_inc(free_of(("nt", n, k)), 1)
                s = filled(act, ("ntp", n, 0))
                for j in range(4):
                    ins = act.activation(HT[:, j, NS:NTOK], s[:, j * P:(j + 1) * P], ACT.Identity, bias=mods[:, L, 3 * w, j, 1:2],
                                         scale=modA[:, L, w, j, 1:2])
                ins.then_inc(free_of(("ntp", n, 0)), 1)

            def ada_read(u):
                s = filled(act, ("ada", u))
                if u > 0:
                    filled(act, ("ada_t", u - 1))
                act.copy(ada_sum, s[:, 0:512]).then_inc(free["AD"], 1)

            act.wait_ge(free["S0"], 1)
            act.activation(csil[:, :, 0:2].rearrange("p k s -> p s k"), VC2[:, 0:16].rearrange("p (s k) -> p s k", s=2), ACT.Silu)\
               .then_inc(csil_ready, 1)
            ada_read(0)
            ada_read(1)
            for t in range(NT):
                square(0, t)
            ada_read(2)
            ada_read(3)
            ht(0)
            act.wait_ge(lam_ready, 1)
            act.activation(lame[:], lam2[:], ACT.Exp).then_inc(lam_exp, 1)

            def raw_read(t):
                r = raw[t % 2]
                kt = t + 2
                for c in range(5):
                    if c == 2:
                        ada_read(4 + 2 * t)
                    s = filled(act, ("proj", t, c))
                    if c == 0 and t >= 2:
                        filled(act, ("kbT", t - 2))
                    if c < 2:
                        ins = act.copy(r[:, c * 512:(c + 1) * 512], s[:, 0:512])
                    elif c == 2:
                        ins = act.copy(va[:, kt, :], s[:, 0:512])
                    elif c == 3:
                        ins = act.copy(r[:, 1024:1536].rearrange("p (h a d) -> p a h d", a=2, h=4),
                                       s[:, 0:512].rearrange("p (a h d) -> p a h d", a=2, h=4))
                    else:
                        act.copy(r[:, 1536:1664], s[:, 0:P])
                        ins = act.copy(vb[:, kt, :], s[:, P:2 * P])
                    ins.then_inc(free_of(("proj", t, c)), 1)

            def q_turned(t):
                s = filled(act, ("qT", t))
                act.copy(QTe[:, t, 0:4, :], s[:, 0:512].rearrange("p (h n) -> p h n", h=4)).then_inc(free_of(("qT", t)), 1)
                s = filled(act, ("qbT", t))
                act.copy(QTe[:, t, 4:8, :], s[:, 0:512].rearrange("p (h n) -> p h n", h=4)).then_inc(free_of(("qbT", t)), 1)

            for t in range(NT):
                raw_read(t)
                if t > 0:
                    q_turned(t - 1)
                ada_read(5 + 2 * t)
            q_turned(NT - 1)

            def gate_rows(L):
                for s_ in range(2):
                    s = filled(act, ("gb", L, s_))
                    act.copy(GB[:, s_ * D:(s_ + 1) * D], s[:, 0:D]).then_inc(free_of(("gb", L, s_)), 1)

            def exps(L, u):
                pl = plans[L]
                kind, t, i, c = pl.units[u]
                nk = len(pl.keys(u)) * P
                b = u % 8
                s = filled(act, ("s", L, u))
                act.wait_ge(nm_done, units_before[L] + u + 1)
                if u >= ROWS[L]:
                    filled(act, ("pt", L, pl.read_at[u - ROWS[L]]))
                scale = HD ** -0.5 if L == 0 else MQ ** -0.5
                act.activation(Prow[L][u % ROWS[L]][:, 0:nk], s[:, 0:nk], ACT.Exp, bias=nm[:, b:b + 1], scale=scale,
                               accum_out=den[:, b:b + 1]).then_inc(free_of(("s", L, u)), 1)
                if kind == "swa":
                    act.wait_ge(snk_done, swa_number(u))
                    act.activation(sne[:, b:b + 1], snk[:, b:b + 1], ACT.Exp).then_inc(sne_done, 1)

            def pt_read(L, k):
                pl = plans[L]
                n = len(pl.keys(pl.parts[k])) * P
                s = filled(act, ("pt", L, k))
                if k >= 2:
                    filled(act, ("pv", L, k - 2))
                act.copy(PTs[L][k % 2][:, 0:n], s[:, 0:n]).then_inc(free["PT"], 1)

            def kv_read(p):
                s = filled(act, ("kT2", p))
                if p == 0:
                    filled(act, ("oq", NT - 1, 3))
                if p >= 2:
                    filled(act, ("s", 1, PAIR * (p - 1) - 1))
                for j in range(2):
                    act.copy(KTh[0:HD, p % 2, j, :], s[j * HD:(j + 1) * HD, 0:KCOL])
                    ins = act.copy(KTh[HD:MQ, p % 2, j, :], krT)
                ins.then_inc(free_of(("kT2", p)), 1)

            def attention(L):
                pl = plans[L]
                exps(L, 0)
                for i in range(pl.steps):
                    if i + 1 < pl.n:
                        exps(L, i + 1)
                    if i in pl.due:
                        pt_read(L, pl.due[i])
                    for what, n in pl.extra.get(i, []):
                        if what == "kv":
                            kv_read(n)
                        elif what == "ada":
                            ada_read(n)
                        elif what == "square":
                            square(2 * L + 1, n)

            def router(L):
                emptied(act, ("lg", L))
                act.activation(lge, lg, ACT.Exp).then_inc(lge_done, 1)

            def experts(L):
                G = S[1][:, 0:320]
                base = L * NE

                def expert(i, b):
                    e = 2 * i + b
                    act.wait_ge(gate_mm, base + e + 1)
                    wait(act, hid_ready, base + e - 1)
                    act.activation(sg[b], G, ACT.Silu).then_inc(silu_done, 1)

                expert(0, 0)
                expert(0, 1)
                with act.Fori(1, NE // 2, 1) as i:
                    expert(i, 0)
                    expert(i, 1)

            def odd_project():
                for t in range(NT):
                    s = filled(act, ("oproj", t))
                    if t >= 2:
                        filled(act, ("oc", t - 2))
                    act.copy(rawo[t % 2], s[:, 0:ODD_IN])
                    if t > 0:
                        emptied(act, ("oproj", t - 1))
                    act.activation(junk[:, 0:QR], s[:, 0:QR], ACT.Square, accum_out=ssk[:, 0, t:t + 1])
                    act.activation(junk[:, QR:640], s[:, QR:640], ACT.Square, accum_out=ssk[:, 1, t:t + 1]).then_inc(free_of(("oproj", t)), 1)

                def q_read(t):
                    if t >= 2:
                        filled(act, ("oq", t - 2, 3))
                    for c in range(3):
                        s = filled(act, ("qup", t, c))
                        act.copy(qraw[t % 2][:, c * 512:(c + 1) * 512], s[:, 0:512]).then_inc(free_of(("qup", t, c)), 1)

                def q_turned(t):
                    for g in range(4):
                        s = filled(act, ("oq", t, g))
                        ins = act.copy(QTo[:, 4 * g:4 * g + 4, t * P:(t + 1) * P], s[0:MQ, 0:512].rearrange("p (h n) -> p h n", h=4))
                        ins.then_inc(free["PT"], 1)

                for t in range(NT):
                    q_read(t)
                    if t > 0:
                        q_turned(t - 1)
                q_turned(NT - 1)

            gate_rows(0)
            attention(0)
            ht(1)
            router(0)
            experts(0)
            for t in range(NT):
                square(2, t)
            ht(2)
            odd_project()
            kv_read(0)
            gate_rows(1)
            attention(1)
            ht(3)
            router(1)
            experts(1)
            for t in range(NT):
                square(4, t)

        @block.gpsimd
        def _(_):
            def rms(n, t):
                pool.wait_ge(ssq_done, NT * n + t + 1)
                plink(pool.tensor_scalar(rstd[:, t:t + 1], ss[:, t:t + 1], 1.0 / D, EPS, ALU.mult, ALU.add))
                pool.tensor_tensor(rstd[:, t:t + 1], rstd[:, t:t + 1], mhalf[:, 0:1], ALU.pow).then_inc(rstd_done, 1)

            x_of = [a["x_sample"].rearrange("b s d -> (b s) d"), a["x_prompt"].rearrange("b s d -> (b s) d")]

            def x_tile(t):
                return x_of[0][t * P:(t + 1) * P, :] if t < TS else x_of[1]

            def load_xin(L, t):
                wait(pool, x1_done, NT * L + t)
                pool.dma_start(xin[L], x_tile(t) if L == 0 else a["xr"][0][t * P:(t + 1) * P, :]).then_inc(xin_in, 16)

            def store_x1(L, t):
                n = 2 * L + 1
                pool.wait_ge(x1_done, NT * L + t + 1)
                pool.dma_start(a["xr"][L][t * P:(t + 1) * P, :], X[:, t, :]).then_inc(x1_out[t], 16)
                rms(n, t)
                pool.wait_ge(xn_done, NT * n + t + 1)
                pool.dma_start(a["xn"][L][t * P:(t + 1) * P, :], xn_tile(n, t)).then_inc(xn_out, 16)

            def sub_norm(t):
                pool.wait_ge(sub_ss, t + 1)
                plink(pool.tensor_scalar(subr[:], sub4[:], 1.0 / P, EPS, ALU.mult, ALU.add))
                pool.tensor_tensor(subr[:], subr[:], mhalf[:, 0:4], ALU.pow).then_inc(sub_rstd, 1)

            def experts(L):
                base, half = L * NE, L * NE // 2

                def column(e):
                    return idxi[:, e:e + 1] if isinstance(e, int) else idxi[:, bass.ds(e, 1)]

                def gather(i, b, e):
                    wait(pool, xt_mm, base + e - 1)
                    wait(pool, xe_in[b], 16 * (half + i))
                    pool.sem_inc(gather_go, 1)
                    pool.tensor_copy(idx_from[b][:], column(e)).then_inc(from_ready, 1)
                    pool.wait_ge(from_ready, base + e + 1)
                    pool.sem_inc(gather_go, 1)
                    pool.indirect_dma_start(xe[b], None, a["xn"][L], bass.IndirectOffsetOnAxis(ap=idx_from[b][:, 0:1], axis=0))\
                        .then_inc(xe_in[b], 16)

                def expert(i, b, last):
                    e = 2 * i + b
                    if not last:
                        gather(i + b, 1 - b, e + 1)
                    wait(pool, added[b], 16 * (half + i))
                    pool.sem_inc(add_go, 1)
                    pool.tensor_copy(idx_to[b][:], column(e)).then_inc(to_ready, 1)
                    pool.wait_ge(to_ready, base + e + 1)
                    pool.wait_ge(y_scaled, base + e + 1)
                    wait(pool, added[1 - b], 16 * (half + i + b))
                    pool.sem_inc(add_go, 1)
                    pool.indirect_dma_start(a["xr"][L], bass.IndirectOffsetOnAxis(ap=idx_to[b][:, 0:1], axis=0), ys[b], None,
                                            compute_op=ALU.add).then_inc(added[b], 16)

                pool.wait_ge(xn_out, 16 * NT * (L + 1))
                for t in range(NT):
                    pool.wait_ge(x1_out[t], 16 * (L + 1))
                emptied(pool, ("idx", L))
                gather(0, 0, 0)
                expert(0, 0, False)
                expert(0, 1, False)
                with pool.Fori(1, NE // 2 - 1, 1) as i:
                    expert(i, 0, False)
                    expert(i, 1, False)
                expert(NE // 2 - 1, 0, False)
                expert(NE // 2 - 1, 1, True)
                for b in range(2):
                    pool.wait_ge(added[b], 16 * (half + NE // 2))

            plink(pool.memset(mhalf[:], -0.5))
            for t in range(NT):
                rms(0, t)
            emptied(pool, ("proj", TS, 4))
            r = raw[TS % 2]
            pool.dma_start(a["new_diff_k"].rearrange("a b s h d -> (a b s) (h d)"), r[:, 512:1024]).then_inc(prompt_out, 16)
            pool.dma_start(a["new_diff_v"].rearrange("a b s h d -> (a b s) (h d)"), va[:, KT - 1, :]).then_inc(prompt_out, 16)
            pool.dma_start(a["new_swa_k"].rearrange("a b s h d -> (a b s) (h d)"), r[:, 1536:1664]).then_inc(prompt_out, 16)
            pool.dma_start(a["new_swa_v"].rearrange("a b s h d -> (a b s) (h d)"), vb[:, KT - 1, :]).then_inc(prompt_out, 16)

            def spread_queries(t, m):
                emptied(pool, ("qbT", t))
                if t > 0:
                    filled(pool, ("s", 0, 16 * (t - 1) + 8 * m + 7))
                for c in range(2):
                    rows = slice(c * HD, (c + 1) * HD)
                    pool.tensor_copy(QZ[rows, m, c], QTe[rows, t, 4 * m:4 * m + 4, :]).then_inc(q_spread, 1)
                    pool.wait_ge(q_spread, 4 * t + 2 * m + c + 1)

            pool.memset(QZ, 0.0).then_inc(zeroed, 1)
            pool.wait_ge(zeroed, 1)
            spread_queries(0, 0)
            spread_queries(0, 1)
            for t in range(NT):
                if t == 0:
                    filled(pool, ("kbT", NT - 1))
                if t < NT - 1:
                    spread_queries(t + 1, 0)
                    spread_queries(t + 1, 1)
                load_xin(0, t)
                sub_norm(t)
                store_x1(0, t)
            experts(0)
            for t in range(NT):
                rms(2, t)
            for t in range(NT):
                emptied(pool, ("oproj", t))
                pool.tensor_scalar(rsk[:, 0, t:t + 1], ssk[:, 0, t:t + 1], 1.0 / QR, EPS, ALU.mult, ALU.add)
                plink(pool.tensor_scalar(rsk[:, 1, t:t + 1], ssk[:, 1, t:t + 1], 1.0 / KVR, EPS, ALU.mult, ALU.add))
                pool.tensor_tensor(rsk[:, :, t:t + 1], rsk[:, :, t:t + 1], mhalf[:, 0:2].rearrange("p (a b) -> p a b", b=1), ALU.pow)\
                    .then_inc(krs_done, 1)
            pool.wait_ge(cq_ready, NT)
            pool.dma_start(a["new_mla_ckv"].rearrange("a b s c -> (a b s) c"), rawo[TS % 2][:, QR:640]).then_inc(prompt_out, 16)
            pool.dma_start(a["new_mla_krope"].rearrange("a b s c -> (a b s) c"), rawo[TS % 2][:, 640:672]).then_inc(prompt_out, 16)
            for t in range(NT):
                if t == 0:
                    filled(pool, ("kT2", 0))
                load_xin(1, t)
                store_x1(1, t)
            experts(1)
            for t in range(NT):
                rms(4, t)
            ys_of = [a["y_sample"].rearrange("b s d -> (b s) d"), a["y_prompt"].rearrange("b s d -> (b s) d")]
            for t in range(NT):
                pool.wait_ge(y_ready, t + 1)
                dst = ys_of[0][t * P:(t + 1) * P, :] if t < TS else ys_of[1]
                pool.dma_start(dst, X[:, t, :]).then_inc(y_out, 16)
            pool.wait_ge(y_out, 16 * NT)
            pool.wait_ge(prompt_out, 16 * 6)

        @block.sync
        def _(_):
            sp.dma_start(C[:], a["consts"]).then_inc(consts_in, 16)
            for L in range(2):
                for row, src, n in ((64 * L, a["b_ada"][L], 48), (64 * L + 48, a["norm_mix"][L], 8), (64 * L + 56, a["norm_ffn"][L], 8)):
                    sp.dma_start(VR[row:row + n, 0, :], src.rearrange("(k n) -> k n", n=P)).then_inc(vec_in, 16)
            for row, src, n in ((0, a["c"][0], 8), (8, a["c_ctx"], 8), (16, a["mla_q_norm"][0], 3), (19, a["mla_kv_norm"][0], 2),
                                (21, a["diff_subln"][0], 1)):
                sp.dma_start(VR[row:row + n, 1, :], src.rearrange("(k n) -> k n", n=P)).then_inc(vec_in, 16)

            def load_ada(u):
                L, c0 = u // 12, (u % 12) * 512
                done = ada_first[u - 1] if 0 < u < 4 else ada_in
                sp.dma_start(ada_buf(u), a["w_ada"][L][:, c0:c0 + 512].rearrange("(k p) n -> p k n", p=P)).then_inc(done, 16)

            load_ada(0)
            x_s, x_p = a["x_sample"].rearrange("b s d -> (b s) d"), a["x_prompt"].rearrange("b s d -> (b s) d")
            for t in range(NT):
                sp.dma_start(X[:, t, :], x_s[t * P:(t + 1) * P, :] if t < TS else x_p).then_inc(x_in[t], 16)
            for u in range(1, 4):
                load_ada(u)
            sp.dma_start(lamv[:], a["diff_lambda"][0].rearrange("a d -> (a d)").partition_broadcast(P)).then_inc(small_in, 16)
            sp.dma_start(sink[:], a["swa_sink"][0].partition_broadcast(P)).then_inc(small_in, 16)
            kd = a["cache_diff_k"].rearrange("a b s h d -> (a b s) (h d)").rearrange("(j p) n -> p j n", p=P)
            vd = a["cache_diff_v"].rearrange("a b s h d -> (a b s) (h d)").rearrange("(j p) n -> p j n", p=P)
            kw = a["cache_swa_k"].rearrange("a b s h d -> (a b s) (h d)").rearrange("(j p) n -> p j n", p=P)
            vw = a["cache_swa_v"].rearrange("a b s h d -> (a b s) (h d)").rearrange("(j p) n -> p j n", p=P)
            sp.dma_start(ctx_k, kd).then_inc(ctx_in, 16)
            sp.dma_start(ctx_ks, kw).then_inc(ctx_in, 16)
            w = a["w_in_even"][0].rearrange("(k p) n -> p k n", p=P)
            for c in range(5):
                sp.wait_ge(ada_in if c == 0 else ada_first[min(c - 1, 2)], 16)
                n = 512 if c < 4 else 256
                sp.dma_start(w_in_e[:, :, c * 512:c * 512 + n], w[:, :, c * 512:c * 512 + n]).then_inc(win_in[c], 16)
            filled(sp, ("ada", 3))
            sp.dma_start(va[:, 0:2, :], vd).then_inc(ctx_in, 16)
            sp.dma_start(vb[:, 0:2, :], vw).then_inc(ctx_in, 16)

            def stage_ada(u):
                filled(sp, ("ada", u - 1))
                load_ada(u)

            def expert_loads(L, e, units="gud"):
                b = e % 2
                for i, (x, name, sems) in enumerate((("g", "w_gate_exp", wg_in), ("u", "w_up_exp", wu_in), ("d", "w_down_exp", wd_in))):
                    if x in units:
                        k = 4 if x == "d" else KD
                        sp.dma_start(ring[:, (3 * b + i) * U:(3 * b + i + 1) * U].rearrange("p (k n) -> p k n", k=k),
                                     a[name][L][e].rearrange("(k p) n -> p k n", p=P)).then_inc(sems[b], 16)

            def expert_stream(L):
                base = L * NE
                with sp.Fori(1, NE // 2, 1) as i:
                    for b in range(2):
                        for x, (name, sems, used) in enumerate((("w_gate_exp", wg_in, gate_mm), ("w_up_exp", wu_in, up_mm),
                                                                ("w_down_exp", wd_in, down_mm))):
                            k = 4 if x == 2 else KD
                            sp.wait_ge(used, base + 2 * i + b - 1)
                            src = a[name][L][bass.ds(2 * i + b, 1)].rearrange("e (k p) n -> p (e k) n", p=P)
                            sp.dma_start(ring[:, (3 * b + x) * U:(3 * b + x + 1) * U].rearrange("p (k n) -> p k n", k=k), src)\
                              .then_inc(sems[b], 16)

            def load_context():
                sp.dma_start(ctx_c, a["cache_mla_ckv"].rearrange("a b s c -> (a b s) c").rearrange("(j p) n -> p j n", p=P)).then_inc(ctxo_in, 16)
                sp.dma_start(ctx_r, a["cache_mla_krope"].rearrange("a b s c -> (a b s) c").rearrange("(j p) n -> p j n", p=P)).then_inc(ctxo_in, 16)
                sp.dma_start(kvn, a["mla_kv_norm"][0].partition_broadcast(P)).then_inc(ctxo_in, 16)

            def load_router(L):
                sp.dma_start(wr[:, :, 0:NE], a["w_router"][L].rearrange("(k p) n -> p k n", p=P)).then_inc(router_in, 16)

            def reload(L):
                for b in range(2):
                    sp.wait_ge(added[b], 16 * (NE // 2) * (L + 1))
                for t in range(NT):
                    sp.dma_start(X[:, t, :], a["xr"][L][t * P:(t + 1) * P, :]).then_inc(x_back[t], 16)

            for u in range(4, 4 + ADA_PROJ):
                stage_ada(u)
            filled(sp, ("kbT", NT - 1))
            stage_ada(4 + ADA_PROJ)
            stage_ada(5 + ADA_PROJ)
            sp.wait_ge(prompt_out, 16 * 4)
            sp.dma_start(w_out, a["w_out_even"][0].rearrange("(k p) n -> p k n", p=P)).then_inc(wout_in, 16)
            stage_ada(6 + ADA_PROJ)
            expert_loads(0, 0, "gu")
            for u in range(7 + ADA_PROJ, 24):
                stage_ada(u)
            filled(sp, ("ada", 23))
            load_router(0)
            sp.wait_ge(x1_done, NT)
            sp.wait_ge(ssq_done, 2 * NT)
            expert_loads(0, 0, "d")
            expert_loads(0, 1)
            expert_stream(0)
            sp.wait_ge(down_mm, NE - 1)
            sp.dma_start(w_in_o, a["w_in_odd"][0].rearrange("(k p) n -> p k n", p=P)).then_inc(odd_in, 16)
            sp.dma_start(w_qup, a["w_q_up"][0].rearrange("(k p) n -> p k n", p=P)).then_inc(qup_in, 16)
            reload(0)
            load_context()
            load_router(1)
            for k in range(2):
                src = a["w_kv_up"][0].rearrange("(k p) (h c n) -> k c p h n", p=P, h=MH, c=2)
                for c in range(2):
                    sp.dma_start(w_kvup[:, k, c * D:(c + 1) * D].rearrange("p (h n) -> p h n", h=MH), src[k, c]).then_inc(kvup_in, 16)
            sp.dma_start(w_out, a["w_out_odd"][0].rearrange("(k p) n -> p k n", p=P)).then_inc(wout_in, 16)
            sp.wait_ge(x1_done, 2 * NT)
            expert_loads(1, 0)
            expert_loads(1, 1)
            expert_stream(1)
            sp.wait_ge(y_scaled, 2 * NE)
            sp.dma_start(fin, a["final_norm"].partition_broadcast(P)).then_inc(fin_in, 16)
            reload(1)


_INS = ["x_prompt", "x_sample", "cache_diff_k", "cache_diff_v", "cache_swa_k", "cache_swa_v", "cache_mla_ckv",
        "cache_mla_krope", "c", "c_ctx", "w_ada", "b_ada", "norm_mix", "norm_ffn", "w_in_even", "w_out_even",
        "diff_lambda", "diff_subln", "swa_sink", "w_in_odd", "mla_q_norm", "w_q_up", "mla_kv_norm", "w_kv_up",
        "w_out_odd", "w_router", "w_gate_exp", "w_up_exp", "w_down_exp", "final_norm"]
_OUTS = [("y_prompt", (1, 128, 1024)), ("y_sample", (1, 512, 1024)), ("new_diff_k", (1, 1, 128, 4, 128)),
         ("new_diff_v", (1, 1, 128, 4, 128)), ("new_swa_k", (1, 1, 128, 2, 64)), ("new_swa_v", (1, 1, 128, 2, 64)),
         ("new_mla_ckv", (1, 1, 128, 256)), ("new_mla_krope", (1, 1, 128, 32))]


def kernel(**inputs):
    import concourse.bacc as bacc
    from concourse.bass_utils import run_bass_kernel_spmd

    nc = bacc.Bacc("TRN2", target_bir_lowering=False, num_devices=1)
    arrays, aps = {}, {}
    for name in _INS:
        x = np.ascontiguousarray(inputs[name])
        arrays["in_" + name] = x
        aps[name] = nc.dram_tensor("in_" + name, x.shape, mybir.dt.from_np(x.dtype), kind="ExternalInput").ap()
    arrays["in_consts"] = constants()
    aps["consts"] = nc.dram_tensor("in_consts", arrays["in_consts"].shape, F32, kind="ExternalInput").ap()
    for name, shape in _OUTS:
        aps[name] = nc.dram_tensor("out_" + name, shape, F32, kind="ExternalOutput").ap()
    for name in ("xn", "xr"):
        aps[name] = [nc.dram_tensor(f"{name}{L}", (NTOK, D), F32).ap() for L in range(2)]
    build(nc, aps)
    r = run_bass_kernel_spmd(nc, [arrays], core_ids=[0])
    return tuple(r.results[0]["out_" + name] for name, _ in _OUTS)
```

```python
import math
from contextlib import ExitStack

import numpy as np

import concourse.bass as bass
from concourse import mybir

P = 128
D = 1024
KD = D // P
NS, NP_ = 512, 128
TS = NS // P
NT = TS + 1
NTOK = NS + NP_
PAST = 256
NKEY = PAST + NS
KCOL = NKEY + NP_
KT = KCOL // P
HD = 64
EVEN_IN = 2304
QK = 1664
ODD_IN = 672
QR, KVR, RD = 384, 256, 32
MH, MQ = 16, 96
NE, FF = 16, 512
CAP_S, CAP_P = 2 * NS // NE, 2 * NP_ // NE
SLOTS = CAP_S + CAP_P
EPS = 1e-6
LAM_INIT = 0.8 - 0.6 * math.exp(-0.3 * 0)
NEG = -1e30
GRID_W = 64

F32 = mybir.dt.float32
BF16 = mybir.dt.bfloat16
I32 = mybir.dt.int32
U32 = mybir.dt.uint32
ALU = mybir.AluOpType
ACT = mybir.ActivationFunctionType
AX = mybir.AxisListType.X

C_ID, C_LEFT, C_RIGHT = 0, 128, 256
C_C64, C_S64 = 384, 384 + TS * 64
C_C32 = C_S64 + TS * 64
C_S32 = C_C32 + TS * 32
C_SEL = C_S32 + TS * 32
C_SELE = C_SEL + 2
N_CONST = C_SELE + NE


def rope_tables(dim):
    half = dim // 4
    tok = np.arange(NS)
    inv = (10000.0 ** (-(np.arange(half, dtype=np.float32) / np.float32(half)))).astype(np.float32)
    cos, sin = [], []
    for pos in (tok // GRID_W, tok % GRID_W):
        ang = pos.astype(np.float32)[:, None] * inv[None, :]
        c, s = np.cos(ang.astype(np.float64)), np.sin(ang.astype(np.float64))
        cos += [c, c]
        sin += [-s, s]
    return np.concatenate(cos, 1), np.concatenate(sin, 1)


def constants():
    out = np.zeros((P, N_CONST), np.float32)
    i = np.arange(P)
    out[:, C_ID:C_ID + P] = np.eye(P)
    out[:, C_LEFT:C_LEFT + P] = np.where(i[None, :] >= i[:, None], 0.0, NEG)
    out[:, C_RIGHT:C_RIGHT + P] = np.where(i[None, :] <= i[:, None], 0.0, NEG)
    for stream in range(2):
        out[stream::32, C_SEL + stream] = 1.0
    for e in range(NE):
        out[e::32, C_SELE + e] = 1.0
    for dim, c0, s0 in ((64, C_C64, C_S64), (32, C_C32, C_S32)):
        cos, sin = rope_tables(dim)
        for t in range(TS):
            out[:, c0 + t * dim:c0 + (t + 1) * dim] = cos[t * P:(t + 1) * P]
            out[:, s0 + t * dim:s0 + (t + 1) * dim] = sin[t * P:(t + 1) * P]
    return out


def bank_pieces(off, n):
    out = []
    while n:
        m = min(n, 512 - off % 512)
        out.append((off, m))
        off, n = off + m, n - m
    return out


def build(nc, a):
    with ExitStack() as ctx:
        def sb(name, shape, dt=F32):
            return ctx.enter_context(nc.sbuf_tensor(name, shape, dt))

        def ps(name, shape):
            return ctx.enter_context(nc.psum_tensor(name, shape, F32))

        def sem(name):
            return ctx.enter_context(nc.semaphore(name))

        pe, dve, act, pool, sp = nc.tensor, nc.vector, nc.scalar, nc.gpsimd, nc.sync

        U = KD * FF
        ring = sb("ring", [P, 6 * U])
        stage = sb("stage", [P, U])
        XH = sb("XH", [P, 2 * NT * D])
        Z = sb("Z", [P, 8960])
        GB = sb("GB", [P, 2048])
        C = sb("C", [P, N_CONST])
        junk = sb("junk", [P, D], BF16)
        X = XH[:, 0:NT * D].rearrange("p (t n) -> p t n", t=NT)
        HT = XH[:, NT * D:2 * NT * D].rearrange("p (k n) -> p k n", k=KD)
        ident = C[:, C_ID:C_ID + P]

        VC1 = sb("VC1", [P, P])
        VC2 = sb("VC2", [P, 22])
        VR = sb("VR", [P, 2, P])
        csil = VR[:].rearrange("p a n -> p (a n)").rearrange("p (k m) -> p k m", k=KD)
        tail = XH[:, NT * D + 4608:NT * D + 5120].bitcast(BF16)
        sqs = tail[:, 0:512]
        xn_p = stage[:, 0:D]
        bf_id, bf_left, bf_right = [tail[:, 512 + i * P:512 + (i + 1) * P] for i in range(3)]
        squares_at = [tail, ring[:, 3 * U - 512:3 * U].bitcast(BF16), junk[:], junk[:], junk[:]]
        ada_sum = junk[:].bitcast(F32)
        mods = sb("mods", [P, 2 * 6 * KD * 2])
        mods = mods[:].rearrange("p (l m k s) -> p l m k s", l=2, m=6, s=2)
        modA = sb("modA", [P, 2 * 2 * KD * 2])
        modA = modA[:].rearrange("p (l w k s) -> p l w k s", l=2, w=2, s=2)
        ss = sb("ss", [P, NT])
        rstd = sb("rstd", [P, NT])
        mhalf = sb("mhalf", [P, 8])
        lamv = sb("lamv", [P, 256])
        lam2 = sb("lam2", [P, 2])
        lame = sb("lame", [P, 2])
        coef = sb("coef", [P, 2])
        sink = sb("sink", [P, 8])
        sink8 = sb("sink8", [P, 8])
        wr = csil
        mx = sb("mx", [P, 8])
        nm = sb("nm", [P, 8])
        den = sb("den", [P, 8])
        snk = sb("snk", [P, 8])
        sne = sb("sne", [P, 8])
        rr = sb("rr", [P, 8])
        sub4 = sb("sub4", [P, 4])
        subr = sb("subr", [P, 4])
        gates = sb("gates", [SLOTS, NE])
        idxi = sb("idxi", [SLOTS, NE], I32)
        idx_from = [sb(f"idx_from{b}", [SLOTS, 1], I32) for b in range(2)]
        idx_to = [sb(f"idx_to{b}", [SLOTS, 1], I32) for b in range(2)]
        rs5 = sb("rs5", [P, 3, NT])
        ssk = sb("ssk", [P, 2, NT])
        rsk = sb("rsk", [P, 2, NT])

        kaT = Z[:, 0:4 * KCOL].rearrange("p (h n) -> p h n", h=4)
        kbT = Z[:, 3584:3584 + KCOL]
        va = Z[:, 4480:4480 + KT * 512].rearrange("p (k n) -> p k n", k=KT)
        vb = Z[:, 8064:8064 + KT * P].rearrange("p (k n) -> p k n", k=KT)
        w_in_e = ring[:, 0:KD * EVEN_IN].rearrange("p (k n) -> p k n", k=KD)
        raw = [ring[:, 18432 + i * QK:18432 + (i + 1) * QK] for i in range(2)]
        rtmp = ring[:, 18432 + 2 * QK:18432 + 3 * QK]
        ctx_k = GB[:, 0:1024].rearrange("p (j n) -> p j n", j=2)
        ctx_ks = GB[:, 1024:1280].rearrange("p (j n) -> p j n", j=2)
        w_out = ring[:, 4 * U:6 * U].rearrange("p (k n) -> p k n", k=KD)
        QTe = XH[:, 0:NT * D].rearrange("p (t k n) -> p t k n", t=NT, k=KD)
        QZ = ring[:, 2 * U:2 * U + 2048].rearrange("p (m c h n) -> p m c h n", m=2, c=2, h=4)
        w_in_o = ring[:, 0:KD * ODD_IN].rearrange("p (k n) -> p k n", k=KD)
        w_qup = ring[:, 5376:5376 + 3 * 1536].rearrange("p (k n) -> p k n", k=3)
        w_kvup = ring[:, 3 * U:4 * U].rearrange("p (k n) -> p k n", k=2)
        cqT = Z[:, 0:3 * NTOK].rearrange("p (k n) -> p k n", k=3)
        ckvT = Z[:, 1920:1920 + 2 * KCOL].rearrange("p (k n) -> p k n", k=2)
        krT = Z[0:RD, 3712:3712 + KCOL]
        Vh = Z[:, 4608:4608 + 2 * KCOL].rearrange("p (b k n) -> p b k n", b=2, k=KT)
        rawo = [Z[:, 6400 + i * ODD_IN:6400 + (i + 1) * ODD_IN] for i in range(2)]
        ctx_c = Z[:, 7744:8256].rearrange("p (j n) -> p j n", j=2)
        ctx_r = Z[:, 8256:8320].rearrange("p (j n) -> p j n", j=2)
        kvn = Z[:, 8320:8576]
        rtk = Z[:, 8576:8608]
        qraw = [stage[:, i * 1536:(i + 1) * 1536] for i in range(2)]
        qtmp = stage[:, 3072:3584]
        KTh = stage[0:MQ, 0:4 * KCOL].rearrange("p (b j n) -> p b j n", b=2, j=2)
        QTo = XH[0:MQ, 0:MH * NTOK].rearrange("p (h n) -> p h n", h=MH)
        pbase = [XH[:, NT * D:NT * D + 4608], ring[:, 5376:5376 + 4608]]
        Pb = [[x[:, b * 1536:(b + 1) * 1536].rearrange("p (c n) -> p c n", c=2) for b in range(2)] for x in pbase]
        Prow = [[Pb[L][n // 2][:, n % 2] for n in range(4)] for L in range(2)]
        Prow[0] += [ring[:, 2 * U + 2048 + n * NKEY:2 * U + 2048 + (n + 1) * NKEY] for n in range(2)]
        ROWS = [len(rows) for rows in Prow]
        PTs = [[x[:, 3072 + b * 768:3072 + (b + 1) * 768] for b in range(2)] for x in pbase]
        Oe = [ring[:, 3 * U + b * D:3 * U + (b + 1) * D] for b in range(2)]
        OTo = ring[:, 0:KD * NTOK].rearrange("p (k n) -> p k n", k=KD)
        PTs[1] += [ring[:, 9984 + b * NKEY:9984 + (b + 1) * NKEY] for b in range(2)]
        OTe = ring[:, 3 * U + 2 * D:3 * U + 3 * D]
        xin = [ring[:, 3 * U + 3 * D:3 * U + 4 * D], Z[:, 7072:7072 + D]]
        lg = Z[:, 0:80]
        lgT = Z[:, 1408:2048]
        lge = Z[:, 80:160]
        aff = Z[:, 160:240]
        R = 32 + NE
        affT = Z[0:R, 256:256 + NS]
        topv = Z[0:R, 1024:1024 + SLOTS]
        topi = Z[0:R, 1152:1152 + SLOTS].bitcast(U32)
        topf = Z[0:R, 1280:1280 + SLOTS]
        xe = [Z[0:SLOTS, 2048 + b * D:2048 + (b + 1) * D] for b in range(2)]
        xeT = [Z[:, 4096 + b * 640:4096 + (b + 1) * 640].rearrange("p (k n) -> p k n", k=KD) for b in range(2)]
        AXs = Z[:, 5376:6016].rearrange("p (k n) -> p k n", k=KD)
        BXs = Z[:, 6016:6656].rearrange("p (k n) -> p k n", k=KD)
        sg = [Z[:, 6656 + b * 320:6656 + (b + 1) * 320] for b in range(2)]
        hid = [Z[:, 7296 + b * 320:7296 + (b + 1) * 320] for b in range(2)]
        g2b = Z[0:SLOTS, 7936:8960]
        gx = XH[:, NT * D:NT * D + 640].rearrange("p (k n) -> p k n", k=KD)
        ys = [GB[0:SLOTS, b * D:(b + 1) * D] for b in range(2)]
        fin = Z[:, 0:D]

        S = [ps("S0", [P, 1024]), ps("S1", [P, 1024])]
        T = ps("T", [P, 1024])
        place = {"S0": S[0][:], "S1": S[1][:], "PT": T[:], "PV": ps("V", [P, 512])[:], "AD": ps("A", [P, 512])[:]}
        full = {r: sem("psum_full_" + r) for r in place}
        free = {r: sem("psum_free_" + r) for r in place}
        uses = {r: 0 for r in place}
        slot = {}

        def claim(tag, r):
            uses[r] += 1
            slot[tag] = (r, uses[r])
            if uses[r] > 1:
                pe.wait_ge(free[r], uses[r] - 1)
            return place[r]

        def filled(eng, tag):
            r, n = slot[tag]
            eng.wait_ge(full[r], n)
            return place[r]

        def emptied(eng, tag):
            r, n = slot[tag]
            eng.wait_ge(free[r], n)

        def full_of(tag):
            return full[slot[tag][0]]

        def free_of(tag):
            return free[slot[tag][0]]

        consts_in, vec_in, small_in = sem("consts_in"), sem("vec_in"), sem("small_in")
        x_in = [sem(f"x_in{t}") for t in range(NT)]
        x_back = [sem(f"x_back{t}") for t in range(NT)]
        ada_first = [sem(f"ada_first{i}") for i in range(3)]
        ada_in = sem("ada_in")
        win_in = [sem(f"win_in{c}") for c in range(5)]
        ctxk_in, ctxv_in, wout_in = sem("ctxk_in"), sem("ctxv_in"), sem("wout_in")
        odd_in, qup_in, kvup_in, ctxo_in = sem("odd_in"), sem("qup_in"), sem("kvup_in"), sem("ctxo_in")
        csil_ready, mod_ready = sem("csil_ready"), sem("mod_ready")
        ssq_done, rstd_done, xn_done = sem("ssq_done"), sem("rstd_done"), sem("xn_done")
        rope_done, zeroed, q_spread = sem("rope_done"), sem("zeroed"), sem("q_spread")
        prompt_out = sem("prompt_out")
        lam_ready, lam_exp = sem("lam_ready"), sem("lam_exp")
        nm_done, snk_done, sne_done = sem("nm_done"), sem("snk_done"), sem("sne_done")
        masks_ready, comb_done, p_scaled = sem("masks_ready"), sem("comb_done"), sem("p_scaled")
        sub_ss, sub_rstd, o_ready = sem("sub_ss"), sem("sub_rstd"), sem("o_ready")
        xin_in, x1_done = sem("xin_in"), sem("x1_done")
        x1_out, xn_out = [sem(f"x1_out{t}") for t in range(NT)], sem("xn_out")
        dve_step, pool_step = sem("dve_step"), sem("pool_step")
        router_in, lge_done, aff_ready, top_ready = sem("router_in"), sem("lge_done"), sem("aff_ready"), sem("top_ready")
        ax_ready = sem("ax_ready")
        wg_in = [sem(f"wg_in{b}") for b in range(2)]
        wu_in = [sem(f"wu_in{b}") for b in range(2)]
        wd_in = [sem(f"wd_in{b}") for b in range(2)]
        from_ready, to_ready = sem("from_ready"), sem("to_ready")
        gather_go, add_go = sem("gather_go"), sem("add_go")
        xe_in = [sem(f"xe_in{b}") for b in range(2)]
        added = [sem(f"added{b}") for b in range(2)]
        xt_mm, xt_read, xt_ready = sem("xt_mm"), sem("xt_read"), sem("xt_ready")
        gate_mm, up_mm, down_mm = sem("gate_mm"), sem("up_mm"), sem("down_mm")
        silu_done, hid_ready, y_scaled = sem("silu_done"), sem("hid_ready"), sem("y_scaled")
        cq_ready, qr_ready = sem("cq_ready"), sem("qr_ready")
        krs_done = sem("krs_done")
        fin_in, y_ready, y_out = sem("fin_in"), sem("y_ready"), sem("y_out")

        steps = {"dve": 0, "pool": 0}

        def dlink(ins):
            steps["dve"] += 1
            ins.then_inc(dve_step, 1)
            dve.wait_ge(dve_step, steps["dve"])

        def plink(ins):
            steps["pool"] += 1
            ins.then_inc(pool_step, 1)
            pool.wait_ge(pool_step, steps["pool"])

        def wait(eng, s, n):
            if not isinstance(n, int) or n > 0:
                eng.wait_ge(s, n)

        def spread(ap, n):
            return ap.rearrange("p (k a) -> p k a", a=1).to_broadcast([ap.shape[0], ap.shape[1], n])

        def over_heads(ap, heads):
            return ap.rearrange("p (a n) -> p a n", a=1).to_broadcast([ap.shape[0], heads, ap.shape[1]])

        LAG = [2, 2]
        class Plan:

            def __init__(self, layer, units, extra, tail):
                self.layer, self.units, self.extra, self.n = layer, units, extra, len(units)
                self.steps = self.n + tail
                self.due = {}
                self.parts = []
                self.of_unit = []
                self.read_at = []
                for u, (kind, t, i, c) in enumerate(units):
                    mine = None
                    self.read_at.append(len(self.parts))
                    if kind != "diff" or c == 1:
                        mine = len(self.parts)
                        self.parts.append(u - 1 if kind == "diff" else u)
                    self.of_unit.append(mine)
                    if mine is not None:
                        self.due[u + LAG[layer]] = mine

            def keys(self, u):
                kind, t = self.units[u][:2]
                if t == TS:
                    return [KT - 1]
                if kind == "swa":
                    return [0, 1] + [2 + s for s in range(max(t - 1, 0), min(t + 2, TS))]
                return list(range(NKEY // P))

        per_tile = [(k, i, c) for k in ("diff", "swa") for i in range(4) for c in range(2)]
        even_units = [(k, t, i, c) for t in range(NT) for k, i, c in per_tile]
        even_extra = {}
        for t in range(NT):
            last = 16 * t + 15
            even_extra.setdefault(last + 2 + LAG[0], []).append(("norm_o", t))
            even_extra.setdefault(last + 3 + LAG[0], []).append(("scale_o", t))
            even_extra.setdefault(last + 5 + LAG[0], []).append(("turn_o", t))
            even_extra.setdefault(last + 7 + LAG[0], []).append(("out", t))
            even_extra.setdefault(last + 8 + LAG[0], []).extend([("add_x", t), ("square", t)])
            even_extra.setdefault(last + 10 + LAG[0], []).append(("scale", t))
        ADA_PROJ = 2 * NT - 1
        for n in range(20 - ADA_PROJ):
            even_extra.setdefault(7 * n, []).append(("ada", 4 + ADA_PROJ + n))
            even_extra.setdefault(7 * n + 1, []).append(("ada_turn", 4 + ADA_PROJ + n))
        even = Plan(0, even_units, even_extra, 11 + LAG[0])
        odd_units = [("mla", t, p, c) for p in range(MH // 2) for t in range(NT) for c in range(2)]
        PAIR = 2 * NT
        odd_extra = {}
        for p in range(1, MH // 2):
            odd_extra.setdefault(PAIR * (p - 1) + 2, []).append(("kv", p))
        for t in range(NT):
            odd_extra.setdefault(PAIR * (MH // 2) + 1 + LAG[1] + t, []).extend([("out", t), ("add_x", t), ("square", t), ("scale", t)])
        odd = Plan(1, odd_units, odd_extra, 7 + LAG[1])
        plans = [even, odd]
        units_before = [0, even.n]

        def diff_number(u):
            return sum(1 for k, _, _, c in even_units[:u + 1] if k == "diff" and c == 1)

        def swa_number(u):
            return sum(1 for k, _, _, _ in even_units[:u + 1] if k == "swa")

        def v_width(kind):
            return P if kind == "diff" else HD

        def values(k, kt):
            kind, t, i, c = even.units[even.parts[k]]
            if kind == "diff":
                return va[:, kt, i * P:(i + 1) * P]
            return vb[:, kt, c * HD:(c + 1) * HD]

        def o_cols(k):
            kind, t, i, c = even.units[even.parts[k]]
            return (i * P, P) if kind == "diff" else (512 + (i + 4 * c) * HD, HD)

        ADA_START = [0, 2, 1, 3]

        def ada_before(u):
            return ADA_START[ADA_START.index(u) - 1] if u < 4 else u - 1

        def ada_buf(u):
            x = [stage[:, :], Z[:, 0:U], XH[:, NT * D:NT * D + U], Z[:, U:2 * U]][u] if u < 4 else stage[:, :]
            return x.rearrange("p (k n) -> p k n", k=KD)

        def xn_tile(n, t):
            return xn_p if n in (1, 3) and t == TS else X[:, t, :]

        block = ctx.enter_context(nc.Block())

        @block.tensor
        def _(_):
            def mm(out, lhsT, rhs, start=True, stop=True):
                return pe.matmul(out, lhsT, rhs, start=start, stop=stop)

            def turn(out, in_):
                return pe.transpose(out, in_, ident[0:in_.shape[0], 0:in_.shape[0]])

            def vectors():
                pe.wait_ge(consts_in, 16)
                pe.wait_ge(vec_in, 16 * 11)
                s = claim("vec", "S0")
                turn(s[:, 0:P], VR[:, 0, :])
                turn(s[:, P:P + 22], VR[0:22, 1, :]).then_inc(full["S0"], 1)

            def ada(u):
                s = claim(("ada", u), "AD")
                if u == 0:
                    pe.wait_ge(csil_ready, 1)
                if 0 < u < 4:
                    pe.wait_ge(ada_first[u - 1], 16)
                else:
                    pe.wait_ge(ada_in, 16 * (1 if u == 0 else u - 2))
                w = ada_buf(u)
                for k in range(KD):
                    g = 32 * (k % 4)
                    ins = mm(s[g:g + 32, 0:512], csil[:, k, :], w[:, k, :], k < 4, k >= 4)
                ins.then_inc(full["AD"], 1)

            def ada_turn(u):
                s = claim(("ada_t", u), "AD")
                for j in range(4):
                    ins = mm(s[:, 2 * j:2 * j + 2], ada_sum[:, j * P:(j + 1) * P], C[:, C_SEL:C_SEL + 2])
                ins.then_inc(full["AD"], 1)

            def turn_x(n, ks=range(KD)):
                for k in ks:
                    s = claim(("nt", n, k), ("S0", "S1", "PT")[k % 3])
                    for t in range(TS):
                        if k == 0:
                            pe.wait_ge(xn_done, NT * n + t + 1)
                        ins = turn(s[:, t * P:(t + 1) * P], X[:, t, k * P:(k + 1) * P])
                    ins.then_inc(full_of(("nt", n, k)), 1)
                if KD - 1 not in ks:
                    return
                pe.wait_ge(xn_done, NT * n + NT)
                for g in range(2):
                    s = claim(("ntp", n, g), ("S0", "S1")[g])
                    for j in range(4):
                        k = 4 * g + j
                        ins = turn(s[:, j * P:(j + 1) * P], xn_tile(n, TS)[:, k * P:(k + 1) * P])
                    ins.then_inc(full_of(("ntp", n, g)), 1)

            def wait_ht(n):
                emptied(pe, ("ntp", n, 0))
                emptied(pe, ("ntp", n, 1))

            def even_project():
                n = [0]

                def region():
                    n[0] += 1
                    return ("S0", "S1", "PT")[n[0] % 3]

                def project(t):
                    for c in range(5):
                        if c == 1 and t > 0:
                            ada_turn(2 + 2 * t)
                        elif c == 2 and t > 0:
                            ada(3 + 2 * t)
                        elif c == 4 and t > 0:
                            ada_turn(3 + 2 * t)
                        w = 512 if c < 4 else 256
                        tag = ("proj", t, c)
                        s = claim(tag, region())
                        if t == 0:
                            pe.wait_ge(win_in[c], 16)
                        for k in range(KD):
                            ins = mm(s[:, 0:w], HT[:, k, t * P:(t + 1) * P], w_in_e[:, k, c * 512:c * 512 + w], k == 0, k == KD - 1)
                        ins.then_inc(full_of(tag), 1)

                def turn_qk(t):
                    r = raw[t % 2]
                    if t < TS:
                        pe.wait_ge(rope_done, t + 1)
                    else:
                        emptied(pe, ("proj", t, 4))
                    s = claim(("qT", t), region())
                    for h in range(4):
                        ins = turn(s[:, h * P:(h + 1) * P], r[:, h * P:(h + 1) * P])
                    ins.then_inc(full_of(("qT", t)), 1)
                    s = claim(("kT", t), region())
                    for h in range(4):
                        ins = turn(s[:, h * P:(h + 1) * P], r[:, 512 + h * P:512 + (h + 1) * P])
                    ins.then_inc(full_of(("kT", t)), 1)
                    s = claim(("qbT", t), region())
                    for h in range(4):
                        ins = turn(s[:, h * P:(h + 1) * P], r[:, 1024 + h * P:1024 + (h + 1) * P])
                    ins.then_inc(full_of(("qbT", t)), 1)
                    s = claim(("kbT", t), region())
                    turn(s[:, 0:P], r[:, 1536:1664]).then_inc(full_of(("kbT", t)), 1)

                def turn_context():
                    pe.wait_ge(ctxk_in, 16 * 2)
                    for j in range(2):
                        s = claim(("ckT", j), region())
                        for h in range(4):
                            ins = turn(s[:, h * P:(h + 1) * P], ctx_k[:, j, h * P:(h + 1) * P])
                        ins.then_inc(full_of(("ckT", j)), 1)
                    s = claim("cksT", region())
                    for j in range(2):
                        ins = turn(s[:, j * P:(j + 1) * P], ctx_ks[:, j, :])
                    ins.then_inc(full_of("cksT"), 1)

                wait_ht(0)
                for t in range(NT):
                    project(t)
                    if t == 0:
                        turn_context()
                    if t > 0:
                        turn_qk(t - 1)
                    ada(4 + 2 * t)
                turn_qk(NT - 1)
                ada_turn(2 + 2 * NT)

            def gate_rows(L):
                emptied(pe, ("ada_t", 12 * L + 5))
                for s_ in range(2):
                    tag = ("gb", L, s_)
                    s = claim(tag, ("S0", "S1")[s_])
                    for k in range(KD):
                        ins = mm(s[:, k * P:(k + 1) * P], mods[:, L, 2, k, s_:s_ + 1].to_broadcast([P, P]), ident)
                    ins.then_inc(full_of(tag), 1)

            def odd_project():
                pe.wait_ge(ctxo_in, 16 * 3)
                s = claim("occ", "PT")
                for j in range(2):
                    for k in range(2):
                        ins = turn(s[:, (2 * k + j) * P:(2 * k + j + 1) * P], ctx_c[:, j, k * P:(k + 1) * P])
                ins.then_inc(full["PT"], 1)
                s = claim("ocr", "S0")
                for j in range(2):
                    ins = turn(s[0:RD, j * P:(j + 1) * P], ctx_r[:, j, :])
                ins.then_inc(full["S0"], 1)
                wait_ht(2)
                pe.wait_ge(odd_in, 16)

                def project(t):
                    s = claim(("oproj", t), ("S0", "S1")[t % 2])
                    for c0, w in ((0, 512), (512, ODD_IN - 512)):
                        for k in range(KD):
                            ins = mm(s[:, c0:c0 + w], HT[:, k, t * P:(t + 1) * P], w_in_o[:, k, c0:c0 + w], k == 0, k == KD - 1)
                    ins.then_inc(full_of(("oproj", t)), 1)

                def turn_c(t):
                    pe.wait_ge(cq_ready, t + 1)
                    s = claim(("oc", t), "PT")
                    for k in range(5):
                        ins = turn(s[:, k * P:(k + 1) * P], rawo[t % 2][:, k * P:(k + 1) * P])
                    ins = turn(s[0:RD, 5 * P:6 * P], rawo[t % 2][:, 640:672])
                    ins.then_inc(full["PT"], 1)

                for t in range(NT):
                    project(t)
                    if t > 0:
                        turn_c(t - 1)
                turn_c(NT - 1)

                def q_up(t):
                    for c in range(3):
                        s = claim(("qup", t, c), ("S0", "S1")[(t + c) % 2])
                        for k in range(3):
                            ins = mm(s[:, 0:512], cqT[:, k, t * P:(t + 1) * P], w_qup[:, k, c * 512:(c + 1) * 512], k == 0, k == 2)
                        ins.then_inc(full_of(("qup", t, c)), 1)

                def turn_q(t):
                    if t < TS:
                        pe.wait_ge(qr_ready, t + 1)
                    else:
                        emptied(pe, ("qup", t, 2))
                    for g in range(4):
                        s = claim(("oq", t, g), ("PT", "AD", "PV")[(4 * t + g) % 3])
                        for j in range(4):
                            h = 4 * g + j
                            ins = turn(s[0:MQ, j * P:(j + 1) * P], qraw[t % 2][:, h * MQ:(h + 1) * MQ])
                        ins.then_inc(full_of(("oq", t, g)), 1)

                pe.wait_ge(qup_in, 16)
                for t in range(NT):
                    if t == 0:
                        emptied(pe, ("oc", NT - 1))
                    q_up(t)
                    if t > 0:
                        turn_q(t - 1)
                turn_q(NT - 1)

            def kv(p):
                if p == 0:
                    pe.wait_ge(kvup_in, 16 * 4)
                s = claim(("kT2", p), ("S0", "S1")[p % 2])
                for c0, w in ((0, 512), (512, KCOL - 512)):
                    for k in range(2):
                        ins = mm(s[:, c0:c0 + w], w_kvup[:, k, p * P:(p + 1) * P], ckvT[:, k, c0:c0 + w], k == 0, k == 1)
                ins.then_inc(full_of(("kT2", p)), 1)
                s = claim(("v2", p), ("S1", "S0")[p % 2])
                for kt in range(KT):
                    for k in range(2):
                        ins = mm(s[:, kt * P:(kt + 1) * P], ckvT[:, k, kt * P:(kt + 1) * P], w_kvup[:, k, D + p * P:D + (p + 1) * P], k == 0, k == 1)
                ins.then_inc(full_of(("v2", p)), 1)

            def scores(L, u):
                pl = plans[L]
                kind, t, i, c = pl.units[u]
                s = claim(("s", L, u), ("S0", "S1")[u % 2])
                if L == 0 and u % 8 == 0:
                    pe.wait_ge(q_spread, 2 * (u // 8 + 1))
                keys = pl.keys(u)
                runs = []
                for n, kt in enumerate(keys):
                    if runs and runs[-1][1] + runs[-1][2] == kt:
                        runs[-1][2] += 1
                    else:
                        runs.append([n, kt, 1])
                for n, kt, cnt in runs:
                    for o, w in bank_pieces(n * P, cnt * P):
                        k0 = kt * P + o - n * P
                        if kind == "diff":
                            q, ks = QZ[:, 0, c, i, :], kaT[:, i, k0:k0 + w]
                        elif kind == "swa":
                            q, ks = QZ[:, 1, c, i, :], kbT[:, k0:k0 + w]
                        else:
                            q, ks = QTo[:, 2 * i + c, t * P:(t + 1) * P], KTh[:, i % 2, c, k0:k0 + w]
                        masks = []
                        if kind == "swa" and t < TS:
                            for m, kk in enumerate(keys):
                                if kk >= 2 and o <= m * P < o + w and kk - 2 != t:
                                    masks.append((m * P, bf_left if kk - 2 < t else bf_right))
                        ins = mm(s[:, o:o + w], q, ks, True, not masks)
                        for x, (at, mask) in enumerate(masks):
                            ins = pe.matmul(s[:, at:at + P], bf_id, mask, start=False, stop=x == len(masks) - 1)
                ins.then_inc(full_of(("s", L, u)), 1)

            def turn_p(L, k):
                pl = plans[L]
                u = pl.parts[k]
                if L == 1:
                    pe.wait_ge(p_scaled, u + 1)
                elif pl.units[u][0] == "diff":
                    pe.wait_ge(comb_done, diff_number(u + 1))
                else:
                    emptied(pe, ("s", L, u))
                s = claim(("pt", L, k), "PT")
                for n in range(len(pl.keys(u))):
                    ins = turn(s[:, n * P:(n + 1) * P], Prow[L][u % ROWS[L]][:, n * P:(n + 1) * P])
                ins.then_inc(full["PT"], 1)

            def pv(k):
                u = even.parts[k]
                keys = even.keys(u)
                s = claim(("pv", 0, k), "PV")
                emptied(pe, ("pt", 0, k))
                w = v_width(even.units[u][0])
                for n, kt in enumerate(keys):
                    ins = mm(s[:, 0:w], PTs[0][k % 2][:, n * P:(n + 1) * P], values(k, kt), n == 0, n == len(keys) - 1)
                ins.then_inc(full["PV"], 1)

            def pv_pair(q):
                kind, t, i, _ = odd.units[2 * q]
                keys = odd.keys(2 * q)
                s = claim(("pv", 1, q), "PV")
                emptied(pe, ("pt", 1, 2 * q + 1))
                for n, kt in enumerate(keys):
                    for c in range(2):
                        rows = slice(c * HD, (c + 1) * HD)
                        ins = mm(s[rows, 0:P], Vh[:, i % 2, kt, rows], PTs[1][(2 * q + c) % 4][:, n * P:(n + 1) * P], n == 0, n == len(keys) - 1)
                ins.then_inc(full["PV"], 1)

            def turn_o(t):
                pe.wait_ge(o_ready, t + 1)
                s = claim(("oT", t), "PT")
                for k in range(KD):
                    ins = turn(s[:, k * P:(k + 1) * P], Oe[t % 2][:, k * P:(k + 1) * P])
                ins.then_inc(full_of(("oT", t)), 1)

            def out(L, t):
                if t == 0:
                    pe.wait_ge(wout_in, 16 * (L + 1))
                    if L == 1:
                        emptied(pe, ("pv", 1, odd.n // 2 - 1))
                if L == 0:
                    emptied(pe, ("oT", t))
                s = claim(("out", L, t), "PT" if L == 0 else "S0" if t % 2 else "S1")
                for c in range(2):
                    for k in range(KD):
                        o = OTe[:, k * P:(k + 1) * P] if L == 0 else OTo[:, k, t * P:(t + 1) * P]
                        ins = mm(s[:, c * 512:(c + 1) * 512], o, w_out[:, k, c * 512:(c + 1) * 512], k == 0, k == KD - 1)
                ins.then_inc(full_of(("out", L, t)), 1)

            def attention(L):
                pl = plans[L]
                if L == 0:
                    emptied(pe, ("qbT", NT - 1))
                    emptied(pe, ("kbT", NT - 1))
                    pe.wait_ge(ctxv_in, 16 * 2)
                    pe.wait_ge(masks_ready, 1)
                else:
                    for g in range(1, 4):
                        emptied(pe, ("oq", NT - 1, g))
                    emptied(pe, ("kT2", 0))
                    emptied(pe, ("v2", 0))
                scores(L, 0)
                for i in range(pl.steps):
                    if i + 1 < pl.n:
                        if L == 1 and (i + 1) % PAIR == 0:
                            emptied(pe, ("kT2", (i + 1) // PAIR))
                            emptied(pe, ("v2", (i + 1) // PAIR))
                        scores(L, i + 1)
                    k = pl.due.get(i)
                    if k is not None:
                        turn_p(L, k)
                        if L == 0 and k > 0:
                            pv(k - 1)
                        elif L == 1 and k > 0 and k % 2 == 0:
                            pv_pair(k // 2 - 1)
                    elif i == pl.n + LAG[L]:
                        if L == 0:
                            pv(len(pl.parts) - 1)
                        else:
                            pv_pair(pl.n // 2 - 1)
                    for what, n in pl.extra.get(i, []):
                        if what == "ada":
                            ada(n)
                        elif what == "ada_turn":
                            ada_turn(n)
                        elif what == "kv":
                            kv(n)
                        elif what == "turn_o":
                            turn_o(n)
                        elif what == "out":
                            out(L, n)

            def router(L):
                wait_ht(2 * L + 1)
                pe.wait_ge(router_in, 16 * (L + 1))
                s = claim(("lgT", L), "S0")
                for c0, w in ((0, NS), (NS, NP_)):
                    for k in range(KD):
                        g = 32 * (k % 4)
                        ins = mm(s[g:g + 32, c0:c0 + w], wr[:, k, :], HT[:, k, c0:c0 + w], k < 4, k >= 4)
                ins.then_inc(full["S0"], 1)
                emptied(pe, ("lgT", L))
                s = claim(("lg", L), "S0")
                for t in range(NT):
                    ins = mm(s[:, t * NE:(t + 1) * NE], lgT[:, t * P:(t + 1) * P], C[:, C_SELE:C_SELE + NE])
                ins.then_inc(full["S0"], 1)
                pe.wait_ge(aff_ready, L + 1)
                s = claim(("affT", L), "S1")
                for t in range(TS):
                    turn(s[0:NE, t * P:(t + 1) * P], aff[:, t * NE:(t + 1) * NE])
                turn(s[0:R, NS:NTOK], aff[:, (NT - 3) * NE:]).then_inc(full["S1"], 1)
                pe.wait_ge(ax_ready, L + 1)
                s = claim(("g2", L), "S0")
                for k in range(KD):
                    ins = mm(s[0:SLOTS, k * P:(k + 1) * P], gx[:, k, :], ident)
                ins.then_inc(full["S0"], 1)
                pe.wait_ge(top_ready, L + 1)
                s = claim(("idx", L), "PT")
                turn(s[0:SLOTS, 0:R], topv)
                turn(s[0:SLOTS, 64:64 + R], topf).then_inc(full["PT"], 1)
                for r in place:
                    if uses[r]:
                        pe.wait_ge(free[r], uses[r])

            def experts(L):
                G, Up, XT = S[1][:, 0:320], S[1][:, 512:832], S[0][:, 0:1024].rearrange("p (k n) -> p k n", k=KD)
                base, half = L * NE, L * NE // 2

                def turn_xe(i, b, e):
                    pe.wait_ge(xe_in[b], 16 * (half + i + 1))
                    wait(pe, xt_read, base + e)
                    for k in range(KD):
                        ins = turn(XT[:, k, 0:SLOTS], xe[b][:, k * P:(k + 1) * P])
                    ins.then_inc(xt_mm, 1)

                def expert(i, b, last):
                    e = 2 * i + b
                    wg = ring[:, (3 * b) * U:(3 * b + 1) * U].rearrange("p (k n) -> p k n", k=KD)
                    wu = ring[:, (3 * b + 1) * U:(3 * b + 2) * U].rearrange("p (k n) -> p k n", k=KD)
                    wd = ring[:, (3 * b + 2) * U:(3 * b + 3) * U].rearrange("p (k n) -> p k n", k=4)
                    pe.wait_ge(xt_ready, base + e + 1)
                    wait(pe, silu_done, base + e)
                    pe.wait_ge(wg_in[b], 16 * (half + i + 1))
                    for f in range(4):
                        for k in range(KD):
                            ins = mm(G[:, f * SLOTS:(f + 1) * SLOTS], wg[:, k, f * P:(f + 1) * P], xeT[b][:, k, :], k == 0, k == KD - 1)
                    ins.then_inc(gate_mm, 1)
                    wait(pe, hid_ready, base + e)
                    pe.wait_ge(wu_in[b], 16 * (half + i + 1))
                    for f in range(4):
                        for k in range(KD):
                            ins = mm(Up[:, f * SLOTS:(f + 1) * SLOTS], wu[:, k, f * P:(f + 1) * P], xeT[b][:, k, :], k == 0, k == KD - 1)
                    ins.then_inc(up_mm, 1)
                    if not last:
                        turn_xe(i + b, 1 - b, e + 1)
                    pe.wait_ge(hid_ready, base + e + 1)
                    wait(pe, y_scaled, base + e)
                    pe.wait_ge(wd_in[b], 16 * (half + i + 1))
                    for c in range(2):
                        for f in range(4):
                            ins = mm(T[0:SLOTS, c * 512:(c + 1) * 512], hid[b][:, f * SLOTS:(f + 1) * SLOTS], wd[:, f, c * 512:(c + 1) * 512], f == 0, f == 3)
                    ins.then_inc(down_mm, 1)

                turn_xe(0, 0, 0)
                expert(0, 0, False)
                expert(0, 1, False)
                with pe.Fori(1, NE // 2 - 1, 1) as i:
                    expert(i, 0, False)
                    expert(i, 1, False)
                expert(NE // 2 - 1, 0, False)
                expert(NE // 2 - 1, 1, True)
                pe.wait_ge(y_scaled, base + NE)

            vectors()
            for u in ADA_START:
                ada(u)
                ada_turn(u)
                if u == 2:
                    turn_x(0, range(0, 4))
            turn_x(0, range(4, KD))
            even_project()
            gate_rows(0)
            attention(0)
            turn_x(1)
            router(0)
            experts(0)
            gate_rows(1)
            turn_x(2)
            odd_project()
            kv(0)
            attention(1)
            turn_x(3)
            router(1)
            experts(1)

        @block.vector
        def _(_):
            def ada_out(u):
                L, m, half = u // 12, (u % 12) // 2, u % 2
                s = filled(dve, ("ada_t", u))
                dst = mods[:, L, m, 4 * half:4 * half + 4, :]
                bias = VC1[:, 64 * L + 8 * m + 4 * half:64 * L + 8 * m + 4 * half + 4]
                dve.tensor_tensor(dst, s[:, 0:8].rearrange("p (k s) -> p k s", s=2), spread(bias, 2), ALU.add).then_inc(free["AD"], 1)
                if m in (1, 4):
                    gain = VC1[:, 64 * L + 48 + 8 * (m == 4) + 4 * half:64 * L + 52 + 8 * (m == 4) + 4 * half]
                    emptied(dve, ("ada_t", u))
                    dve.scalar_tensor_tensor(modA[:, L, int(m == 4), 4 * half:4 * half + 4, :], dst, 1.0, spread(gain, 2),
                                             ALU.add, ALU.mult).then_inc(mod_ready, 1)

            def scale_x(n, t):
                if n in (1, 3) and t < TS:
                    dve.wait_ge(x1_out[t], 16 * (n // 2 + 1))
                dve.wait_ge(rstd_done, NT * n + t + 1)
                dve.tensor_scalar(xn_tile(n, t), X[:, t, :], rstd[:, t:t + 1], None, ALU.mult).then_inc(xn_done, 1)

            def ht_tile(n, k):
                L, w = n // 2, n % 2
                dve.wait_ge(mod_ready, 2 * n + 1 + (k >= 4))
                s = filled(dve, ("nt", n, k))
                dve.tensor_scalar(HT[:, k, 0:NS], s[:, 0:NS], modA[:, L, w, k, 0:1], mods[:, L, 3 * w, k, 0:1], ALU.mult, ALU.add)\
                   .then_inc(free_of(("nt", n, k)), 1)

            def ht_prompt(n):
                L, w = n // 2, n % 2
                s = filled(dve, ("ntp", n, 1))
                for j in range(4):
                    k = 4 + j
                    ins = dve.tensor_scalar(HT[:, k, NS:NTOK], s[:, j * P:(j + 1) * P], modA[:, L, w, k, 1:2], mods[:, L, 3 * w, k, 1:2],
                                            ALU.mult, ALU.add)
                ins.then_inc(free_of(("ntp", n, 1)), 1)

            def ht(n):
                for k in range(1, KD, 2):
                    ht_tile(n, k)
                ht_prompt(n)

            dlink(dve.memset(coef[:, 0:1], 1.0))
            s = filled(dve, "vec")
            dve.memset(csil, 0.0)
            dve.tensor_copy(VC1[:], s[:, 0:P])
            dve.tensor_copy(VC2[:], s[:, P:P + 22]).then_inc(free["S0"], 1)
            dve.wait_ge(free["S0"], 1)
            dlink(dve.tensor_scalar(VC2[:, 21:22], VC2[:, 21:22], 1.0 - LAM_INIT, None, ALU.mult))
            ada_out(0)
            for t in range(NT):
                scale_x(0, t)
            ada_out(2)
            for k in (1, 3):
                ht_tile(0, k)
            ada_out(1)
            ada_out(3)
            for k in (5, 7):
                ht_tile(0, k)
            ht_prompt(0)
            dve.wait_ge(small_in, 16 * 2)
            lq = lamv[:].rearrange("p (a b n) -> p a b n", a=2, b=2)
            lprod = GB[:, 1280:1408]
            dlink(dve.tensor_tensor(lprod.rearrange("p (a n) -> p a n", a=2), lq[:, :, 0, :], lq[:, :, 1, :], ALU.mult))
            dve.tensor_reduce(lam2[:], lprod.rearrange("p (a n) -> p a n", a=2), AX, ALU.add).then_inc(lam_ready, 1)
            dve.tensor_scalar(sink8[:], sink[:], 8.0, None, ALU.mult)
            dve.wait_ge(lam_exp, 1)
            dlink(dve.tensor_tensor(coef[:, 1:2], lame[:, 1:2], lame[:, 0:1], ALU.subtract))
            dlink(dve.tensor_scalar(coef[:, 1:2], coef[:, 1:2], -LAM_INIT, None, ALU.add))

            def rope(dst, tmp, cos, sin, heads, done):
                d4 = dst.rearrange("p h (r x q) -> p h r x q", r=2, x=2)
                t4 = tmp.rearrange("p h (r x q) -> p h r x q", r=2, x=2)
                s4 = over_heads(sin, heads).rearrange("p h (r x q) -> p h r x q", r=2, x=2)
                for x in range(2):
                    ins = dve.tensor_tensor(t4[:, :, :, x, :], d4[:, :, :, 1 - x, :], s4[:, :, :, x, :], ALU.mult)
                dlink(ins)
                dlink(dve.tensor_tensor(dst, dst, over_heads(cos, heads), ALU.mult))
                dve.tensor_tensor(dst, dst, tmp, ALU.add).then_inc(done, 1)

            def context_turned():
                for j in range(2):
                    s = filled(dve, ("ckT", j))
                    dve.tensor_copy(kaT[:, :, j * P:(j + 1) * P], s[:, 0:512].rearrange("p (h n) -> p h n", h=4)).then_inc(free_of(("ckT", j)), 1)
                s = filled(dve, "cksT")
                dve.tensor_copy(kbT[:, 0:PAST], s[:, 0:PAST]).then_inc(free_of("cksT"), 1)

            def k_turned(t):
                kt = t + 2
                s = filled(dve, ("kT", t))
                dve.tensor_copy(kaT[:, :, kt * P:(kt + 1) * P], s[:, 0:512].rearrange("p (h n) -> p h n", h=4)).then_inc(free_of(("kT", t)), 1)
                s = filled(dve, ("kbT", t))
                dve.tensor_copy(kbT[:, kt * P:(kt + 1) * P], s[:, 0:P]).then_inc(free_of(("kbT", t)), 1)

            for t in range(NT):
                if t == 0:
                    context_turned()
                else:
                    ada_out(2 + 2 * t)
                    ada_out(3 + 2 * t)
                    k_turned(t - 1)
                if t < TS:
                    emptied(dve, ("proj", t, 4))
                    rope(raw[t % 2].rearrange("p (h n) -> p h n", n=HD), rtmp.rearrange("p (h n) -> p h n", n=HD),
                         C[:, C_C64 + 64 * t:C_C64 + 64 * (t + 1)], C[:, C_S64 + 64 * t:C_S64 + 64 * (t + 1)], QK // HD, rope_done)
            k_turned(NT - 1)
            ada_out(2 + 2 * NT)

            dve.wait_ge(ssq_done, NT)
            for to, at in ((bf_id, C_ID), (bf_left, C_LEFT), (bf_right, C_RIGHT)):
                ins = dve.tensor_copy(to, C[:, at:at + P])
            ins.then_inc(masks_ready, 1)

            def row_max(L, u):
                pl = plans[L]
                kind, t, i, c = pl.units[u]
                nk = len(pl.keys(u)) * P
                b = u % 8
                s = filled(dve, ("s", L, u))[:, 0:nk]
                g = units_before[L] + u
                if u >= 8:
                    emptied(dve, ("s", L, u - 8))
                    if pl.units[u - 8][0] == "swa":
                        dve.wait_ge(sne_done, swa_number(u - 8))
                dlink(dve.tensor_reduce(mx[:, b:b + 1], s, AX, ALU.max))
                scale = -(HD ** -0.5) if L == 0 else -(MQ ** -0.5)
                if kind == "swa":
                    h = i + 4 * c
                    dve.tensor_scalar(nm[:, b:b + 1], mx[:, b:b + 1], sink8[:, h:h + 1], scale, ALU.max, ALU.mult).then_inc(nm_done, 1)
                    dve.wait_ge(nm_done, g + 1)
                    dve.tensor_tensor(snk[:, b:b + 1], sink[:, h:h + 1], nm[:, b:b + 1], ALU.add).then_inc(snk_done, 1)
                else:
                    dve.tensor_scalar(nm[:, b:b + 1], mx[:, b:b + 1], scale, None, ALU.mult).then_inc(nm_done, 1)

            def combine(L, u):
                pl = plans[L]
                kind, t, i, c = pl.units[u]
                nk = len(pl.keys(u)) * P
                b = u % 8
                emptied(dve, ("s", L, u))
                if kind == "swa":
                    dve.wait_ge(sne_done, swa_number(u))
                    dlink(dve.tensor_tensor(den[:, b:b + 1], den[:, b:b + 1], sne[:, b:b + 1], ALU.add))
                dlink(dve.reciprocal(rr[:, b:b + 1], den[:, b:b + 1]))
                if kind == "mla":
                    row = Prow[L][u % ROWS[L]][:, 0:nk]
                    dve.tensor_scalar(row, row, rr[:, b:b + 1], None, ALU.mult).then_inc(p_scaled, 1)
                if kind == "diff" and c == 1:
                    p0, p1 = Prow[L][(u - 1) % ROWS[L]][:, 0:nk], Prow[L][u % ROWS[L]][:, 0:nk]
                    dlink(dve.tensor_scalar(p1, p1, rr[:, b:b + 1], coef[:, 1:2], ALU.mult, ALU.mult))
                    dve.scalar_tensor_tensor(p0, p0, rr[:, b - 1:b], p1, ALU.mult, ALU.add).then_inc(comb_done, 1)

            def pv_read(k):
                u = even.parts[k]
                kind, t, i, c = even.units[u]
                s = filled(dve, ("pv", 0, k))
                c0, w = o_cols(k)
                o = Oe[t % 2]
                if t >= 2:
                    filled(dve, ("oT", t - 2))
                if kind == "diff":
                    dve.tensor_copy(o[:, c0:c0 + w], s[:, 0:w]).then_inc(free["PV"], 1)
                else:
                    dve.tensor_scalar(o[:, c0:c0 + w], s[:, 0:w], rr[:, u % 8:u % 8 + 1], None, ALU.mult).then_inc(free["PV"], 1)

            def pair_read(q):
                kind, t, i, _ = odd.units[2 * q]
                s = filled(dve, ("pv", 1, q))
                dve.tensor_copy(OTo[:, i, t * P:(t + 1) * P], s[:, 0:P]).then_inc(free["PV"], 1)

            def norm_o(t):
                o = Oe[t % 2]
                emptied(dve, ("pv", 0, even.of_unit[16 * t + 15]))
                o3 = o[:, 0:512].rearrange("p (h n) -> p h n", h=4)
                for h in range(4):
                    ins = dve.scalar_tensor_tensor(sqs[:, h * P:(h + 1) * P], o3[:, h, :], 1.0, o3[:, h, :], ALU.mult, ALU.mult, accum_out=sub4[:, h:h + 1])
                ins.then_inc(sub_ss, 1)

            def scale_o(t):
                o3 = Oe[t % 2][:, 0:512].rearrange("p (h n) -> p h n", h=4)
                dve.wait_ge(sub_rstd, t + 1)
                dve.tensor_tensor(o3, o3, spread(subr[:], P), ALU.mult).then_inc(o_ready, 1)

            def o_turned(t):
                s = filled(dve, ("oT", t))
                if t > 0:
                    filled(dve, ("out", 0, t - 1))
                dve.tensor_scalar(OTe[:, 0:512], s[:, 0:512], VC2[:, 21:22], None, ALU.mult)
                dve.tensor_copy(OTe[:, 512:1024], s[:, 512:1024]).then_inc(free_of(("oT", t)), 1)

            def residual(L, t):
                if t == 0:
                    emptied(dve, ("gb", L, 0))
                    emptied(dve, ("gb", L, 1))
                s = filled(dve, ("out", L, t))
                g = GB[:, 0:D] if t < TS else GB[:, D:2 * D]
                dve.tensor_tensor(X[:, t, :], s[:, 0:D], g, ALU.mult).then_inc(free_of(("out", L, t)), 1)

            def add_x(L, t):
                dve.wait_ge(xin_in, 16 * (NT * L + t + 1))
                emptied(dve, ("out", L, t))
                dve.tensor_tensor(X[:, t, :], X[:, t, :], xin[L], ALU.add).then_inc(x1_done, 1)

            def attention(L):
                pl = plans[L]
                row_max(L, 0)
                for i in range(pl.steps):
                    if i + 1 < pl.n:
                        row_max(L, i + 1)
                    if i < pl.n:
                        combine(L, i)
                    k = pl.due.get(i)
                    if L == 0 and k:
                        pv_read(k - 1)
                    elif L == 1 and k and k % 2 == 0:
                        pair_read(k // 2 - 1)
                    elif i == pl.n + LAG[L]:
                        if L == 0:
                            pv_read(len(pl.parts) - 1)
                        else:
                            pair_read(pl.n // 2 - 1)
                    for what, n in pl.extra.get(i, []):
                        if what == "ada_turn":
                            ada_out(n)
                        elif what == "norm_o":
                            norm_o(n)
                        elif what == "scale_o":
                            scale_o(n)
                        elif what == "add_x":
                            add_x(L, n)
                        elif what == "turn_o":
                            o_turned(n)
                        elif what == "out":
                            residual(L, n)
                        elif what == "scale":
                            scale_x(2 * L + 1, n)
                        elif what == "kv":
                            kv_read(n)

            def router(L):
                dve.memset(topv[:, CAP_S:], 0.0)
                dve.memset(topf[:, CAP_S:], 0.0)
                dve.memset(affT, -1.0)
                s = filled(dve, ("lgT", L))
                dve.tensor_copy(lgT, s[:, 0:NTOK]).then_inc(free["S0"], 1)
                s = filled(dve, ("lg", L))
                s3 = s[:, 0:NT * NE].rearrange("p (t e) -> p t e", t=NT)
                dlink(dve.tensor_reduce(rs5[:, 0, :], s3, AX, ALU.max))
                dve.tensor_tensor(lg.rearrange("p (t e) -> p t e", t=NT), s3, spread(rs5[:, 0, :], NE), ALU.subtract).then_inc(free["S0"], 1)
                for dst, src in ((AXs, modA[:, L, 1]), (BXs, mods[:, L, 3]), (gx, mods[:, L, 5])):
                    dve.tensor_copy(dst[:, :, 0:CAP_S], spread(src[:, :, 0], CAP_S))
                    ins = dve.tensor_copy(dst[:, :, CAP_S:SLOTS], spread(src[:, :, 1], CAP_P))
                ins.then_inc(ax_ready, 1)
                dve.wait_ge(lge_done, L + 1)
                dlink(dve.tensor_reduce(rs5[:, 1, :], lge.rearrange("p (t e) -> p t e", t=NT), AX, ALU.add))
                dlink(dve.reciprocal(rs5[:, 2, :], rs5[:, 1, :]))
                dve.tensor_tensor(aff.rearrange("p (t e) -> p t e", t=NT), lge.rearrange("p (t e) -> p t e", t=NT),
                                  spread(rs5[:, 2, :], NE), ALU.mult).then_inc(aff_ready, 1)
                s = filled(dve, ("affT", L))
                dve.tensor_copy(affT[0:NE, :], s[0:NE, 0:NS])
                dve.tensor_copy(affT[32:R, 0:NP_], s[32:R, NS:NTOK]).then_inc(free["S1"], 1)
                emptied(dve, ("affT", L))
                for r in range(CAP_S // 8):
                    v, ix = topv[:, 8 * r:8 * r + 8], topi[:, 8 * r:8 * r + 8]
                    dlink(dve.max(v, affT))
                    ins = dve.max_index(ix, v, affT)
                    if r < CAP_S // 8 - 1:
                        dlink(dve.match_replace(affT, v, affT, -1.0))
                dlink(ins)
                dve.tensor_copy(topv[32:R, CAP_S:], topv[32:R, 0:CAP_P])
                dve.tensor_copy(topf[32:R, CAP_S:], topi[32:R, 0:CAP_P])
                dlink(dve.tensor_copy(topf[:, 0:CAP_S], topi[:, 0:CAP_S]))
                dve.tensor_scalar(topf[32:R, CAP_S:], topf[32:R, CAP_S:], float(NS), None, ALU.add).then_inc(top_ready, 1)
                s = filled(dve, ("idx", L))
                for to, at in ((gates, 0), (idxi, 64)):
                    dve.tensor_copy(to[0:CAP_S, :], s[0:CAP_S, at:at + NE])
                    ins = dve.tensor_copy(to[CAP_S:, :], s[CAP_S:SLOTS, at + 32:at + R])
                ins.then_inc(free["PT"], 1)

            def experts(L):
                G, Up, XT = S[1][:, 0:320], S[1][:, 512:832], S[0][:, 0:1024].rearrange("p (k n) -> p k n", k=KD)
                base, half = L * NE, L * NE // 2

                def modulate_xe(b, e):
                    dve.wait_ge(xt_mm, base + e + 1)
                    wait(dve, up_mm, base + e - 1)
                    dve.tensor_tensor(xeT[b], XT[:, :, 0:SLOTS], AXs, ALU.mult).then_inc(xt_read, 1)
                    dve.wait_ge(xt_read, base + e + 1)
                    dve.tensor_tensor(xeT[b], xeT[b], BXs, ALU.add).then_inc(xt_ready, 1)

                def expert(i, b, last):
                    e = 2 * i + b
                    dve.wait_ge(silu_done, base + e + 1)
                    dve.wait_ge(up_mm, base + e + 1)
                    wait(dve, down_mm, base + e - 1)
                    dve.tensor_tensor(hid[b], sg[b], Up, ALU.mult).then_inc(hid_ready, 1)
                    if not last:
                        modulate_xe(1 - b, e + 1)
                    dve.wait_ge(down_mm, base + e + 1)
                    wait(dve, added[b], 16 * (half + i))
                    dve.scalar_tensor_tensor(ys[b], T[0:SLOTS, 0:D], gates[:, bass.ds(e, 1)] if not isinstance(e, int) else gates[:, e:e + 1],
                                             g2b, ALU.mult, ALU.mult).then_inc(y_scaled, 1)

                dve.wait_ge(free["S0"], slot[("g2", L)][1])
                modulate_xe(0, 0)
                expert(0, 0, False)
                expert(0, 1, False)
                with dve.Fori(1, NE // 2 - 1, 1) as i:
                    expert(i, 0, False)
                    expert(i, 1, False)
                expert(NE // 2 - 1, 0, False)
                expert(NE // 2 - 1, 1, True)

            def odd_project():
                s = filled(dve, "occ")
                dve.tensor_copy(ckvT[:, :, 0:PAST], s[:, 0:512].rearrange("p (k n) -> p k n", k=2)).then_inc(free["PT"], 1)
                s = filled(dve, "ocr")
                dve.tensor_copy(krT[:, 0:PAST], s[0:RD, 0:PAST]).then_inc(free["S0"], 1)

                def c_turned(t):
                    kt = t + 2
                    s = filled(dve, ("oc", t))
                    for k in range(3):
                        dve.tensor_scalar(cqT[:, k, t * P:(t + 1) * P], s[:, k * P:(k + 1) * P], VC2[:, 16 + k:17 + k], None, ALU.mult)
                    dve.tensor_copy(ckvT[:, :, kt * P:(kt + 1) * P], s[:, 384:640].rearrange("p (k n) -> p k n", k=2))
                    dve.tensor_copy(krT[:, kt * P:(kt + 1) * P], s[0:RD, 640:768]).then_inc(free["PT"], 1)

                for t in range(NT):
                    r = rawo[t % 2]
                    dve.wait_ge(krs_done, t + 1)
                    wait(dve, cq_ready, t)
                    dve.tensor_scalar(r[:, 0:QR], r[:, 0:QR], rsk[:, 0, t:t + 1], None, ALU.mult)
                    if t < TS:
                        x = r[:, 640:672].rearrange("p (h n) -> p h n", h=1)
                        d4 = x.rearrange("p h (r x q) -> p h r x q", r=2, x=2)
                        t4 = rtk.rearrange("p (h n) -> p h n", h=1).rearrange("p h (r x q) -> p h r x q", r=2, x=2)
                        sn = C[:, C_S32 + 32 * t:C_S32 + 32 * (t + 1)].rearrange("p (h r x q) -> p h r x q", h=1, r=2, x=2)
                        for xx in range(2):
                            ins = dve.tensor_tensor(t4[:, :, :, xx, :], d4[:, :, :, 1 - xx, :], sn[:, :, :, xx, :], ALU.mult)
                        dlink(ins)
                        dlink(dve.tensor_tensor(r[:, 640:672], r[:, 640:672], C[:, C_C32 + 32 * t:C_C32 + 32 * (t + 1)], ALU.mult))
                        dve.tensor_tensor(r[:, 640:672], r[:, 640:672], rtk, ALU.add)
                    dve.scalar_tensor_tensor(r[:, QR:640], r[:, QR:640], rsk[:, 1, t:t + 1], kvn, ALU.mult, ALU.mult).then_inc(cq_ready, 1)
                    if t > 0:
                        c_turned(t - 1)
                c_turned(NT - 1)

                def q_rope(t):
                    q = qraw[t % 2].rearrange("p (h n) -> p h n", n=MQ)[:, :, HD:MQ]
                    rope(q, qtmp.rearrange("p (h n) -> p h n", n=RD), C[:, C_C32 + 32 * t:C_C32 + 32 * (t + 1)],
                         C[:, C_S32 + 32 * t:C_S32 + 32 * (t + 1)], MH, qr_ready)

                for t in range(TS):
                    emptied(dve, ("qup", t, 2))
                    wait(dve, qr_ready, t)
                    q_rope(t)

            def kv_read(p):
                s = filled(dve, ("v2", p))
                if p >= 2:
                    filled(dve, ("pv", 1, NT * (p - 1) - 1))
                dve.tensor_copy(Vh[:, p % 2], s[:, 0:KCOL].rearrange("p (k n) -> p k n", k=KT)).then_inc(free_of(("v2", p)), 1)

            attention(0)
            ht(1)
            router(0)
            experts(0)
            for t in range(NT):
                scale_x(2, t)
            ht(2)
            odd_project()
            kv_read(0)
            attention(1)
            ht(3)
            router(1)
            experts(1)
            dve.wait_ge(fin_in, 16)
            for t in range(NT):
                dve.wait_ge(rstd_done, 4 * NT + t + 1)
                dve.scalar_tensor_tensor(X[:, t, :], X[:, t, :], rstd[:, t:t + 1], fin, ALU.mult, ALU.mult).then_inc(y_ready, 1)

        @block.scalar
        def _(_):
            def square(n, t):
                if n == 0:
                    act.wait_ge(x_in[t], 16)
                elif n in (1, 3):
                    act.wait_ge(x1_done, NT * (n // 2) + t + 1)
                else:
                    act.wait_ge(x_back[t], 16 * (n // 2))
                wait(act, rstd_done, NT * (n - 1) + t + 1)
                wait(act, ssq_done, NT * n + t)
                act.activation(squares_at[n], X[:, t, :], ACT.Square, accum_out=ss[:, t:t + 1]).then_inc(ssq_done, 1)

            def ht_tile(n, k):
                L, w = n // 2, n % 2
                act.wait_ge(mod_ready, 2 * n + 1 + (k >= 4))
                s = filled(act, ("nt", n, k))
                act.activation(HT[:, k, 0:NS], s[:, 0:NS], ACT.Identity, bias=mods[:, L, 3 * w, k, 0:1], scale=modA[:, L, w, k, 0:1])\
                   .then_inc(free_of(("nt", n, k)), 1)

            def ht_prompt(n):
                L, w = n // 2, n % 2
                s = filled(act, ("ntp", n, 0))
                for j in range(4):
                    ins = act.activation(HT[:, j, NS:NTOK], s[:, j * P:(j + 1) * P], ACT.Identity, bias=mods[:, L, 3 * w, j, 1:2],
                                         scale=modA[:, L, w, j, 1:2])
                ins.then_inc(free_of(("ntp", n, 0)), 1)

            def ht(n):
                for k in range(0, KD, 2):
                    ht_tile(n, k)
                ht_prompt(n)

            def ada_read(u):
                s = filled(act, ("ada", u))
                if u > 0:
                    filled(act, ("ada_t", ada_before(u)))
                act.copy(ada_sum, s[:, 0:512]).then_inc(free["AD"], 1)

            act.wait_ge(free["S0"], 1)
            act.activation(csil[:, :, 0:2].rearrange("p k s -> p s k"), VC2[:, 0:16].rearrange("p (s k) -> p s k", s=2), ACT.Silu)\
               .then_inc(csil_ready, 1)
            ada_read(0)
            for t in range(NT):
                square(0, t)
            ada_read(2)
            for k in (0, 2):
                ht_tile(0, k)
            ada_read(1)
            ada_read(3)
            for k in (4, 6):
                ht_tile(0, k)
            ht_prompt(0)
            act.wait_ge(lam_ready, 1)
            act.activation(lame[:], lam2[:], ACT.Exp).then_inc(lam_exp, 1)

            def raw_read(t):
                r = raw[t % 2]
                kt = t + 2
                for c in range(5):
                    if c == 2 and t > 0:
                        ada_read(3 + 2 * t)
                    s = filled(act, ("proj", t, c))
                    if c == 0 and t >= 2:
                        filled(act, ("kbT", t - 2))
                    if c < 2:
                        ins = act.copy(r[:, c * 512:(c + 1) * 512], s[:, 0:512])
                    elif c == 2:
                        ins = act.copy(va[:, kt, :], s[:, 0:512])
                    elif c == 3:
                        ins = act.copy(r[:, 1024:1536].rearrange("p (h a d) -> p a h d", a=2, h=4),
                                       s[:, 0:512].rearrange("p (a h d) -> p a h d", a=2, h=4))
                    else:
                        act.copy(r[:, 1536:1664], s[:, 0:P])
                        ins = act.copy(vb[:, kt, :], s[:, P:2 * P])
                    ins.then_inc(free_of(("proj", t, c)), 1)

            def q_turned(t):
                s = filled(act, ("qT", t))
                act.copy(QTe[:, t, 0:4, :], s[:, 0:512].rearrange("p (h n) -> p h n", h=4)).then_inc(free_of(("qT", t)), 1)
                s = filled(act, ("qbT", t))
                act.copy(QTe[:, t, 4:8, :], s[:, 0:512].rearrange("p (h n) -> p h n", h=4)).then_inc(free_of(("qbT", t)), 1)

            for t in range(NT):
                raw_read(t)
                if t > 0:
                    q_turned(t - 1)
                ada_read(4 + 2 * t)
            q_turned(NT - 1)

            def gate_rows(L):
                if L == 1:
                    for b in range(2):
                        act.wait_ge(added[b], 16 * (NE // 2))
                for s_ in range(2):
                    s = filled(act, ("gb", L, s_))
                    act.copy(GB[:, s_ * D:(s_ + 1) * D], s[:, 0:D]).then_inc(free_of(("gb", L, s_)), 1)

            def exps(L, u):
                pl = plans[L]
                kind, t, i, c = pl.units[u]
                nk = len(pl.keys(u)) * P
                b = u % 8
                s = filled(act, ("s", L, u))
                act.wait_ge(nm_done, units_before[L] + u + 1)
                if u >= ROWS[L]:
                    filled(act, ("pt", L, pl.read_at[u - ROWS[L]]))
                scale = HD ** -0.5 if L == 0 else MQ ** -0.5
                act.activation(Prow[L][u % ROWS[L]][:, 0:nk], s[:, 0:nk], ACT.Exp, bias=nm[:, b:b + 1], scale=scale,
                               accum_out=den[:, b:b + 1]).then_inc(free_of(("s", L, u)), 1)
                if kind == "swa":
                    act.wait_ge(snk_done, swa_number(u))
                    act.activation(sne[:, b:b + 1], snk[:, b:b + 1], ACT.Exp).then_inc(sne_done, 1)

            def pt_read(L, k):
                pl = plans[L]
                n = len(pl.keys(pl.parts[k])) * P
                s = filled(act, ("pt", L, k))
                if L == 0 and k >= 2:
                    filled(act, ("pv", 0, k - 2))
                elif L == 1 and k >= 4:
                    filled(act, ("pv", 1, k // 2 - 2))
                act.copy(PTs[L][k % len(PTs[L])][:, 0:n], s[:, 0:n]).then_inc(free["PT"], 1)

            def kv_read(p):
                s = filled(act, ("kT2", p))
                if p == 0:
                    filled(act, ("oq", NT - 1, 3))
                if p >= 2:
                    filled(act, ("s", 1, PAIR * (p - 1) - 1))
                for j in range(2):
                    act.copy(KTh[0:HD, p % 2, j, :], s[j * HD:(j + 1) * HD, 0:KCOL])
                    ins = act.copy(KTh[HD:MQ, p % 2, j, :], krT)
                ins.then_inc(free_of(("kT2", p)), 1)

            def attention(L):
                pl = plans[L]
                exps(L, 0)
                for i in range(pl.steps):
                    if i in pl.due:
                        pt_read(L, pl.due[i])
                    if i + 1 < pl.n:
                        exps(L, i + 1)
                    for what, n in pl.extra.get(i, []):
                        if what == "kv":
                            kv_read(n)
                        elif what == "ada":
                            ada_read(n)
                        elif what == "square":
                            square(2 * L + 1, n)

            def router(L):
                emptied(act, ("lg", L))
                act.activation(lge, lg, ACT.Exp).then_inc(lge_done, 1)
                s = filled(act, ("g2", L))
                act.copy(g2b, s[0:SLOTS, 0:D]).then_inc(free["S0"], 1)

            def experts(L):
                G = S[1][:, 0:320]
                base = L * NE

                def expert(i, b):
                    e = 2 * i + b
                    act.wait_ge(gate_mm, base + e + 1)
                    wait(act, hid_ready, base + e - 1)
                    act.activation(sg[b], G, ACT.Silu).then_inc(silu_done, 1)

                expert(0, 0)
                expert(0, 1)
                with act.Fori(1, NE // 2, 1) as i:
                    expert(i, 0)
                    expert(i, 1)

            def odd_project():
                for t in range(NT):
                    s = filled(act, ("oproj", t))
                    if t >= 2:
                        filled(act, ("oc", t - 2))
                    act.copy(rawo[t % 2], s[:, 0:ODD_IN])
                    if t > 0:
                        emptied(act, ("oproj", t - 1))
                    act.activation(junk[:, 0:QR], s[:, 0:QR], ACT.Square, accum_out=ssk[:, 0, t:t + 1])
                    act.activation(junk[:, QR:640], s[:, QR:640], ACT.Square, accum_out=ssk[:, 1, t:t + 1]).then_inc(free_of(("oproj", t)), 1)

                def q_read(t):
                    if t >= 2:
                        filled(act, ("oq", t - 2, 3))
                    for c in range(3):
                        s = filled(act, ("qup", t, c))
                        act.copy(qraw[t % 2][:, c * 512:(c + 1) * 512], s[:, 0:512]).then_inc(free_of(("qup", t, c)), 1)

                def q_turned(t):
                    for g in range(4):
                        s = filled(act, ("oq", t, g))
                        ins = act.copy(QTo[:, 4 * g:4 * g + 4, t * P:(t + 1) * P], s[0:MQ, 0:512].rearrange("p (h n) -> p h n", h=4))
                        ins.then_inc(free_of(("oq", t, g)), 1)

                for t in range(NT):
                    q_read(t)
                    if t > 0:
                        q_turned(t - 1)
                q_turned(NT - 1)

            gate_rows(0)
            attention(0)
            ht(1)
            router(0)
            experts(0)
            gate_rows(1)
            for t in range(NT):
                square(2, t)
            ht(2)
            odd_project()
            kv_read(0)
            attention(1)
            ht(3)
            router(1)
            experts(1)
            for t in range(NT):
                square(4, t)

        @block.gpsimd
        def _(_):
            def rms(n, t):
                pool.wait_ge(ssq_done, NT * n + t + 1)
                plink(pool.tensor_scalar(rstd[:, t:t + 1], ss[:, t:t + 1], 1.0 / D, EPS, ALU.mult, ALU.add))
                pool.tensor_tensor(rstd[:, t:t + 1], rstd[:, t:t + 1], mhalf[:, 0:1], ALU.pow).then_inc(rstd_done, 1)

            x_of = [a["x_sample"].rearrange("b s d -> (b s) d"), a["x_prompt"].rearrange("b s d -> (b s) d")]

            def x_tile(t):
                return x_of[0][t * P:(t + 1) * P, :] if t < TS else x_of[1]

            def load_xin(L, t):
                wait(pool, x1_done, NT * L + t)
                pool.dma_start(xin[L], x_tile(t) if L == 0 else a["xr"][0][t * P:(t + 1) * P, :]).then_inc(xin_in, 16)

            def store_x1(L, t):
                n = 2 * L + 1
                pool.wait_ge(x1_done, NT * L + t + 1)
                pool.dma_start(a["xr"][L][t * P:(t + 1) * P, :], X[:, t, :]).then_inc(x1_out[t], 16)
                rms(n, t)
                pool.wait_ge(xn_done, NT * n + t + 1)
                pool.dma_start(a["xn"][L][t * P:(t + 1) * P, :], xn_tile(n, t)).then_inc(xn_out, 16)

            def sub_norm(t):
                pool.wait_ge(sub_ss, t + 1)
                plink(pool.tensor_scalar(subr[:], sub4[:], 1.0 / P, EPS, ALU.mult, ALU.add))
                pool.tensor_tensor(subr[:], subr[:], mhalf[:, 0:4], ALU.pow).then_inc(sub_rstd, 1)

            def experts(L):
                base, half = L * NE, L * NE // 2

                def column(e):
                    return idxi[:, e:e + 1] if isinstance(e, int) else idxi[:, bass.ds(e, 1)]

                def gather(i, b, e):
                    wait(pool, xt_mm, base + e - 1)
                    wait(pool, xe_in[b], 16 * (half + i))
                    pool.sem_inc(gather_go, 1)
                    pool.tensor_copy(idx_from[b][:], column(e)).then_inc(from_ready, 1)
                    pool.wait_ge(from_ready, base + e + 1)
                    pool.sem_inc(gather_go, 1)
                    pool.indirect_dma_start(xe[b], None, a["xn"][L], bass.IndirectOffsetOnAxis(ap=idx_from[b][:, 0:1], axis=0))\
                        .then_inc(xe_in[b], 16)

                def expert(i, b, last):
                    e = 2 * i + b
                    if not last:
                        gather(i + b, 1 - b, e + 1)
                    wait(pool, added[b], 16 * (half + i))
                    pool.sem_inc(add_go, 1)
                    pool.tensor_copy(idx_to[b][:], column(e)).then_inc(to_ready, 1)
                    pool.wait_ge(to_ready, base + e + 1)
                    pool.wait_ge(y_scaled, base + e + 1)
                    wait(pool, added[1 - b], 16 * (half + i + b))
                    pool.sem_inc(add_go, 1)
                    pool.indirect_dma_start(a["xr"][L], bass.IndirectOffsetOnAxis(ap=idx_to[b][:, 0:1], axis=0), ys[b], None,
                                            compute_op=ALU.add).then_inc(added[b], 16)

                pool.wait_ge(xn_out, 16 * NT * (L + 1))
                for t in range(NT):
                    pool.wait_ge(x1_out[t], 16 * (L + 1))
                emptied(pool, ("idx", L))
                gather(0, 0, 0)
                expert(0, 0, False)
                expert(0, 1, False)
                with pool.Fori(1, NE // 2 - 1, 1) as i:
                    expert(i, 0, False)
                    expert(i, 1, False)
                expert(NE // 2 - 1, 0, False)
                expert(NE // 2 - 1, 1, True)
                for b in range(2):
                    pool.wait_ge(added[b], 16 * (half + NE // 2))

            plink(pool.memset(mhalf[:], -0.5))
            for t in range(NT):
                rms(0, t)
            emptied(pool, ("proj", TS, 4))
            r = raw[TS % 2]
            pool.dma_start(a["new_diff_k"].rearrange("a b s h d -> (a b s) (h d)"), r[:, 512:1024]).then_inc(prompt_out, 16)
            pool.dma_start(a["new_diff_v"].rearrange("a b s h d -> (a b s) (h d)"), va[:, KT - 1, :]).then_inc(prompt_out, 16)
            pool.dma_start(a["new_swa_k"].rearrange("a b s h d -> (a b s) (h d)"), r[:, 1536:1664]).then_inc(prompt_out, 16)
            pool.dma_start(a["new_swa_v"].rearrange("a b s h d -> (a b s) (h d)"), vb[:, KT - 1, :]).then_inc(prompt_out, 16)

            def spread_queries(t, m):
                emptied(pool, ("qbT", t))
                if t > 0:
                    filled(pool, ("s", 0, 16 * (t - 1) + 8 * m + 7))
                for c in range(2):
                    rows = slice(c * HD, (c + 1) * HD)
                    pool.tensor_copy(QZ[rows, m, c], QTe[rows, t, 4 * m:4 * m + 4, :]).then_inc(q_spread, 1)
                    pool.wait_ge(q_spread, 4 * t + 2 * m + c + 1)

            pool.memset(QZ, 0.0).then_inc(zeroed, 1)
            pool.wait_ge(zeroed, 1)
            spread_queries(0, 0)
            spread_queries(0, 1)
            for t in range(NT):
                if t == 0:
                    filled(pool, ("kbT", NT - 1))
                if t < NT - 1:
                    spread_queries(t + 1, 0)
                    spread_queries(t + 1, 1)
                load_xin(0, t)
                sub_norm(t)
                store_x1(0, t)
            experts(0)
            for t in range(NT):
                rms(2, t)
            for t in range(NT):
                emptied(pool, ("oproj", t))
                pool.tensor_scalar(rsk[:, 0, t:t + 1], ssk[:, 0, t:t + 1], 1.0 / QR, EPS, ALU.mult, ALU.add)
                plink(pool.tensor_scalar(rsk[:, 1, t:t + 1], ssk[:, 1, t:t + 1], 1.0 / KVR, EPS, ALU.mult, ALU.add))
                pool.tensor_tensor(rsk[:, :, t:t + 1], rsk[:, :, t:t + 1], mhalf[:, 0:2].rearrange("p (a b) -> p a b", b=1), ALU.pow)\
                    .then_inc(krs_done, 1)
            pool.wait_ge(cq_ready, NT)
            pool.dma_start(a["new_mla_ckv"].rearrange("a b s c -> (a b s) c"), rawo[TS % 2][:, QR:640]).then_inc(prompt_out, 16)
            pool.dma_start(a["new_mla_krope"].rearrange("a b s c -> (a b s) c"), rawo[TS % 2][:, 640:672]).then_inc(prompt_out, 16)
            for t in range(NT):
                if t == 0:
                    filled(pool, ("kT2", 0))
                load_xin(1, t)
                store_x1(1, t)
            experts(1)
            for t in range(NT):
                rms(4, t)
            pool.wait_ge(prompt_out, 16 * 6)

        @block.sync
        def _(_):
            sp.dma_start(C[:], a["consts"]).then_inc(consts_in, 16)
            for L in range(2):
                for row, src, n in ((64 * L, a["b_ada"][L], 48), (64 * L + 48, a["norm_mix"][L], 8), (64 * L + 56, a["norm_ffn"][L], 8)):
                    sp.dma_start(VR[row:row + n, 0, :], src.rearrange("(k n) -> k n", n=P)).then_inc(vec_in, 16)
            for row, src, n in ((0, a["c"][0], 8), (8, a["c_ctx"], 8), (16, a["mla_q_norm"][0], 3), (19, a["mla_kv_norm"][0], 2),
                                (21, a["diff_subln"][0], 1)):
                sp.dma_start(VR[row:row + n, 1, :], src.rearrange("(k n) -> k n", n=P)).then_inc(vec_in, 16)

            def load_ada(u):
                L, c0 = u // 12, (u % 12) * 512
                done = ada_first[u - 1] if 0 < u < 4 else ada_in
                sp.dma_start(ada_buf(u), a["w_ada"][L][:, c0:c0 + 512].rearrange("(k p) n -> p k n", p=P)).then_inc(done, 16)

            load_ada(0)
            x_s, x_p = a["x_sample"].rearrange("b s d -> (b s) d"), a["x_prompt"].rearrange("b s d -> (b s) d")
            for t in range(NT):
                sp.dma_start(X[:, t, :], x_s[t * P:(t + 1) * P, :] if t < TS else x_p).then_inc(x_in[t], 16)
            for u in ADA_START[1:]:
                load_ada(u)
            sp.dma_start(lamv[:], a["diff_lambda"][0].rearrange("a d -> (a d)").partition_broadcast(P)).then_inc(small_in, 16)
            sp.dma_start(sink[:], a["swa_sink"][0].partition_broadcast(P)).then_inc(small_in, 16)
            kd = a["cache_diff_k"].rearrange("a b s h d -> (a b s) (h d)").rearrange("(j p) n -> p j n", p=P)
            vd = a["cache_diff_v"].rearrange("a b s h d -> (a b s) (h d)").rearrange("(j p) n -> p j n", p=P)
            kw = a["cache_swa_k"].rearrange("a b s h d -> (a b s) (h d)").rearrange("(j p) n -> p j n", p=P)
            vw = a["cache_swa_v"].rearrange("a b s h d -> (a b s) (h d)").rearrange("(j p) n -> p j n", p=P)
            sp.dma_start(ctx_k, kd).then_inc(ctxk_in, 16)
            sp.dma_start(ctx_ks, kw).then_inc(ctxk_in, 16)
            w = a["w_in_even"][0].rearrange("(k p) n -> p k n", p=P)
            for c in range(5):
                sp.wait_ge(ada_in if c == 0 else ada_first[ADA_START[min(c, 3)] - 1], 16)
                n = 512 if c < 4 else 256
                sp.dma_start(w_in_e[:, :, c * 512:c * 512 + n], w[:, :, c * 512:c * 512 + n]).then_inc(win_in[c], 16)
            filled(sp, ("ada", 3))
            sp.dma_start(va[:, 0:2, :], vd).then_inc(ctxv_in, 16)
            sp.dma_start(vb[:, 0:2, :], vw).then_inc(ctxv_in, 16)

            def stage_ada(u):
                filled(sp, ("ada", u - 1))
                load_ada(u)

            def expert_loads(L, e, units="gud"):
                b = e % 2
                for i, (x, name, sems) in enumerate((("g", "w_gate_exp", wg_in), ("u", "w_up_exp", wu_in), ("d", "w_down_exp", wd_in))):
                    if x in units:
                        k = 4 if x == "d" else KD
                        sp.dma_start(ring[:, (3 * b + i) * U:(3 * b + i + 1) * U].rearrange("p (k n) -> p k n", k=k),
                                     a[name][L][e].rearrange("(k p) n -> p k n", p=P)).then_inc(sems[b], 16)

            def expert_stream(L):
                base = L * NE
                with sp.Fori(1, NE // 2, 1) as i:
                    for b in range(2):
                        for x, (name, sems, used) in enumerate((("w_gate_exp", wg_in, gate_mm), ("w_up_exp", wu_in, up_mm),
                                                                ("w_down_exp", wd_in, down_mm))):
                            k = 4 if x == 2 else KD
                            sp.wait_ge(used, base + 2 * i + b - 1)
                            src = a[name][L][bass.ds(2 * i + b, 1)].rearrange("e (k p) n -> p (e k) n", p=P)
                            sp.dma_start(ring[:, (3 * b + x) * U:(3 * b + x + 1) * U].rearrange("p (k n) -> p k n", k=k), src)\
                              .then_inc(sems[b], 16)

            def load_context():
                sp.dma_start(ctx_c, a["cache_mla_ckv"].rearrange("a b s c -> (a b s) c").rearrange("(j p) n -> p j n", p=P)).then_inc(ctxo_in, 16)
                sp.dma_start(ctx_r, a["cache_mla_krope"].rearrange("a b s c -> (a b s) c").rearrange("(j p) n -> p j n", p=P)).then_inc(ctxo_in, 16)
                sp.dma_start(kvn, a["mla_kv_norm"][0].partition_broadcast(P)).then_inc(ctxo_in, 16)

            def load_router(L):
                sp.dma_start(wr[:, :, 0:NE], a["w_router"][L].rearrange("(k p) n -> p k n", p=P)).then_inc(router_in, 16)

            def reload(L):
                for b in range(2):
                    sp.wait_ge(added[b], 16 * (NE // 2) * (L + 1))
                for t in range(NT):
                    sp.dma_start(X[:, t, :], a["xr"][L][t * P:(t + 1) * P, :]).then_inc(x_back[t], 16)

            for u in range(4, 4 + ADA_PROJ):
                stage_ada(u)
            filled(sp, ("kbT", NT - 1))
            stage_ada(4 + ADA_PROJ)
            stage_ada(5 + ADA_PROJ)
            sp.wait_ge(prompt_out, 16 * 4)
            sp.dma_start(w_out, a["w_out_even"][0].rearrange("(k p) n -> p k n", p=P)).then_inc(wout_in, 16)
            stage_ada(6 + ADA_PROJ)
            expert_loads(0, 0, "gu")
            for u in range(7 + ADA_PROJ, 24):
                stage_ada(u)
            filled(sp, ("ada", 23))
            load_router(0)
            sp.wait_ge(x1_done, NT)
            sp.wait_ge(ssq_done, 2 * NT)
            expert_loads(0, 0, "d")
            expert_loads(0, 1)
            expert_stream(0)
            sp.wait_ge(down_mm, NE - 1)
            sp.dma_start(w_in_o, a["w_in_odd"][0].rearrange("(k p) n -> p k n", p=P)).then_inc(odd_in, 16)
            sp.dma_start(w_qup, a["w_q_up"][0].rearrange("(k p) n -> p k n", p=P)).then_inc(qup_in, 16)
            reload(0)
            load_context()
            load_router(1)
            for k in range(2):
                src = a["w_kv_up"][0].rearrange("(k p) (h c n) -> k c p h n", p=P, h=MH, c=2)
                for c in range(2):
                    sp.dma_start(w_kvup[:, k, c * D:(c + 1) * D].rearrange("p (h n) -> p h n", h=MH), src[k, c]).then_inc(kvup_in, 16)
            sp.dma_start(w_out, a["w_out_odd"][0].rearrange("(k p) n -> p k n", p=P)).then_inc(wout_in, 16)
            sp.wait_ge(x1_done, 2 * NT)
            expert_loads(1, 0)
            expert_loads(1, 1)
            emptied(sp, ("idx", 1))
            sp.dma_start(fin, a["final_norm"].partition_broadcast(P)).then_inc(fin_in, 16)
            expert_stream(1)
            reload(1)
            ys_of = [a["y_sample"].rearrange("b s d -> (b s) d"), a["y_prompt"].rearrange("b s d -> (b s) d")]
            for t in range(NT):
                sp.wait_ge(y_ready, t + 1)
                dst = ys_of[0][t * P:(t + 1) * P, :] if t < TS else ys_of[1]
                sp.dma_start(dst, X[:, t, :]).then_inc(y_out, 16)
            sp.wait_ge(y_out, 16 * NT)


_INS = ["x_prompt", "x_sample", "cache_diff_k", "cache_diff_v", "cache_swa_k", "cache_swa_v", "cache_mla_ckv",
        "cache_mla_krope", "c", "c_ctx", "w_ada", "b_ada", "norm_mix", "norm_ffn", "w_in_even", "w_out_even",
        "diff_lambda", "diff_subln", "swa_sink", "w_in_odd", "mla_q_norm", "w_q_up", "mla_kv_norm", "w_kv_up",
        "w_out_odd", "w_router", "w_gate_exp", "w_up_exp", "w_down_exp", "final_norm"]
_OUTS = [("y_prompt", (1, 128, 1024)), ("y_sample", (1, 512, 1024)), ("new_diff_k", (1, 1, 128, 4, 128)),
         ("new_diff_v", (1, 1, 128, 4, 128)), ("new_swa_k", (1, 1, 128, 2, 64)), ("new_swa_v", (1, 1, 128, 2, 64)),
         ("new_mla_ckv", (1, 1, 128, 256)), ("new_mla_krope", (1, 1, 128, 32))]


def kernel(**inputs):
    import concourse.bacc as bacc
    from concourse.bass_utils import run_bass_kernel_spmd

    nc = bacc.Bacc("TRN2", target_bir_lowering=False, num_devices=1)
    arrays, aps = {}, {}
    for name in _INS:
        x = np.ascontiguousarray(inputs[name])
        arrays["in_" + name] = x
        aps[name] = nc.dram_tensor("in_" + name, x.shape, mybir.dt.from_np(x.dtype), kind="ExternalInput").ap()
    arrays["in_consts"] = constants()
    aps["consts"] = nc.dram_tensor("in_consts", arrays["in_consts"].shape, F32, kind="ExternalInput").ap()
    for name, shape in _OUTS:
        aps[name] = nc.dram_tensor("out_" + name, shape, F32, kind="ExternalOutput").ap()
    for name in ("xn", "xr"):
        aps[name] = [nc.dram_tensor(f"{name}{L}", (NTOK, D), F32).ap() for L in range(2)]
    build(nc, aps)
    r = run_bass_kernel_spmd(nc, [arrays], core_ids=[0])
    return tuple(r.results[0]["out_" + name] for name, _ in _OUTS)
```
